# Optimizing a Trainium2 kernel written in Bass

```python
import math
import jax, jax.numpy as jnp
from jax import lax
import numpy as np

D_MODEL = 2048
BATCH = 1
SEQ = 256
DEPTH = 2

CHUNK = 64
QBLOCK = 128
N_MIXERS = 2
N_SB_LAYERS = (DEPTH + 1) // 2
N_ML_LAYERS = DEPTH // 2
EPS = 1e-6

SB_HEADS = 16
SB_HEAD_DIM = D_MODEL // SB_HEADS
SB_WIDTH = SB_HEADS * SB_HEAD_DIM

ML_HEADS = 8
ML_QK_DIM = (D_MODEL // 2) // ML_HEADS
ML_V_DIM = D_MODEL // ML_HEADS
ML_QK_WIDTH = ML_HEADS * ML_QK_DIM
ML_V_WIDTH = ML_HEADS * ML_V_DIM
ML_IN_WIDTH = 2 * ML_QK_WIDTH + 2 * ML_V_WIDTH + 2 * ML_HEADS

N_GROUPS = 4
EXPERTS_PER_GROUP = 8
N_EXPERTS = N_GROUPS * EXPERTS_PER_GROUP
TOP_K = 2
EXPERT_FF = D_MODEL // 8

kernel_name = "hybrid_stickbreaking_mlstm_hmoe"

def rmsnorm(x, g):
    xf = x.astype(jnp.float32)
    y = xf * lax.rsqrt(jnp.mean(xf * xf, axis=-1, keepdims=True) + EPS)
    return (y * g.astype(jnp.float32)).astype(x.dtype)

def stick_breaking_mixer(h, w_in, w_out):
    B, S, _ = h.shape
    qkv = h @ w_in
    q, k, v = jnp.split(qkv, 3, axis=-1)
    to_heads = lambda a: a.reshape(B, S, SB_HEADS, SB_HEAD_DIM).transpose(0, 2, 1, 3).astype(jnp.float32)
    q = to_heads(q) * (SB_HEAD_DIM ** -0.5)
    k, v = to_heads(k), to_heads(v)
    outs = []
    for blk in range(S // QBLOCK):
        t0 = blk * QBLOCK
        kn = t0 + QBLOCK
        qb, kb, vb = q[:, :, t0:kn], k[:, :, :kn], v[:, :, :kn]
        z = jnp.einsum('bhqd,bhkd->bhqk', qb, kb)
        t_idx = t0 + jnp.arange(QBLOCK)[:, None]
        s_idx = jnp.arange(kn)[None, :]
        mask = s_idx < t_idx
        log_1m = jnp.where(mask, jax.nn.log_sigmoid(-z), 0.0)
        suffix = lax.cumsum(log_1m, axis=3, reverse=True) - log_1m
        A = jnp.where(mask, jnp.exp(jax.nn.log_sigmoid(z) + suffix), 0.0)
        outs.append(jnp.einsum('bhqk,bhkd->bhqd', A, vb))
    o = jnp.concatenate(outs, axis=2)
    o = o.transpose(0, 2, 1, 3).reshape(B, S, SB_WIDTH).astype(h.dtype)
    return o @ w_out

def _mlstm_chunk_step(carry, inp):
    C, n, m = carry
    qc, kc, vc, ic, fc = inp
    L = qc.shape[2]
    b = jnp.cumsum(fc, axis=-1)
    bL = b[..., -1]
    causal = jnp.tril(jnp.ones((L, L), dtype=bool))
    D = b[..., :, None] - b[..., None, :] + ic[..., None, :]
    D = jnp.where(causal, D, -1e30)
    m_inter = b + m[..., None]
    m_t = jnp.maximum(m_inter, jnp.max(D, axis=-1))
    W = jnp.einsum('bhtd,bhsd->bhts', qc, kc) * jnp.where(causal, jnp.exp(D - m_t[..., None]), 0.0)
    inter = jnp.exp(m_inter - m_t)
    num = inter[..., None] * jnp.einsum('bhtd,bhde->bhte', qc, C) + jnp.einsum('bhts,bhse->bhte', W, vc)
    den = inter * jnp.einsum('bhtd,bhd->bht', qc, n) + jnp.sum(W, axis=-1)
    h = num / jnp.maximum(jnp.abs(den), jnp.exp(-m_t))[..., None]
    key_log = bL[..., None] - b + ic
    m_new = jnp.maximum(bL + m, jnp.max(key_log, axis=-1))
    decay = jnp.exp(key_log - m_new[..., None])
    carry_scale = jnp.exp(bL + m - m_new)
    C_new = carry_scale[..., None, None] * C + jnp.einsum('bhs,bhsd,bhse->bhde', decay, kc, vc)
    n_new = carry_scale[..., None] * n + jnp.einsum('bhs,bhsd->bhd', decay, kc)
    return (C_new, n_new, m_new), h

def mlstm_mixer(h, w_in, b_i, b_f, g_head, w_out):
    B, S, _ = h.shape
    NC = S // CHUNK
    proj = (h @ w_in).astype(jnp.float32)
    q, k, v, o, i_raw, f_raw = jnp.split(
        proj, np.cumsum([ML_QK_WIDTH, ML_QK_WIDTH, ML_V_WIDTH, ML_V_WIDTH, ML_HEADS]).tolist(), axis=-1)
    i_log = i_raw + b_i.astype(jnp.float32)
    f_log = jax.nn.log_sigmoid(f_raw + b_f.astype(jnp.float32))
    def chunked(a, d):
        return a.reshape(B, NC, CHUNK, ML_HEADS, d).transpose(1, 0, 3, 2, 4)
    qc = chunked(q, ML_QK_DIM) * (ML_QK_DIM ** -0.5)
    kc = chunked(k, ML_QK_DIM)
    vc = chunked(v, ML_V_DIM)
    ic = i_log.reshape(B, NC, CHUNK, ML_HEADS).transpose(1, 0, 3, 2)
    fc = f_log.reshape(B, NC, CHUNK, ML_HEADS).transpose(1, 0, 3, 2)
    init = (jnp.zeros((B, ML_HEADS, ML_QK_DIM, ML_V_DIM), jnp.float32),
            jnp.zeros((B, ML_HEADS, ML_QK_DIM), jnp.float32),
            jnp.zeros((B, ML_HEADS), jnp.float32))
    _, hs = lax.scan(_mlstm_chunk_step, init, (qc, kc, vc, ic, fc))
    hs = hs.transpose(1, 0, 3, 2, 4).reshape(B, S, ML_HEADS, ML_V_DIM)
    hs = hs * lax.rsqrt(jnp.mean(hs * hs, axis=-1, keepdims=True) + EPS)
    hs = hs.reshape(B, S, ML_V_WIDTH) * g_head.astype(jnp.float32)
    out = (jax.nn.sigmoid(o) * hs).astype(h.dtype)
    return out @ w_out

def hierarchical_moe(h, w_group, b_group, w_expert, b_expert, w1, w3, w2):
    B, S, D = h.shape
    t = h.reshape(B * S, D)
    g_logits = (t @ w_group + b_group).astype(jnp.float32)
    p_group = jax.nn.softmax(g_logits, axis=-1)
    g_sel = jnp.argmax(g_logits, axis=-1)
    p_sel = jnp.take_along_axis(p_group, g_sel[:, None], axis=-1)
    e_logits = (t @ w_expert + b_expert).astype(jnp.float32).reshape(-1, N_GROUPS, EXPERTS_PER_GROUP)
    e_sel = jnp.take_along_axis(e_logits, g_sel[:, None, None], axis=1)[:, 0]
    top_v, top_i = lax.top_k(e_sel, TOP_K)
    w = jax.nn.softmax(top_v, axis=-1) * p_sel
    e_idx = g_sel[:, None] * EXPERTS_PER_GROUP + top_i
    gates = jnp.sum(jax.nn.one_hot(e_idx, N_EXPERTS, dtype=jnp.float32) * w[..., None], axis=1)
    hid = jax.nn.silu(jnp.einsum('td,edf->tef', t, w1)) * jnp.einsum('td,edf->tef', t, w3)
    hid = hid * gates[..., None].astype(hid.dtype)
    out = jnp.einsum('tef,efd->td', hid, w2)
    return out.reshape(B, S, D)

def setup_inputs(seed: int = 0) -> dict:
    key = jax.random.key(seed)
    ks = jax.random.split(key, 20)
    f32 = jnp.float32
    nrm = lambda k, shape, scale: jax.random.normal(k, shape, f32) * scale
    x = nrm(ks[0], (BATCH, SEQ, D_MODEL), 1.0)
    norm_mix = 1.0 + nrm(ks[1], (DEPTH, D_MODEL), 0.01)
    norm_ffn = 1.0 + nrm(ks[2], (DEPTH, D_MODEL), 0.01)
    norm_final = 1.0 + nrm(ks[3], (D_MODEL,), 0.01)
    sb_w_in = nrm(ks[4], (N_SB_LAYERS, D_MODEL, 3 * SB_WIDTH), D_MODEL ** -0.5)
    sb_w_out = nrm(ks[5], (N_SB_LAYERS, SB_WIDTH, D_MODEL), SB_WIDTH ** -0.5)
    ml_w_in = nrm(ks[6], (N_ML_LAYERS, D_MODEL, ML_IN_WIDTH), D_MODEL ** -0.5)
    ml_b_i = nrm(ks[7], (N_ML_LAYERS, ML_HEADS), 0.1)
    ml_b_f = jnp.linspace(3.0, 6.0, ML_HEADS, dtype=f32)[None, :] + nrm(ks[8], (N_ML_LAYERS, ML_HEADS), 0.1)
    ml_g_head = 1.0 + nrm(ks[9], (N_ML_LAYERS, ML_V_WIDTH), 0.01)
    ml_w_out = nrm(ks[10], (N_ML_LAYERS, ML_V_WIDTH, D_MODEL), ML_V_WIDTH ** -0.5)
    moe_w_group = nrm(ks[11], (DEPTH, D_MODEL, N_GROUPS), D_MODEL ** -0.5)
    moe_b_group = nrm(ks[12], (DEPTH, N_GROUPS), 0.01)
    moe_w_expert = nrm(ks[13], (DEPTH, D_MODEL, N_EXPERTS), D_MODEL ** -0.5)
    moe_b_expert = nrm(ks[14], (DEPTH, N_EXPERTS), 0.01)
    moe_w1 = nrm(ks[15], (DEPTH, N_EXPERTS, D_MODEL, EXPERT_FF), D_MODEL ** -0.5)
    moe_w3 = nrm(ks[16], (DEPTH, N_EXPERTS, D_MODEL, EXPERT_FF), D_MODEL ** -0.5)
    moe_w2 = nrm(ks[17], (DEPTH, N_EXPERTS, EXPERT_FF, D_MODEL), EXPERT_FF ** -0.5)
    return {"x": x, "norm_mix": norm_mix, "norm_ffn": norm_ffn, "norm_final": norm_final,
            "sb_w_in": sb_w_in, "sb_w_out": sb_w_out,
            "ml_w_in": ml_w_in, "ml_b_i": ml_b_i, "ml_b_f": ml_b_f, "ml_g_head": ml_g_head,
            "ml_w_out": ml_w_out,
            "moe_w_group": moe_w_group, "moe_b_group": moe_b_group,
            "moe_w_expert": moe_w_expert, "moe_b_expert": moe_b_expert,
            "moe_w1": moe_w1, "moe_w3": moe_w3, "moe_w2": moe_w2}

def reference(x, norm_mix, norm_ffn, norm_final, sb_w_in, sb_w_out,
              ml_w_in, ml_b_i, ml_b_f, ml_g_head, ml_w_out,
              moe_w_group, moe_b_group, moe_w_expert, moe_b_expert, moe_w1, moe_w3, moe_w2):
    for i in range(DEPTH):
        h = rmsnorm(x, norm_mix[i])
        j = i // N_MIXERS
        if i % N_MIXERS == 0:
            x = x + stick_breaking_mixer(h, sb_w_in[j], sb_w_out[j])
        else:
            x = x + mlstm_mixer(h, ml_w_in[j], ml_b_i[j], ml_b_f[j], ml_g_head[j], ml_w_out[j])
        h = rmsnorm(x, norm_ffn[i])
        x = x + hierarchical_moe(h, moe_w_group[i], moe_b_group[i], moe_w_expert[i], moe_b_expert[i],
                                 moe_w1[i], moe_w3[i], moe_w2[i])
    return rmsnorm(x, norm_final)


_drawn_inputs = setup_inputs


def setup_inputs(seed=0):
    import zlib

    import numpy as np

    out = dict(_drawn_inputs(seed))
    spreads = {}
    factors = {'norm_final': 34.599,
     'ml_b_i': 64.0,
     'ml_g_head': 13.208,
     'moe_b_group': 2.768,
     'moe_b_expert': 2.706}
    for name, (base, spread) in spreads.items():
        noise = np.random.default_rng([zlib.crc32(name.encode()), seed]).standard_normal(out[name].shape)
        drawn = base * np.exp(spread * noise) if base else spread * noise
        out[name] = __import__('jax').numpy.asarray(drawn.astype(out[name].dtype))
    for name, factor in factors.items():
        out[name] = (out[name] * factor).astype(out[name].dtype)
    return out
```

```python
from contextlib import ExitStack

import numpy as np

import concourse.bass as bass
from concourse import mybir

F32 = mybir.dt.float32
I32 = mybir.dt.int32
ALU = mybir.AluOpType
ACT = mybir.ActivationFunctionType
AX = mybir.AxisListType.X

P = 128
D = 2048
T = 256
TB = T // P
KT = D // P
EPS = 1e-6
SB_HEADS, SB_DH = 16, 128
ML_HEADS, ML_DQ, ML_DV = 8, 128, 256
GROUPS, PER_GROUP = 4, 8
EXPERTS = GROUPS * PER_GROUP
FF = D // 8
ROUTER = GROUPS + EXPERTS
CAP = 32
QUAD = P // CAP
NQUAD = EXPERTS // QUAD
SLOTS = 12
SLOT = 2048
COLS = 512
CSLOT = 4
TRI = 384
CLAMP = 40.0
SBG = 4
MLG = 2
NGROUP = 4
BANKS = ["T0", "T1", "A0", "A1", "G0", "G1", "S0", "S1"]
NORM_BANKS = ["T0", "T1", "A0", "A1"]

SB_EVENTS = [(0, "turn", 0), (0, "turn", 1), (0, "turn", 2), (0, "turn", 3),
             (4, "score", 0), (10, "score", 1), (14, "suffix", 0), (20, "suffix", 1),
             (24, "out", 0), (30, "out", 1), (32, "chunk", 0), (34, "score", 2), (40, "score", 3),
             (46, "suffix", 2), (52, "suffix", 3), (58, "out", 2), (62, "out", 3),
             (64, "chunk", 1), (96, "chunk", 2)]
ML_EVENTS = [(0, "turn", 0), (0, "turn", 1), (4, "score", 0), (8, "score", 1), (12, "num", 0),
             (20, "num", 1), (32, "chunk", 0), (42, "join", 0), (58, "join", 1),
             (64, "chunk", 1), (96, "chunk", 2)]


def bank_uses():
    total = {b: 0 for b in BANKS}
    first = {}

    def phase(name, **n):
        first[name] = dict(total)
        for k, v in n.items():
            for b in BANKS:
                if b == k or b[0] == k:
                    total[b] += v

    for layer in (0, 1):
        phase(("norm_mix", layer), T=2, A=2)
        if layer:
            phase(("gates", layer), T=1, A=ML_HEADS // 2)
        phase(("mix", layer), G=2 * NGROUP, S=NGROUP, T=4 * NGROUP, A=(1 if layer else 2) * NGROUP)
        phase(("out", layer), G=2, S=2)
        phase(("norm_ffn", layer), T=2, A=2)
        phase(("route", layer), S=1, G0=1)
        phase(("gather", layer), G=2)
        phase(("moe", layer), G=5 * NQUAD - 2, A=2 * NQUAD, T=2 * NQUAD, S=4 * NQUAD)
    return first


def ring_slots():
    n, first = 0, {}
    for layer in (0, 1):
        for name, count in (("mix", 3 * CSLOT * NGROUP), ("out", 4 * CSLOT), ("moe", 6 * EXPERTS)):
            first[name, layer] = n
            n += count
    return first


def build(nc, x_in, norm_mix, norm_ffn, norm_final, sb_w_in, sb_w_out, ml_w_in, ml_b_i, ml_b_f,
          ml_g_head, ml_w_out, moe_w_group, moe_b_group, moe_w_expert, moe_b_expert,
          moe_w1, moe_w3, moe_w2, out):
    first_use, first_slot = bank_uses(), ring_slots()
    ctx = ExitStack()
    with ctx:
        def sb(name, shape, dt=F32):
            return ctx.enter_context(nc.sbuf_tensor(name, shape, dt))

        def sem(name):
            return ctx.enter_context(nc.semaphore(name))

        ring = sb("ring", [P, SLOTS, SLOT])
        x = sb("x", [P, TB, D])
        h = sb("h", [P, TB, D])
        hT = sb("hT", [P, KT, T])
        grow = sb("grow", [P, D])
        ident = sb("ident", [P, P])
        neg_suffix = sb("neg_suffix", [P, P])
        neg_ones = sb("neg_ones", [P, P])
        before = sb("before", [P, P])
        ones = sb("ones", [P, P])
        fold = sb("fold", [P, CAP])
        iota = sb("iota", [P, CAP])
        thresholds = sb("thresholds", [1, T // CAP - 1])
        eps_col = sb("eps_col", [P, 1])
        router_w = sb("router_w", [P, KT, ROUTER])
        router_b = sb("router_b", [1, ROUTER])
        gate_w = sb("gate_w", [P, KT, 2 * ML_HEADS])
        gate_b = sb("gate_b", [ML_HEADS, 2])
        sumsq = sb("sumsq", [P, TB])
        mean_eps = sb("mean_eps", [P, TB])
        rstd = sb("rstd", [P, TB])
        newton = sb("newton", [P, TB])
        extra_f = sb("extra_f", [1, 1])
        extra_i = sb("extra_i", [1, 1], I32)
        count_max = sb("count_max", [1, 1])
        count_lt = sb("count_lt", [1, T // CAP - 1])
        arena = sb("arena", [P, 12288 - 256])
        over_w = hT[:, :, :].rearrange("p k t -> p (k t)")[:, 0:2 * SLOT].rearrange("p (s n) -> p s n", s=2)
        oT = h[:, :, :].rearrange("p b d -> p (b d)").rearrange("p (k t) -> p k t", t=T)
        hv = h[:, :, :].rearrange("p b (c k) -> p b k c", k=KT)

        class Region:
            def __init__(self):
                self.at = 0

            def __call__(self, *shape):
                n = int(np.prod(shape))
                view = arena[:, self.at:self.at + n]
                self.at += n
                assert self.at <= arena.shape[1], self.at
                names = " ".join("abcd"[:len(shape)])
                sizes = {"abcd"[k]: s for k, s in enumerate(shape) if k}
                return view.rearrange(f"p ({names}) -> p {names}", **sizes) if len(shape) > 1 else view

        r = Region()
        q_raw, k_raw, v_raw = r(TB, COLS), r(TB, COLS), r(TB, COLS)
        qT, kT = r(SBG, T), r(SBG, T)
        soft, sp, prob = r(2, TRI), r(2, TRI), r(2, TRI)
        r = Region()
        decay = r(ML_HEADS, TRI)
        qk_raw, v_one, o_exp = r(TB, COLS), r(TB, MLG, ML_DV + 1), r(TB, COLS)
        at_selector = r.at
        qkT = r(MLG, 2, T)
        weights = r(MLG, TRI)
        at_rows = r.at
        gated = r(MLG, TB, ML_DV)
        hs, sig = r(TB, ML_DV), r(TB, ML_DV)
        u_col, m_col = r(TB, ML_HEADS), r(TB, ML_HEADS)
        den, ssq, ms, hrs, hnw = r(TB), r(TB), r(TB), r(TB), r(TB)
        junk = r(ML_DV)
        r = Region()
        r.at = at_rows
        g_y, g_clip, g_sp, g_negb, g_u, g_m, g_em = (r(T)[0:ML_HEADS] for _ in range(7))
        r = Region()
        r.at = at_selector
        selector = r(ML_HEADS, P)[0:ML_HEADS]
        r = Region()
        disp = r(TB, EXPERTS, CAP)
        xe = r(KT, P)
        acc = r(2, COLS)
        y = r(D)
        disp_g, spread = r(TB, P), r(TB, P)
        hid = r(QUAD, 2 * CAP)
        ex, sg, t13 = r(2 * CAP), r(2 * CAP), r(2 * CAP)
        logits = r(TB, ROUTER)
        gsel, gexp, gcmp = r(TB, GROUPS), r(TB, GROUPS), r(TB, GROUPS)
        gmax, gsum, tie, psel = r(TB, 1), r(TB, 1), r(TB, 1), r(TB, 1)
        picked = r(TB, GROUPS, PER_GROUP)
        es, cmp8, s1, s2, gate8, tmp8 = (r(TB, PER_GROUP) for _ in range(6))
        m1, m2, dm, w1c, w2c = (r(TB, 1) for _ in range(5))
        gates, mask, posm = (r(TB, EXPERTS) for _ in range(3))
        rank = r(PER_GROUP)
        over_d, over_g = r(TB, CAP), r(TB, CAP)

        psum = {b: ctx.enter_context(nc.psum_tensor(f"psum_{b}", [P, 512], F32)) for b in BANKS}

        filled = {b: sem(f"filled_{b}") for b in BANKS}
        emptied = {b: sem(f"emptied_{b}") for b in BANKS}
        slot_loaded = [sem(f"slot_loaded_{n}") for n in range(SLOTS)]
        x_loaded = [sem(f"x_loaded_{b}") for b in range(TB)]
        grow_loaded = sem("grow_loaded")
        grow_used = sem("grow_used")
        small_loaded = [sem("small_loaded_0"), sem("small_loaded_1")]
        consts_made = sem("consts_made")
        squares_done = sem("squares_done")
        mean_ready = sem("mean_ready")
        rstd_seed = sem("rstd_seed")
        h_ready = sem("h_ready")
        clipped = sem("clipped")
        softplus_log = sem("softplus_log")
        softplus_full = sem("softplus_full")
        softplus_masked = sem("softplus_masked")
        suffix_summed = sem("suffix_summed")
        prob_exp = sem("prob_exp")
        mask_begun = sem("mask_begun")
        prob_masked = sem("prob_masked")
        gate_clip = sem("gate_clip")
        gate_log = sem("gate_log")
        gate_rows = sem("gate_rows")
        gate_exp = sem("gate_exp")
        decay_exp = sem("decay_exp")
        decay_masked = sem("decay_masked")
        ones_set = sem("ones_set")
        weights_ready = sem("weights_ready")
        head_squares = sem("head_squares")
        head_seed = sem("head_seed")
        gated_ready = sem("gated_ready")
        group_shift = sem("group_shift")
        group_exp = sem("group_exp")
        top2_gap = sem("top2_gap")
        top2_exp = sem("top2_exp")
        mask_ready = sem("mask_ready")
        disp_ready = sem("disp_ready")
        extra_ready = sem("extra_ready")
        disp_gated = sem("disp_gated")
        silu_exp = sem("silu_exp")
        exp_taken = sem("exp_taken")
        hid_ready = sem("hid_ready")
        moe_done = sem("moe_done")
        over = [{n: sem(f"over_{n}_{layer}") for n in (
            "slots", "rows_filled", "rows", "spread_filled", "spread", "w_loaded", "w_used", "acc",
            "turned", "exp", "hid", "y", "scattered")} for layer in (0, 1)]
        out_ready = sem("out_ready")
        out_stored = sem("out_stored")

        block = ctx.enter_context(nc.Block())

        def copies_to_hT(eng, copy, phase, layer, kind):
            for u in range(2 * KT // 4):
                bank = NORM_BANKS[u % 4]
                if bank[0] == kind:
                    b, k0 = u // 4, 4 * (u % 4)
                    eng.wait_ge(filled[bank], first_use[phase, layer][bank] + u // 4 + 1)
                    copy(hT[:, k0:k0 + 4, b * P:(b + 1) * P],
                         psum[bank][:, :].rearrange("p (k t) -> p k t", k=4)).then_inc(emptied[bank], 1)

        def copy_chunk(eng, copy, layer, i, c, b):
            base = first_use["mix", layer]
            bank = f"{'GSG'[c]}{b}"
            eng.wait_ge(filled[bank], i * (1 if c == 1 else 2) + (base[bank] + c // 2 + 1))
            src = psum[bank][:, :]
            if layer and c == 2:
                eng.activation(o_exp[:, b, :], src, ACT.Exp, scale=-1.0).then_inc(emptied[bank], 1)
            elif layer and c == 1:
                copy(v_one[:, b, :, 0:ML_DV], src.rearrange("p (h n) -> p h n", h=MLG)).then_inc(emptied[bank], 1)
            else:
                dst = qk_raw if layer else (q_raw, k_raw, v_raw)[c]
                copy(dst[:, b, :], src).then_inc(emptied[bank], 1)

        def overflow_passes(eng, layer, expert):
            eng.wait_ge(extra_ready, layer + 1)
            extra = eng.value_load(extra_i[0:1, 0:1], min_val=0, max_val=T // CAP - 1)
            with eng.If(extra > 0):
                with eng.Fori(0, extra) as turn:
                    with eng.Fori(0, EXPERTS) as e:
                        expert(turn * EXPERTS + e, e)

        def slot_at(n):
            return n % SLOTS

        def slot_value(n0, i, per, j):
            return 16 * ((n0 + j) // SLOTS + 1) + i * (16 * per // SLOTS)

        def chunk_slot(n, k):
            return ring[:, slot_at(n + k // 4), (k % 4) * COLS:(k % 4 + 1) * COLS]

        def w13_tile(n, k):
            s = slot_at(n + 2 * (k // 8))
            return ring[:, s:s + 2, (k % 8) * FF:(k % 8 + 1) * FF]

        @block.sync
        def _(sp_eng):
            def freed_mix(layer, i):
                base = first_use["mix", layer]
                return [(filled[b], i * (1 if c == 1 else 2) + (base[b] + c // 2 + 1))
                        for c, b in enumerate(("G1", "S1", "G1"))]

            def freed_out(layer):
                base = first_use["out", layer]
                return [(filled[b], base[b] + c // 2 + 1) for c, b in enumerate(("G1", "S1", "G1", "S1"))]

            def freed_moe(layer, i):
                base = first_use["moe", layer]
                last = isinstance(i, int) and i == NQUAD - 1
                return ([(filled[f"A{q % 2}"], i * 2 + (base[f"A{q % 2}"] + q // 2 + 1)) for q in range(QUAD)]
                        + [(filled["G1"], i * 5 + (base["G1"] + (3 if last else 5)))] * 2)

            def stream(n0, units, before, now, parts):
                freed = before + now
                for u in range(units):
                    if len(before) + u >= SLOTS // CSLOT:
                        sp_eng.wait_ge(*freed[len(before) + u - SLOTS // CSLOT])
                    for j in range(u * CSLOT, (u + 1) * CSLOT):
                        s = slot_at(n0 + j)
                        dst, src = parts(ring[:, s, :], j)
                        sp_eng.dma_start(dst, src).then_inc(slot_loaded[s], 16)

            def mix_stream(layer, i, before):
                def parts(s, j):
                    c, k0 = j // CSLOT, 4 * (j % CSLOT)
                    w = (ml_w_in if layer else sb_w_in)[0].rearrange("(p k) n -> p k n", k=KT)
                    if layer and c == 0:
                        k8 = 8 * (j // 2)
                        src = w[:, k8:k8 + 8, bass.ds(i * FF + (j % 2) * ML_HEADS * ML_DQ, FF)]
                        return s.rearrange("p (k n) -> p k n", k=8), src
                    src = w[:, k0:k0 + 4, bass.ds(i * COLS + c * D, COLS)]
                    return s.rearrange("p (k n) -> p k n", k=4), src

                stream(first_slot["mix", layer], 3, before, freed_mix(layer, i), parts)

            def out_stream(layer):
                w = (ml_w_out if layer else sb_w_out)[0].rearrange("(k p) n -> p k n", p=P)

                def parts(s, j):
                    c, k0 = j // CSLOT, 4 * (j % CSLOT)
                    return s.rearrange("p (k n) -> p k n", k=4), w[:, k0:k0 + 4, c * COLS:(c + 1) * COLS]

                stream(first_slot["out", layer], 4, freed_mix(layer, NGROUP - 1), freed_out(layer), parts)

            def moe_stream(layer, i, before):
                def parts(s, j):
                    if j < 4 * QUAD:
                        w = (moe_w1, moe_w3)[j % 2][layer].rearrange("e (p k) f -> p e (k f)", k=KT)
                        e, half = j // 4, (j % 4) // 2
                        return s.unsqueeze(1), w[:, bass.ds(i * QUAD + e, 1), half * SLOT:(half + 1) * SLOT]
                    w = moe_w2[layer].rearrange("e (k p) n -> k p e n", p=P)
                    e, ft = (j - 4 * QUAD) // 2, j % 2
                    return s.unsqueeze(1), w[ft, :, bass.ds(i * QUAD + e, 1), :]

                stream(first_slot["moe", layer], 6, before, freed_moe(layer, i), parts)

            def overflow(layer):
                o = over[layer]

                def expert(k, e):
                    for half in range(2):
                        sp_eng.wait_ge(o["w_used"], k * 3 + (half + 1))
                        for n, w in enumerate((moe_w1, moe_w3)):
                            src = w[layer].rearrange("e (p k) f -> p e (k f)", k=KT)
                            sp_eng.dma_start(over_w[:, n:n + 1, :], src[:, bass.ds(e, 1), half * SLOT:(half + 1) * SLOT]
                                             ).then_inc(o["w_loaded"], 16)
                    sp_eng.wait_ge(o["w_used"], k * 3 + 3)
                    src = moe_w2[layer].rearrange("e (k p) n -> k p e n", p=P)
                    for ft in range(2):
                        sp_eng.dma_start(over_w[:, ft:ft + 1, :], src[ft, :, bass.ds(e, 1), :]
                                         ).then_inc(o["w_loaded"], 16)

                overflow_passes(sp_eng, layer, expert)

            for layer in (0, 1):
                mix_stream(layer, 0, freed_moe(0, NQUAD - 1) if layer else [])
                with sp_eng.Fori(1, NGROUP) as g:
                    mix_stream(layer, g, freed_mix(layer, g - 1))
                out_stream(layer)
                moe_stream(layer, 0, freed_out(layer))
                with sp_eng.Fori(1, NQUAD) as i:
                    moe_stream(layer, i, freed_moe(layer, i - 1))
                overflow(layer)
            for b in range(TB):
                sp_eng.wait_ge(out_ready, b + 1)
                sp_eng.dma_start(out[0, b * P:(b + 1) * P, :], h[:, b, :]).then_inc(out_stored, 16)
            sp_eng.wait_ge(out_stored, 16 * TB)

        @block.gpsimd
        def _(pool):
            def load_grow(row, n):
                if n:
                    pool.wait_ge(grow_used, n)
                pool.dma_start(grow[:, :], row.partition_broadcast(P)).then_inc(grow_loaded, 16)

            def load_small(layer):
                s = small_loaded[layer]
                pool.dma_start(router_w[:, :, 0:GROUPS], moe_w_group[layer].rearrange("(p k) n -> p k n", k=KT)).then_inc(s, 16)
                pool.dma_start(router_w[:, :, GROUPS:ROUTER], moe_w_expert[layer].rearrange("(p k) n -> p k n", k=KT)).then_inc(s, 16)
                pool.dma_start(router_b[:, 0:GROUPS], moe_b_group[layer:layer + 1, :]).then_inc(s, 16)
                pool.dma_start(router_b[:, GROUPS:ROUTER], moe_b_expert[layer:layer + 1, :]).then_inc(s, 16)

            load_grow(norm_mix[0], 0)
            pool.memset(ident[:, :], 0.0)
            pool.memset(fold[:, :], 0.0)
            pool.memset(neg_ones[:, :], -1.0)
            pool.memset(ones[:, :], 1.0)
            pool.memset(eps_col[:, :], EPS)
            pool.iota(iota[:, :], pattern=[[1, CAP]], base=0, channel_multiplier=0,
                      allow_small_or_imprecise_dtypes=True)
            pool.drain()
            pool.affine_select(out=ident[:, :], in_=ident[:, :], compare_op=ALU.not_equal, fill=1.0,
                               base=0, pattern=[[-1, P]], channel_multiplier=1)
            pool.affine_select(out=neg_suffix[:, :], in_=neg_ones[:, :], compare_op=ALU.is_ge, fill=0.0,
                               base=0, pattern=[[-1, P]], channel_multiplier=1)
            pool.affine_select(out=before[:, :], in_=ones[:, :], compare_op=ALU.is_gt, fill=0.0,
                               base=0, pattern=[[1, P]], channel_multiplier=-1)
            for q in range(QUAD):
                pool.affine_select(out=fold[:, :], in_=fold[:, :], compare_op=ALU.not_equal, fill=1.0,
                                   base=-q * CAP, pattern=[[-1, CAP]], channel_multiplier=1)
                pool.drain()
            pool.drain().then_inc(consts_made, 1)
            load_small(0)
            pool.dma_start(gate_w[:, :, :], ml_w_in[0, :, 3 * D:3 * D + 2 * ML_HEADS].rearrange("(p k) n -> p k n", k=KT)).then_inc(small_loaded[0], 16)
            pool.dma_start(gate_b[:, 0:1], ml_b_i.rearrange("o n -> n o")).then_inc(small_loaded[0], 16)
            pool.dma_start(gate_b[:, 1:2], ml_b_f.rearrange("o n -> n o")).then_inc(small_loaded[0], 16)
            load_grow(norm_ffn[0], 1)

            def keep_causal(view, strict):
                pool.affine_select(out=view, in_=view, compare_op=ALU.is_gt if strict else ALU.is_ge,
                                   fill=0.0, base=0, pattern=[[0, 2], [1, P]], channel_multiplier=-1)
                return pool.drain()

            def diagonals(tile):
                return tile.rearrange("p (c n) -> p c n", n=P)[:, 0:3:2, :]

            def sb_group(g):
                for _, step, k in SB_EVENTS:
                    if step == "score":
                        pool.wait_ge(softplus_full, g * SBG + k + 1)
                        pool.sem_inc(mask_begun, 1)
                        keep_causal(diagonals(sp[:, k % 2, :]), True).then_inc(softplus_masked, 1)
                    if step == "suffix":
                        pool.wait_ge(prob_exp, g * SBG + k + 1)
                        pool.sem_inc(mask_begun, 1)
                        keep_causal(diagonals(prob[:, k % 2, :]), True).then_inc(prob_masked, 1)

            with pool.Fori(0, NGROUP) as g:
                sb_group(g)

            load_grow(norm_mix[1], 2)
            pool.wait_ge(mask_ready, 1)
            load_small(1)
            pool.wait_ge(h_ready, 3 * TB)
            pool.memset(v_one[:, :, :, ML_DV:ML_DV + 1], 1.0)
            pool.memset(selector, 1.0)
            pool.drain()
            pool.affine_select(out=selector, in_=selector, compare_op=ALU.is_equal, fill=0.0, base=0,
                               pattern=[[-1, ML_HEADS], [0, P]], channel_multiplier=1)
            pool.drain().then_inc(ones_set, 1)
            load_grow(ml_g_head[0], 3)
            for hd in range(ML_HEADS):
                pool.wait_ge(decay_exp, hd + 1)
                keep_causal(diagonals(decay[:, hd, :]), False).then_inc(decay_masked, 1)
            load_grow(norm_ffn[1], 4)
            load_grow(norm_final, 5)

        @block.tensor
        def _(pe):
            def claim(b, n):
                if not (isinstance(n, int) and n == 0):
                    pe.wait_ge(emptied[b], n)

            def mm(dst, lhsT, rhs, start, stop):
                return pe.matmul(dst, lhsT, rhs, start=start, stop=stop, skip_group_check=True)

            def turn_rows(phase, layer):
                base = first_use[phase, layer]
                for u in range(2 * KT // 4):
                    bank = NORM_BANKS[u % 4]
                    b, k0 = u // 4, 4 * (u % 4)
                    if u % 4 == 0:
                        pe.wait_ge(h_ready, {("norm_mix", 0): 0, ("norm_ffn", 0): 1, ("norm_mix", 1): 2,
                                             ("norm_ffn", 1): 3}[phase, layer] * TB + b + 1)
                    claim(bank, base[bank] + u // 4)
                    for k in range(4):
                        last = pe.transpose(psum[bank][:, k * P:(k + 1) * P], hv[:, b, k0 + k, :], ident[:, :])
                    last.then_inc(filled[bank], 1)

            def wait_turned(phase, layer):
                for b in NORM_BANKS:
                    pe.wait_ge(emptied[b], first_use[phase, layer][b] + 2)

            def gates_in():
                base = first_use["gates", 1]
                pe.wait_ge(small_loaded[0], 16 * 7)
                claim("T0", base["T0"])
                for half in range(2):
                    for k in range(KT):
                        last = mm(psum["T0"][0:ML_HEADS, half * T:(half + 1) * T],
                                  gate_w[:, k, half * ML_HEADS:(half + 1) * ML_HEADS], hT[:, k, :],
                                  k == 0, k == KT - 1)
                last.then_inc(filled["T0"], 1)

            def gates_turn():
                base = first_use["gates", 1]
                pe.wait_ge(gate_rows, 1)
                pe.wait_ge(gate_exp, 1)
                claim("T1", base["T1"])
                for n, row in enumerate((g_u, g_em)):
                    for b in range(TB):
                        c = (n * TB + b) * ML_HEADS
                        last = pe.transpose(psum["T1"][:, c:c + ML_HEADS], row[:, b * P:(b + 1) * P],
                                            ident[0:ML_HEADS, 0:ML_HEADS])
                last.then_inc(filled["T1"], 1)

            def gates_spread(hd):
                bank = ("A0", "A1")[hd % 2]
                if hd == 0:
                    pe.wait_ge(ones_set, 1)
                claim(bank, first_use["gates", 1][bank] + hd // 2)
                mm(psum[bank][:, 0:T], selector[:, hd, :], g_m, True, True).then_inc(filled[bank], 1)

            def project(layer, i, event):
                n0 = first_slot["mix", layer]
                base = first_use["mix", layer]
                m = 0
                for c in range(3):
                    banks = ("G0", "G1") if c != 1 else ("S0", "S1")
                    for b in banks:
                        claim(b, i * (1 if c == 1 else 2) + base[b] + c // 2)
                    for k in range(KT):
                        paired = layer == 1 and c == 0
                        held = 2 if paired else 1
                        if k % (4 * held) == 0:
                            for j in range(c * CSLOT + k // 4, c * CSLOT + k // 4 + held):
                                pe.wait_ge(slot_loaded[slot_at(n0 + j)], slot_value(n0, i, 3 * CSLOT, j))
                        w = (w13_tile if paired else chunk_slot)(n0 + c * CSLOT, k)
                        for b in range(TB):
                            event(m)
                            m += 1
                            last = mm(psum[banks[b]][:, :], hT[:, k, b * P:(b + 1) * P], w, k == 0, k == KT - 1)
                            if k == KT - 1:
                                last.then_inc(filled[banks[b]], 1)
                event(m)

            def wait_chunk(layer, i, c):
                base = first_use["mix", layer]
                for b in (("G0", "G1") if c != 1 else ("S0", "S1")):
                    pe.wait_ge(emptied[b], i * (1 if c == 1 else 2) + (base[b] + c // 2 + 1))

            def sb_step(g, step, k):
                base = first_use["mix", 0]
                t, a = f"T{k % 2}", f"A{k % 2}"
                if step == "turn":
                    if k == 0:
                        wait_chunk(0, g, 0)
                        wait_chunk(0, g, 1)
                    claim(t, g * 4 + base[t] + k // 2)
                    for n, raw in enumerate((q_raw, k_raw)):
                        for b in range(TB):
                            last = pe.transpose(psum[t][:, n * T + b * P:n * T + (b + 1) * P],
                                                raw[:, b, k * SB_DH:(k + 1) * SB_DH], ident[:, :])
                    last.then_inc(filled[t], 1)
                if step == "score":
                    pe.wait_ge(emptied[t], g * 4 + (base[t] + k // 2 + 1))
                    claim(a, g * 2 + base[a] + k // 2)
                    mm(psum[a][:, 0:T], kT[:, k, 0:P], qT[:, k, :], True, False)
                    mm(psum[a][:, T:TRI], kT[:, k, P:T], qT[:, k, P:T], False, True).then_inc(filled[a], 1)
                if step == "suffix":
                    pe.wait_ge(softplus_masked, g * SBG + k + 1)
                    s = sp[:, k % 2, :]
                    mm(psum[a][:, 0:T], neg_suffix[:, :], s[:, 0:T], False, False)
                    mm(psum[a][:, P:T], neg_ones[:, :], s[:, T:TRI], False, False)
                    mm(psum[a][:, T:TRI], neg_suffix[:, :], s[:, T:TRI], False, True).then_inc(suffix_summed, 1)
                if step == "out":
                    if k == 0:
                        wait_chunk(0, g, 2)
                    pe.wait_ge(prob_masked, g * SBG + k + 1)
                    claim(t, g * 4 + base[t] + 2 + k // 2)
                    v = v_raw[:, :, k * SB_DH:(k + 1) * SB_DH]
                    mm(psum[t][:, 0:T], v[:, 0, :], prob[:, k % 2, 0:T], True, False)
                    mm(psum[t][:, P:T], v[:, 1, :], prob[:, k % 2, T:TRI], False, True).then_inc(filled[t], 1)

            def ml_step(g, step, k):
                base = first_use["mix", 1]
                t, a = f"T{k}", f"A{k}"
                if step == "turn":
                    if k == 0:
                        wait_chunk(1, g, 0)
                    claim(t, g * 4 + base[t])
                    for n in range(2):
                        for b in range(TB):
                            c = n * (COLS // 2) + k * ML_DQ
                            last = pe.transpose(psum[t][:, n * T + b * P:n * T + (b + 1) * P],
                                                qk_raw[:, b, c:c + ML_DQ], ident[:, :])
                    last.then_inc(filled[t], 1)
                if step == "score":
                    pe.wait_ge(emptied[t], g * 4 + (base[t] + 1))
                    claim(a, g + base[a])
                    q, kk = qkT[:, k, 0, :], qkT[:, k, 1, :]
                    mm(psum[a][:, 0:T], kk[:, 0:P], q, True, False)
                    mm(psum[a][:, T:TRI], kk[:, P:T], q[:, P:T], False, True).then_inc(filled[a], 1)
                if step == "num":
                    if k == 0:
                        wait_chunk(1, g, 1)
                    pe.wait_ge(weights_ready, g * MLG + k + 1)
                    claim("T0", g * 4 + base["T0"] + 1 + k)
                    claim("T1", g * 4 + base["T1"] + 1 + k)
                    w = weights[:, k, :]
                    mm(psum["T0"][:, 0:ML_DV + 1], w[:, 0:P], v_one[:, 0, k, :], True, True).then_inc(filled["T0"], 1)
                    mm(psum["T1"][:, 0:ML_DV + 1], w[:, P:T], v_one[:, 0, k, :], True, False)
                    mm(psum["T1"][:, 0:ML_DV + 1], w[:, T:TRI], v_one[:, 1, k, :], False, True).then_inc(filled["T1"], 1)
                if step == "join":
                    pe.wait_ge(gated_ready, g * MLG + k + 1)
                    claim(t, g * 4 + base[t] + 3)
                    for n in range(2):
                        for b in range(TB):
                            last = pe.transpose(psum[t][:, n * T + b * P:n * T + (b + 1) * P],
                                                gated[:, k, b, n * P:(n + 1) * P], ident[:, :])
                    last.then_inc(filled[t], 1)

            def mix(layer):
                step = ml_step if layer else sb_step
                events = ML_EVENTS if layer else SB_EVENTS

                def first_group(m):
                    if layer and m == 32:
                        gates_turn()
                    if layer and m >= 66 and m % 3 == 0 and (m - 66) // 3 < ML_HEADS:
                        gates_spread((m - 66) // 3)

                if layer:
                    gates_in()
                project(layer, 0, first_group)

                def group(i):
                    def event(m):
                        for at, name, k in events:
                            if at == m and name != "chunk":
                                step(i - 1, name, k)
                    project(layer, i, event)

                with pe.Fori(1, NGROUP) as i:
                    group(i)
                for _, name, k in events:
                    if name != "chunk":
                        step(NGROUP - 1, name, k)

            def project_out(layer):
                n0 = first_slot["out", layer]
                base = first_use["out", layer]
                last_t = first_use["mix", layer]
                for t in ("T0", "T1"):
                    pe.wait_ge(emptied[t], last_t[t] + 4 * NGROUP)
                for c in range(4):
                    banks = ("G0", "G1") if c % 2 == 0 else ("S0", "S1")
                    for b in banks:
                        claim(b, base[b] + c // 2)
                    for k in range(KT):
                        if k % 4 == 0:
                            j = c * CSLOT + k // 4
                            pe.wait_ge(slot_loaded[slot_at(n0 + j)], slot_value(n0, 0, 0, j))
                        for b in range(TB):
                            last = mm(psum[banks[b]][:, :], oT[:, k, b * P:(b + 1) * P],
                                      chunk_slot(n0 + c * CSLOT, k), k == 0, k == KT - 1)
                            if k == KT - 1:
                                last.then_inc(filled[banks[b]], 1)

            def route(layer):
                base = first_use["route", layer]
                pe.wait_ge(small_loaded[layer], 16 * (4 if layer else 7))
                for b in range(TB):
                    bank = f"S{b}"
                    claim(bank, base[bank])
                    for k in range(KT):
                        mm(psum[bank][:, 0:ROUTER], hT[:, k, b * P:(b + 1) * P], router_w[:, k, :], k == 0, False)
                    mm(psum[bank][:, 0:ROUTER], ones[0:1, :], router_b[0:1, :], False, True).then_inc(filled[bank], 1)
                pe.wait_ge(mask_ready, layer + 1)
                claim("G0", base["G0"])
                g = psum["G0"]
                mm(g[:, 0:EXPERTS], before[:, :], mask[:, 0, :], True, True)
                mm(g[:, EXPERTS:2 * EXPERTS], before[:, :], mask[:, 1, :], True, False)
                mm(g[:, EXPERTS:2 * EXPERTS], ones[:, :], mask[:, 0, :], False, True)
                mm(g[:, 2 * EXPERTS:3 * EXPERTS], ones[:, :], mask[:, 0, :], True, False)
                mm(g[:, 2 * EXPERTS:3 * EXPERTS], ones[:, :], mask[:, 1, :], False, True).then_inc(filled["G0"], 1)

            def gather(layer, i, c, n):
                bank = f"G{c % 2}"
                claim(bank, n)
                for k in range(4):
                    for b in range(TB):
                        rhs = disp[:, b, :, :].rearrange("p e s -> p (e s)")[:, bass.ds(i * P, P)]
                        last = mm(psum[bank][:, k * P:(k + 1) * P], hv[:, b, 4 * c + k, :], rhs, b == 0, b == 1)
                last.then_inc(filled[bank], 1)

            def up(bank, n0, q):
                for k in range(KT):
                    if k % 8 == 0:
                        yield k // 8
                    j = k % QUAD
                    last = mm(psum[bank][CAP * j:CAP * (j + 1), :], xe[:, k, CAP * q:CAP * (q + 1)],
                              w13_tile(n0, k), k < QUAD, k >= KT - QUAD)
                last.then_inc(filled[bank], 1)

            def fold_turn(bank, a):
                for c in range(4):
                    last = mm(psum[bank][:, c * CAP:(c + 1) * CAP], a[:, c * P:(c + 1) * P], fold[:, :], True, True)
                last.then_inc(filled[bank], 1)

            def quad(layer, i, more):
                n0 = first_slot["moe", layer]
                base = first_use["moe", layer]
                per = 6 * QUAD

                def turned(q):
                    t, a = f"T{q % 2}", f"A{q % 2}"
                    pe.wait_ge(emptied[a], i * 2 + (base[a] + q // 2 + 1))
                    claim(t, i * 2 + base[t] + q // 2)
                    fold_turn(t, acc[:, q % 2, :])

                pe.wait_ge(disp_gated, i + (layer * NQUAD + 1))
                for b in range(TB):
                    claim(f"G{b}", i * 5 + base[f"G{b}"])
                    pe.transpose(psum[f"G{b}"][:, 0:P], disp_g[:, b, :], ident[:, :]).then_inc(filled[f"G{b}"], 1)
                for b in range(2):
                    pe.wait_ge(emptied[f"G{b}"], i * 5 + base[f"G{b}"])
                for q in range(QUAD):
                    a = f"A{q % 2}"
                    claim(a, i * 2 + base[a] + q // 2)
                    for half in up(a, n0 + 4 * q, q):
                        for j in (4 * q + 2 * half, 4 * q + 2 * half + 1):
                            pe.wait_ge(slot_loaded[slot_at(n0 + j)], slot_value(n0, i, per, j))
                    if q:
                        turned(q - 1)
                if more:
                    for c in range(2):
                        gather(layer, i + 1, c, i * 5 + base[f"G{c}"] + 1)
                turned(QUAD - 1)
                if more:
                    for c in range(2, 4):
                        gather(layer, i + 1, c, i * 5 + base[f"G{c % 2}"] + 2)
                pe.wait_ge(hid_ready, i * QUAD + (layer * EXPERTS + QUAD))
                for j in range(4 * QUAD, 6 * QUAD):
                    pe.wait_ge(slot_loaded[slot_at(n0 + j)], slot_value(n0, i, per, j))
                for dc in range(4):
                    g = f"G{dc % 2}"
                    claim(g, i * 5 + base[g] + (3 if more else 1) + dc // 2)
                    for ft in range(2):
                        for q in range(QUAD):
                            w2 = ring[:, slot_at(n0 + 4 * QUAD + 2 * q + ft), dc * COLS:(dc + 1) * COLS]
                            last = mm(psum[g][CAP * q:CAP * (q + 1), :], hid[:, q, ft * CAP:(ft + 1) * CAP], w2,
                                      ft == 0, ft == 1)
                    last.then_inc(filled[g], 1)
                for dc in range(4):
                    g = f"G{dc % 2}"
                    pe.wait_ge(emptied[g], i * 5 + (base[g] + (3 if more else 1) + dc // 2 + 1))
                    for b in range(TB):
                        s = f"S{b}"
                        claim(s, i * 4 + base[s] + dc)
                        mm(psum[s][:, :], spread[:, b, :], y[:, dc * COLS:(dc + 1) * COLS], True, True).then_inc(filled[s], 1)

            def experts(layer):
                pe.wait_ge(disp_ready, layer + 1)
                base = first_use["gather", layer]
                for c in range(4):
                    gather(layer, 0, c, base[f"G{c % 2}"] + c // 2)
                with pe.Fori(0, NQUAD - 1) as i:
                    quad(layer, i, True)
                quad(layer, NQUAD - 1, False)

            def overflow(layer):
                o = over[layer]
                over_x = xe[:, 0:QUAD, :].rearrange("p k n -> p (k n)").rearrange("p (k s) -> p k s", s=CAP)

                def expert(k, e):
                    pe.wait_ge(o["slots"], k + 1)
                    for kt in range(KT):
                        for b in range(TB):
                            last = mm(psum["G0"][:, kt * CAP:(kt + 1) * CAP], hv[:, b, kt, :], over_d[:, b, :], b == 0, b == 1)
                    last.then_inc(o["rows_filled"], 1)
                    for b in range(TB):
                        last = pe.transpose(psum["G1"][0:CAP, b * P:(b + 1) * P], over_g[:, b, :], ident[:, :])
                    last.then_inc(o["spread_filled"], 1)
                    pe.wait_ge(o["rows"], k + 1)
                    for kt in range(KT):
                        if kt % 8 == 0:
                            pe.wait_ge(o["w_loaded"], k * 96 + 32 * (kt // 8 + 1))
                        j = kt % QUAD
                        last = mm(psum["A0"][CAP * j:CAP * (j + 1), :], over_x[:, kt, :],
                                  over_w[:, :, (kt % 8) * FF:(kt % 8 + 1) * FF], kt < QUAD, kt >= KT - QUAD)
                        if kt % 8 == 7:
                            last.then_inc(o["w_used"], 1)
                    pe.wait_ge(o["acc"], k + 1)
                    for c in range(4):
                        last = mm(psum["T0"][:, c * CAP:(c + 1) * CAP], acc[:, 0, c * P:(c + 1) * P], fold[:, :], True, True)
                    last.then_inc(o["turned"], 1)
                    pe.wait_ge(o["hid"], k + 1)
                    pe.wait_ge(o["w_loaded"], k * 96 + 96)
                    for dc in range(4):
                        for ft in range(2):
                            last = mm(psum[("A1", "T1", "S0", "S1")[dc]][0:CAP, :], hid[:, 0, ft * CAP:(ft + 1) * CAP],
                                      over_w[:, ft, dc * COLS:(dc + 1) * COLS], ft == 0, ft == 1)
                    last.then_inc(o["w_used"], 1)
                    pe.wait_ge(o["y"], k + 1)
                    pe.wait_ge(o["spread"], k + 1)
                    for dc in range(4):
                        for b in range(TB):
                            last = mm(psum[BANKS[2 * dc + b]][:, :], spread[0:CAP, b, :], y[0:CAP, dc * COLS:(dc + 1) * COLS],
                                      True, True)
                    last.then_inc(o["scattered"], 1)

                overflow_passes(pe, layer, expert)

            pe.wait_ge(consts_made, 1)
            for layer in (0, 1):
                turn_rows("norm_mix", layer)
                wait_turned("norm_mix", layer)
                mix(layer)
                project_out(layer)
                turn_rows("norm_ffn", layer)
                wait_turned("norm_ffn", layer)
                route(layer)
                experts(layer)
                overflow(layer)

        @block.scalar
        def _(act):
            act.preload_act_table_set("natural_log_exp_and_others")

            def norm(n, phase, layer):
                for b in range(TB):
                    if n == 0:
                        act.wait_ge(x_loaded[b], 16)
                    act.activation(h[:, b, :], x[:, b, :], ACT.Square, accum_out=sumsq[:, b:b + 1])
                act.drain().then_inc(squares_done, 1)
                act.activation(rstd[:, :], sumsq[:, :], ACT.Ln, scale=1.0 / D, bias=eps_col[:, 0:1])
                act.drain()
                act.activation(rstd[:, :], rstd[:, :], ACT.Exp, scale=-0.5).then_inc(rstd_seed, 1)
                if phase:
                    copies_to_hT(act, act.copy, phase, layer, "T")

            def sb_group(g, late):
                base = first_use["mix", 0]
                for _, step, k in SB_EVENTS:
                    t, a = f"T{k % 2}", f"A{k % 2}"
                    if step == "chunk":
                        if late is not None:
                            copy_chunk(act, act.copy, 0, late, k, 0)
                        continue
                    if g is None:
                        continue
                    if step == "turn":
                        act.wait_ge(filled[t], g * 4 + (base[t] + k // 2 + 1))
                        act.mul(qT[:, k, :], psum[t][:, 0:T], SB_DH ** -0.5)
                        act.copy(kT[:, k, :], psum[t][:, T:2 * T]).then_inc(emptied[t], 1)
                    if step == "score":
                        act.wait_ge(clipped, g * SBG + k + 1)
                        s = soft[:, k % 2, :]
                        act.activation(s, s, ACT.Exp)
                        act.drain()
                        act.activation(s, s, ACT.Ln, bias=1.0).then_inc(softplus_log, 1)
                    if step == "suffix":
                        act.wait_ge(suffix_summed, g * SBG + k + 1)
                        act.activation(prob[:, k % 2, :], psum[a][:, 0:TRI], ACT.Exp).then_inc(emptied[a], 1)
                        act.drain().then_inc(prob_exp, 1)

            def ml_group(g, late):
                base = first_use["mix", 1]
                for _, step, k in ML_EVENTS:
                    t = f"T{k % 2}"
                    if step == "chunk":
                        if late is not None:
                            copy_chunk(act, act.copy, 1, late, k, 0)
                            if k == 2:
                                copy_chunk(act, act.copy, 1, late, k, 1)
                        continue
                    if g is None:
                        continue
                    if step == "turn":
                        act.wait_ge(filled[t], g * 4 + (base[t] + 1))
                        act.mul(qkT[:, k, 0, :], psum[t][:, 0:T], ML_DQ ** -0.5)
                        act.copy(qkT[:, k, 1, :], psum[t][:, T:2 * T]).then_inc(emptied[t], 1)
                    if step == "num":
                        act.wait_ge(head_squares, g * MLG + k + 1)
                        act.activation(hrs, ms, ACT.Ln)
                        act.drain()
                        act.activation(hrs, hrs, ACT.Exp, scale=-0.5).then_inc(head_seed, 1)
                    if step == "join":
                        act.wait_ge(filled[t], g * 4 + (base[t] + 4))
                        dst = oT[:, bass.ds((g * MLG + k) * 2, 2), :]
                        act.copy(dst, psum[t][:, :].rearrange("p (k t) -> p k t", k=2)).then_inc(emptied[t], 1)

            def gates_early():
                act.wait_ge(gate_clip, 1)
                act.activation(g_clip, g_clip, ACT.Exp)
                act.drain()
                act.activation(g_clip, g_clip, ACT.Ln, bias=1.0).then_inc(gate_log, 1)
                act.wait_ge(gate_rows, 1)
                act.activation(g_em, g_em, ACT.Exp)
                act.drain().then_inc(gate_exp, 1)

            def gates_decay():
                act.wait_ge(emptied["T1"], first_use["gates", 1]["T1"] + 1)
                for hd in range(ML_HEADS):
                    a = f"A{hd % 2}"
                    act.wait_ge(filled[a], first_use["gates", 1][a] + hd // 2 + 1)
                    act.activation(decay[:, hd, 0:T], psum[a][:, 0:T], ACT.Exp, bias=u_col[:, 0, hd:hd + 1])
                    act.activation(decay[:, hd, T:TRI], psum[a][:, P:T], ACT.Exp, bias=u_col[:, 1, hd:hd + 1]).then_inc(emptied[a], 1)
                    act.drain().then_inc(decay_exp, 1)

            def experts(layer):
                base = first_use["gather", layer]

                def take(c, n):
                    g = f"G{c % 2}"
                    act.wait_ge(filled[g], n + 1)
                    act.copy(xe[:, 4 * c:4 * c + 4, :].rearrange("p k n -> p (k n)"), psum[g][:, :]).then_inc(emptied[g], 1)

                act.wait_ge(group_shift, layer + 1)
                act.activation(gexp, gexp, ACT.Exp).then_inc(group_exp, 1)
                act.wait_ge(top2_gap, layer + 1)
                act.activation(dm, dm, ACT.Exp).then_inc(top2_exp, 1)
                for c in range(4):
                    take(c, base[f"G{c % 2}"] + c // 2)

                def quad(i, more):
                    base = first_use["moe", layer]

                    def silu(q):
                        t = f"T{q % 2}"
                        act.wait_ge(filled[t], i * 2 + (base[t] + q // 2 + 1))
                        act.wait_ge(exp_taken, i * QUAD + (layer * EXPERTS + q + 1))
                        act.activation(ex, psum[t][:, 0:2 * CAP], ACT.Exp, scale=-1.0).then_inc(silu_exp, 1)

                    for b in range(TB):
                        g = f"G{b}"
                        act.wait_ge(filled[g], i * 5 + (base[g] + 1))
                        act.copy(spread[:, b, :], psum[g][:, 0:P]).then_inc(emptied[g], 1)
                    for q in range(QUAD - 1):
                        silu(q)
                    if more:
                        for c in range(2):
                            take(c, i * 5 + (base[f"G{c}"] + 1))
                    silu(QUAD - 1)
                    if more:
                        for c in range(2, 4):
                            take(c, i * 5 + (base[f"G{c % 2}"] + 2))
                    for dc in range(4):
                        g = f"G{dc % 2}"
                        act.wait_ge(filled[g], i * 5 + (base[g] + (3 if more else 1) + dc // 2 + 1))
                        act.copy(y[:, dc * COLS:(dc + 1) * COLS], psum[g][:, :]).then_inc(emptied[g], 1)

                with act.Fori(0, NQUAD - 1) as i:
                    quad(i, True)
                quad(NQUAD - 1, False)

            def overflow(layer):
                o = over[layer]

                def expert(k, e):
                    act.wait_ge(o["rows_filled"], k + 1)
                    act.copy(xe[:, 0:QUAD, :].rearrange("p k n -> p (k n)"), psum["G0"][:, :]).then_inc(o["rows"], 1)
                    act.wait_ge(o["spread_filled"], k + 1)
                    act.copy(spread[0:CAP, :, :].rearrange("p b t -> p (b t)"), psum["G1"][0:CAP, 0:T]).then_inc(o["spread"], 1)
                    act.wait_ge(o["turned"], k + 1)
                    act.activation(ex, psum["T0"][:, 0:2 * CAP], ACT.Exp, scale=-1.0).then_inc(o["exp"], 1)
                    act.wait_ge(o["w_used"], k * 3 + 4)
                    for dc in range(4):
                        act.copy(y[0:CAP, dc * COLS:(dc + 1) * COLS], psum[("A1", "T1", "S0", "S1")[dc]][0:CAP, :])
                    act.drain().then_inc(o["y"], 1)

                overflow_passes(act, layer, expert)

            for b in range(TB):
                act.dma_start(x[:, b, :], x_in[0, b * P:(b + 1) * P, :]).then_inc(x_loaded[b], 16)
            act.wait_ge(consts_made, 1)
            for layer in (0, 1):
                group = ml_group if layer else sb_group
                norm(2 * layer, "norm_mix", layer)
                if layer:
                    gates_early()
                    copy_chunk(act, act.copy, 1, 0, 0, 0)
                    copy_chunk(act, act.copy, 1, 0, 1, 0)
                    gates_decay()
                    copy_chunk(act, act.copy, 1, 0, 2, 0)
                    copy_chunk(act, act.copy, 1, 0, 2, 1)
                else:
                    group(None, 0)
                with act.Fori(1, NGROUP) as i:
                    group(i - 1, i)
                group(NGROUP - 1, None)
                for b in ("G0", "G1", "S0", "S1"):
                    act.wait_ge(emptied[b], first_use["out", layer][b] + 2)
                norm(2 * layer + 1, "norm_ffn", layer)
                experts(layer)
                overflow(layer)
                act.wait_ge(moe_done, layer + 1)
            norm(4, None, 0)

        @block.vector
        def _(dve):
            def norm(n, phase, layer):
                dve.wait_ge(squares_done, n + 1)
                dve.tensor_scalar(mean_eps[:, :], sumsq[:, :], 1.0 / D, EPS, ALU.mult, ALU.add)
                dve.drain()
                dve.wait_ge(rstd_seed, n + 1)
                refine(rstd[:, :], mean_eps[:, :], newton[:, :])
                dve.wait_ge(grow_loaded, 16 * ({0: 0, 1: 1, 2: 2, 3: 4, 4: 5}[n] + 1))
                for b in range(TB):
                    dve.scalar_tensor_tensor(out=h[:, b, :], in0=x[:, b, :], scalar=rstd[:, b:b + 1],
                                             in1=grow[:, :], op0=ALU.mult, op1=ALU.mult
                                             ).then_inc(h_ready if phase else out_ready, 1)
                if phase:
                    dve.drain().then_inc(grow_used, 1)
                    copies_to_hT(dve, dve.tensor_copy, phase, layer, "A")

            def refine(r_, v_, t_):
                dve.tensor_tensor(t_, r_, r_, ALU.mult)
                dve.drain()
                dve.tensor_tensor(t_, t_, v_, ALU.mult)
                dve.drain()
                dve.tensor_scalar(t_, t_, -0.5, 1.5, ALU.mult, ALU.add)
                dve.drain()
                dve.tensor_tensor(r_, r_, t_, ALU.mult)
                dve.drain()

            def sb_group(g, late):
                base = first_use["mix", 0]
                for _, step, k in SB_EVENTS:
                    t, a = f"T{k % 2}", f"A{k % 2}"
                    if step == "chunk":
                        if late is not None:
                            copy_chunk(dve, dve.tensor_copy, 0, late, k, 1)
                        continue
                    if g is None:
                        continue
                    if step == "score":
                        dve.wait_ge(filled[a], g * 2 + (base[a] + k // 2 + 1))
                        dve.tensor_scalar(soft[:, k % 2, :], psum[a][:, 0:TRI], CLAMP, None, ALU.min).then_inc(clipped, 1)
                        dve.wait_ge(softplus_log, g * SBG + k + 1)
                        dve.tensor_tensor(sp[:, k % 2, :], soft[:, k % 2, :], psum[a][:, 0:TRI], ALU.max)
                        dve.drain().then_inc(softplus_full, 1)
                    if step == "out":
                        dve.wait_ge(filled[t], g * 4 + (base[t] + 2 + k // 2 + 1))
                        dve.tensor_copy(oT[:, bass.ds(g * SBG + k, 1), :], psum[t][:, 0:T].unsqueeze(1)).then_inc(emptied[t], 1)

            def ml_group(g, late):
                base = first_use["mix", 1]
                for _, step, k in ML_EVENTS:
                    t, a = f"T{k}", f"A{k % 2}"
                    if step == "chunk":
                        if late is not None and k < 2:
                            copy_chunk(dve, dve.tensor_copy, 1, late, k, 1)
                        continue
                    if g is None:
                        continue
                    hd = g * MLG + k
                    if step == "score":
                        dve.wait_ge(filled[a], g + (base[a] + 1))
                        dve.wait_ge(decay_masked, ML_HEADS)
                        dve.tensor_tensor(weights[:, k, :].unsqueeze(1), psum[a][:, 0:TRI].unsqueeze(1),
                                          decay[:, bass.ds(hd, 1), :], ALU.mult).then_inc(emptied[a], 1)
                        dve.drain().then_inc(weights_ready, 1)
                    if step == "num":
                        if k == 0:
                            for b in range(TB):
                                dve.wait_ge(emptied[f"G{b}"], g * 2 + (base[f"G{b}"] + 2))
                        for b in range(TB):
                            dve.tensor_scalar(sig[:, b, :], o_exp[:, b, k * ML_DV:(k + 1) * ML_DV], 1.0, None, ALU.add)
                        dve.drain()
                        dve.reciprocal(sig, sig)
                        for b in range(TB):
                            n = psum[f"T{b}"]
                            dve.wait_ge(filled[f"T{b}"], g * 4 + (base[f"T{b}"] + 1 + k + 1))
                            dve.tensor_scalar(ssq[:, b:b + 1], n[:, ML_DV:ML_DV + 1], -1.0, None, ALU.mult)
                        dve.drain()
                        for b in range(TB):
                            dve.tensor_tensor(den[:, b:b + 1], psum[f"T{b}"][:, ML_DV:ML_DV + 1], ssq[:, b:b + 1], ALU.max)
                        dve.drain()
                        dve.tensor_tensor(den.unsqueeze(2), den.unsqueeze(2), m_col[:, :, bass.ds(hd, 1)], ALU.max)
                        dve.drain()
                        dve.reciprocal(den, den)
                        dve.drain()
                        for b in range(TB):
                            n = psum[f"T{b}"]
                            dve.tensor_scalar(hs[:, b, :], n[:, 0:ML_DV], den[:, b:b + 1], None, ALU.mult
                                              ).then_inc(emptied[f"T{b}"], 1)
                        dve.drain()
                        for b in range(TB):
                            dve.tensor_tensor_reduce(junk, hs[:, b, :], hs[:, b, :], 1.0, 0.0,
                                                     ALU.mult, ALU.add, ssq[:, b:b + 1])
                            dve.drain()
                        dve.tensor_scalar(ms, ssq, 1.0 / ML_DV, EPS, ALU.mult, ALU.add)
                        dve.drain().then_inc(head_squares, 1)
                        dve.wait_ge(head_seed, g * MLG + k + 1)
                        refine(hrs, ms, hnw)
                        if k == 0:
                            dve.wait_ge(grow_loaded, 16 * 4)
                        for b in range(TB):
                            dve.scalar_tensor_tensor(out=hs[:, b, :], in0=hs[:, b, :], scalar=hrs[:, b:b + 1],
                                                     in1=grow[:, bass.ds(hd * ML_DV, ML_DV)],
                                                     op0=ALU.mult, op1=ALU.mult)
                        dve.drain()
                        dve.tensor_tensor(gated[:, k, :, :], hs, sig, ALU.mult)
                        dve.drain().then_inc(gated_ready, 1)

            def gates_early():
                pg = psum["T0"]
                dve.wait_ge(filled["T0"], first_use["gates", 1]["T0"] + 1)
                dve.tensor_scalar(g_y, pg[0:ML_HEADS, T:2 * T], gate_b[:, 1:2], -1.0, ALU.add, ALU.mult)
                dve.drain()
                dve.tensor_scalar(g_clip, g_y, CLAMP, None, ALU.min).then_inc(gate_clip, 1)
                dve.wait_ge(gate_log, 1)
                dve.tensor_tensor(g_sp, g_clip, g_y, ALU.max)
                dve.drain()
                dve.memset(g_y, 1.0)
                dve.drain()
                dve.tensor_tensor_scan(g_negb, g_y, g_sp, 0.0, ALU.mult, ALU.add)
                dve.drain()
                dve.scalar_tensor_tensor(out=g_u, in0=pg[0:ML_HEADS, 0:T], scalar=gate_b[:, 0:1], in1=g_negb,
                                         op0=ALU.add, op1=ALU.add).then_inc(emptied["T0"], 1)
                dve.drain()
                dve.tensor_tensor_scan(g_m, g_u, g_u, 0.0, ALU.max, ALU.max)
                dve.drain()
                dve.tensor_tensor(g_em, g_negb, g_m, ALU.subtract)
                dve.drain()
                dve.tensor_scalar(g_m, g_m, -1.0, None, ALU.mult)
                dve.drain().then_inc(gate_rows, 1)

            def gates_cols():
                dve.wait_ge(filled["T1"], first_use["gates", 1]["T1"] + 1)
                pg = psum["T1"]
                w = TB * ML_HEADS
                dve.tensor_copy(u_col.rearrange("p b h -> p (b h)"), pg[:, 0:w])
                dve.tensor_copy(m_col.rearrange("p b h -> p (b h)"), pg[:, w:2 * w]).then_inc(emptied["T1"], 1)

            def add_chunks(layer):
                base = first_use["out", layer]
                for c in range(4):
                    for b in range(TB):
                        bank = f"{'GS'[c % 2]}{b}"
                        dve.wait_ge(filled[bank], base[bank] + c // 2 + 1)
                        xs = x[:, b, c * COLS:(c + 1) * COLS]
                        dve.tensor_tensor(xs, xs, psum[bank][:, :], ALU.add).then_inc(emptied[bank], 1)

            def wide(view, shape):
                return view.to_broadcast(shape)

            def route(layer):
                base = first_use["route", layer]
                for b in range(TB):
                    dve.wait_ge(filled[f"S{b}"], base[f"S{b}"] + 1)
                    dve.tensor_copy(logits[:, b, :], psum[f"S{b}"][:, 0:ROUTER]).then_inc(emptied[f"S{b}"], 1)
                dve.tensor_scalar(rank, iota[:, 0:PER_GROUP], -1.0, float(PER_GROUP), ALU.mult, ALU.add)
                dve.drain()
                gl = logits[:, :, 0:GROUPS]
                g4 = [P, TB, GROUPS]
                e8 = [P, TB, PER_GROUP]

                def first_max(vals, top, cmp_, sel, shape, n):
                    dve.tensor_reduce(top, vals, AX, ALU.max)
                    dve.drain()
                    dve.tensor_tensor(cmp_, vals, wide(top, shape), ALU.is_equal)
                    dve.drain()
                    dve.tensor_tensor(cmp_, cmp_, wide(rank[:, 0:n].unsqueeze(1), shape), ALU.mult)
                    dve.drain()
                    dve.tensor_reduce(tie, cmp_, AX, ALU.max)
                    dve.drain()
                    dve.tensor_tensor(sel, cmp_, wide(tie, shape), ALU.is_equal)
                    dve.drain()

                first_max(gl, gmax, gcmp, gsel, g4, GROUPS)
                dve.tensor_tensor(gexp, gl, wide(gmax, g4), ALU.subtract).then_inc(group_shift, 1)
                el = logits[:, :, GROUPS:ROUTER].rearrange("p b (g e) -> p b g e", g=GROUPS)
                for b in range(TB):
                    dve.tensor_tensor(picked[:, b], el[:, b],
                                      wide(gsel[:, b, :].unsqueeze(2), [P, GROUPS, PER_GROUP]), ALU.mult)
                dve.drain()
                for b in range(TB):
                    dve.tensor_reduce(es[:, b, :].unsqueeze(2), picked[:, b].rearrange("p g e -> p e g"), AX, ALU.add)
                dve.drain()
                first_max(es, m1, cmp8, s1, e8, PER_GROUP)
                dve.scalar_tensor_tensor(out=tmp8, in0=s1, scalar=-3e38, in1=es, op0=ALU.mult, op1=ALU.add)
                dve.drain()
                first_max(tmp8, m2, cmp8, s2, e8, PER_GROUP)
                dve.tensor_tensor(dm, m2, m1, ALU.subtract).then_inc(top2_gap, 1)
                dve.tensor_tensor(tmp8, s1, s2, ALU.add)
                dve.drain()
                m4 = mask.rearrange("p b (g e) -> p b g e", g=GROUPS)
                ge = [P, GROUPS, PER_GROUP]
                for b in range(TB):
                    dve.tensor_tensor(m4[:, b], wide(gsel[:, b, :].unsqueeze(2), ge), wide(tmp8[:, b, :].unsqueeze(1), ge), ALU.mult)
                dve.drain().then_inc(mask_ready, 1)
                dve.wait_ge(group_exp, layer + 1)
                dve.tensor_reduce(gsum, gexp, AX, ALU.add)
                dve.drain()
                dve.reciprocal(psel, gsum)
                dve.wait_ge(top2_exp, layer + 1)
                dve.tensor_scalar(w1c, dm, 1.0, None, ALU.add)
                dve.drain()
                dve.reciprocal(w1c, w1c)
                dve.drain()
                dve.tensor_tensor(w1c, w1c, psel, ALU.mult)
                dve.drain()
                dve.tensor_tensor(w2c, w1c, dm, ALU.mult)
                dve.tensor_tensor(gate8, s1, wide(w1c, e8), ALU.mult)
                dve.drain()
                dve.tensor_tensor(tmp8, s2, wide(w2c, e8), ALU.mult)
                dve.drain()
                dve.tensor_tensor(gate8, gate8, tmp8, ALU.add)
                dve.drain()
                w4 = gates.rearrange("p b (g e) -> p b g e", g=GROUPS)
                for b in range(TB):
                    dve.tensor_tensor(w4[:, b], wide(gsel[:, b, :].unsqueeze(2), ge), wide(gate8[:, b, :].unsqueeze(1), ge), ALU.mult)
                dve.wait_ge(filled["G0"], base["G0"] + 1)
                pg = psum["G0"]
                dve.scalar_tensor_tensor(out=posm.rearrange("p b e -> p (b e)"), in0=pg[:, 0:TB * EXPERTS], scalar=1.0,
                                         in1=mask.rearrange("p b e -> p (b e)"), op0=ALU.add, op1=ALU.mult)
                dve.tensor_reduce(count_max[:, :], pg[0:1, 2 * EXPERTS:3 * EXPERTS], AX, ALU.max).then_inc(emptied["G0"], 1)
                dve.drain()
                dve.tensor_scalar(posm, posm, -1.0, None, ALU.add)
                dve.tensor_scalar(count_lt[:, :], thresholds[:, :], count_max[:, 0:1], None, ALU.is_lt)
                dve.drain()
                dve.tensor_reduce(extra_f[:, :], count_lt[:, :], AX, ALU.add)
                dve.drain()
                dve.tensor_copy(extra_i[:, :], extra_f[:, :])
                dve.drain().then_inc(extra_ready, 1)
                full = [P, EXPERTS, CAP]
                for b in range(TB):
                    dve.tensor_tensor(disp[:, b], wide(iota[:, :].unsqueeze(1), full),
                                      wide(posm[:, b, :].unsqueeze(2), full), ALU.is_equal)
                dve.drain().then_inc(disp_ready, 1)

            def experts(layer):
                base = first_use["moe", layer]

                def quad(i):
                    for b in range(TB):
                        dve.tensor_tensor(disp_g[:, b, :].rearrange("p (e s) -> p e s", e=QUAD),
                                          disp[:, b, bass.ds(i * QUAD, QUAD), :],
                                          wide(gates[:, b, bass.ds(i * QUAD, QUAD)].unsqueeze(2), [P, QUAD, CAP]), ALU.mult)
                    dve.drain().then_inc(disp_gated, 1)

                    def take(q):
                        a = f"A{q % 2}"
                        dve.wait_ge(filled[a], i * 2 + (base[a] + q // 2 + 1))
                        dve.tensor_copy(acc[:, q % 2, :], psum[a][:, :]).then_inc(emptied[a], 1)

                    def silu(q):
                        t = f"T{q % 2}"
                        dve.wait_ge(silu_exp, i * QUAD + (layer * EXPERTS + q + 1))
                        dve.tensor_scalar(sg, ex, 1.0, None, ALU.add).then_inc(exp_taken, 1)
                        dve.drain()
                        dve.reciprocal(sg, sg)
                        dve.drain()
                        dve.tensor_tensor(t13, sg, psum[t][:, 0:2 * CAP], ALU.mult)
                        dve.drain()
                        dve.tensor_tensor(hid[:, q, :], t13, psum[t][:, 2 * CAP:4 * CAP], ALU.mult).then_inc(emptied[t], 1)
                        dve.drain().then_inc(hid_ready, 1)

                    take(0)
                    for q in range(1, QUAD):
                        take(q)
                        silu(q - 1)
                    silu(QUAD - 1)
                    for dc in range(4):
                        for b in range(TB):
                            s = f"S{b}"
                            dve.wait_ge(filled[s], i * 4 + (base[s] + dc + 1))
                            xs = x[:, b, dc * COLS:(dc + 1) * COLS]
                            dve.tensor_tensor(xs, xs, psum[s][:, :], ALU.add).then_inc(emptied[s], 1)
                    dve.drain()

                with dve.Fori(0, NQUAD) as i:
                    quad(i)
                dve.drain()

            def overflow(layer):
                o = over[layer]
                dve.sem_inc(o["w_used"], 1)

                def expert(k, e):
                    for b in range(TB):
                        at = posm[:, b, bass.ds(e, 1)]
                        dve.tensor_scalar(at, at, -float(CAP), None, ALU.add)
                    dve.drain()
                    for b in range(TB):
                        dve.tensor_scalar(over_d[:, b, :], iota[:, :], posm[:, b, bass.ds(e, 1)], None, ALU.is_equal)
                    dve.drain()
                    for b in range(TB):
                        dve.tensor_scalar(over_g[:, b, :], over_d[:, b, :], gates[:, b, bass.ds(e, 1)], None, ALU.mult)
                    dve.drain().then_inc(o["slots"], 1)
                    dve.wait_ge(o["w_used"], k * 3 + 3)
                    dve.tensor_copy(acc[:, 0, :], psum["A0"][:, :]).then_inc(o["acc"], 1)
                    dve.wait_ge(o["exp"], k + 1)
                    dve.tensor_scalar(sg, ex, 1.0, None, ALU.add)
                    dve.drain()
                    dve.reciprocal(sg, sg)
                    dve.drain()
                    dve.tensor_tensor(t13, sg, psum["T0"][:, 0:2 * CAP], ALU.mult)
                    dve.drain()
                    dve.tensor_tensor(hid[:, 0, :], t13, psum["T0"][:, 2 * CAP:4 * CAP], ALU.mult)
                    dve.drain().then_inc(o["hid"], 1)
                    dve.wait_ge(o["scattered"], k + 1)
                    for dc in range(4):
                        for b in range(TB):
                            xs = x[:, b, dc * COLS:(dc + 1) * COLS]
                            dve.tensor_tensor(xs, xs, psum[BANKS[2 * dc + b]][:, :], ALU.add)
                    dve.drain()

                overflow_passes(dve, layer, expert)

            dve.wait_ge(consts_made, 1)
            dve.tensor_scalar(thresholds[:, :], iota[0:1, 0:T // CAP - 1], float(CAP), float(CAP), ALU.mult, ALU.add)
            dve.drain().then_inc(exp_taken, 1)
            for b in range(TB):
                dve.wait_ge(x_loaded[b], 16)
            for layer in (0, 1):
                group = ml_group if layer else sb_group
                norm(2 * layer, "norm_mix", layer)
                if layer:
                    gates_early()
                    copy_chunk(dve, dve.tensor_copy, 1, 0, 0, 1)
                    gates_cols()
                    copy_chunk(dve, dve.tensor_copy, 1, 0, 1, 1)
                else:
                    group(None, 0)
                with dve.Fori(1, NGROUP) as i:
                    group(i - 1, i)
                group(NGROUP - 1, None)
                if layer:
                    dve.drain().then_inc(grow_used, 1)
                add_chunks(layer)
                dve.drain()
                norm(2 * layer + 1, "norm_ffn", layer)
                route(layer)
                experts(layer)
                overflow(layer)
                dve.drain().then_inc(moe_done, 1)
            norm(4, None, 0)



_INS = ["x", "norm_mix", "norm_ffn", "norm_final", "sb_w_in", "sb_w_out", "ml_w_in", "ml_b_i", "ml_b_f",
        "ml_g_head", "ml_w_out", "moe_w_group", "moe_b_group", "moe_w_expert", "moe_b_expert",
        "moe_w1", "moe_w3", "moe_w2"]


def kernel(**inputs):
    import concourse.bacc as bacc
    from concourse.bass_utils import run_bass_kernel_spmd

    nc = bacc.Bacc("TRN2", target_bir_lowering=False, num_devices=1)
    arrays, args = {}, []
    for name in _INS:
        a = np.ascontiguousarray(inputs[name])
        arrays[f"in_{name}"] = a
        args.append(nc.dram_tensor(f"in_{name}", a.shape, mybir.dt.from_np(a.dtype), kind="ExternalInput").ap())
    args.append(nc.dram_tensor("out_x", (1, T, D), F32, kind="ExternalOutput").ap())
    build(nc, *args)
    r = run_bass_kernel_spmd(nc, [arrays], core_ids=[0])
    return r.results[0]["out_x"]
```

```python
from contextlib import ExitStack

import numpy as np

import concourse.bass as bass
from concourse import mybir

F32 = mybir.dt.float32
F32R = mybir.dt.float32r
I32 = mybir.dt.int32
ALU = mybir.AluOpType
ACT = mybir.ActivationFunctionType
AX = mybir.AxisListType.X

P = 128
D = 2048
T = 256
TB = T // P
KT = D // P
EPS = 1e-6
SB_HEADS, SB_DH = 16, 128
ML_HEADS, ML_DQ, ML_DV = 8, 128, 256
GROUPS, PER_GROUP = 4, 8
EXPERTS = GROUPS * PER_GROUP
FF = D // 8
ROUTER = GROUPS + EXPERTS
CAP = 32
QUAD = P // CAP
NQUAD = EXPERTS // QUAD
SLOTS = 12
SLOT = 2048
COLS = 512
CSLOT = 4
TRI = 384
CLAMP = 40.0
SBG = 4
MLG = 2
NGROUP = 4
BANKS = ["T0", "T1", "A0", "A1", "G0", "G1", "S0", "S1"]
NORM_BANKS = ["T0", "T1", "A0", "A1"]

RAW = 4
MIX_SLOTS = 12 * NGROUP + 16
OUT_ORDER = [(0, 0), (0, 1), (0, 2), (1, 0), (1, 1), (1, 2), (0, 3), (1, 3),
             (2, 0), (2, 1), (2, 2), (2, 3), (3, 0), (3, 1), (3, 2), (3, 3)]

SB_STEPS = [(0, "turn", 0), (0, "turn", 1), (0, "turn", 2), (0, "turn", 3),
            (4, "score", 0), (10, "score", 1), (14, "suffix", 0), (20, "suffix", 1),
            (24, "out", 0), (30, "out", 1), (34, "score", 2), (38, "score", 3),
            (44, "suffix", 2), (48, "suffix", 3), (54, "out", 2), (58, "out", 3)]
ML_STEPS = [(0, "turn", 0), (0, "turn", 1), (2, "score", 0), (4, "score", 1), (10, "num", 0),
            (18, "gate", 0), (26, "num", 1), (34, "gate", 1), (38, "join", 0), (50, "join", 1)]
GATE_STEPS = [(0, "logits", 0), (10, "rows", 0), (34, "columns", 0)] + [(66 + 3 * n, "spread", n) for n in range(8)]


def schedule(steps, slots, ends, scale=1.0):
    found = [(8 * (j - 1), 0, "split", j) for j in range(1, slots + 1)]
    found += [(int(at * scale), 1 + n / 100, name, k) for n, (at, name, k) in enumerate(steps)]
    found += [(at, 0.5, "chunk", c) for c, at in enumerate(ends)]
    return [(at, name, k) for at, _, name, k in sorted(found)]


GROUP_ENDS = (32, 64, 96)
OUT_ENDS = (56, 64, 96, 128)
SCHEDULES = {}
for _layer, _steps in ((0, SB_STEPS), (1, ML_STEPS)):
    SCHEDULES[_layer, "first"] = schedule(GATE_STEPS if _layer else [], 12, GROUP_ENDS)
    SCHEDULES[_layer, "group"] = schedule(_steps, 12, GROUP_ENDS)
    SCHEDULES[_layer, "out"] = schedule(_steps, 15, OUT_ENDS, 0.75)


def bank_uses():
    total = {b: 0 for b in BANKS}
    first = {}

    def phase(name, **n):
        first[name] = dict(total)
        for k, v in n.items():
            for b in BANKS:
                if b == k or b[0] == k:
                    total[b] += v

    for layer in (0, 1):
        phase(("norm_mix", layer), T=2, A=2)
        if layer:
            phase(("gates", layer), T0=2, T1=1, A=ML_HEADS // 2)
        phase(("mix", layer), G=2 * NGROUP, S=NGROUP, T=4 * NGROUP, A=(1 if layer else 2) * NGROUP)
        phase(("out", layer), G=2, S=2)
        phase(("norm_ffn", layer), T=2, A=2)
        phase(("route", layer), S=1, G0=1)
        phase(("gather", layer), G=2)
        phase(("moe", layer), G=5 * NQUAD - 2, A=2 * NQUAD, T=2 * NQUAD, S=4 * NQUAD)
    return first


def build(nc, x_in, norm_mix, norm_ffn, norm_final, sb_w_in, sb_w_out, ml_w_in, ml_b_i, ml_b_f,
          ml_g_head, ml_w_out, moe_w_group, moe_b_group, moe_w_expert, moe_b_expert,
          moe_w1, moe_w3, moe_w2, out):
    first_use = bank_uses()
    ctx = ExitStack()
    with ctx:
        def sb(name, shape, dt=F32):
            return ctx.enter_context(nc.sbuf_tensor(name, shape, dt))

        def sem(name):
            return ctx.enter_context(nc.semaphore(name))

        place = [(nc.sbuf_base + 63) // 64 * 64]

        def at(name, offset, shape, dt=F32):
            return nc.alloc_sbuf_tensor_at(name, shape, dt, offset=offset)

        def sb(name, shape, dt=F32):
            size = 4 * int(np.prod(shape[1:]))
            offset = place[0]
            place[0] += (size + 63) // 64 * 64
            return at(name, offset, shape, dt)

        def sem(name):
            return ctx.enter_context(nc.semaphore(name))

        KB = 1024
        x = sb("x", [P, TB, D])
        grow = sb("grow", [P, D])
        ident = sb("ident", [P, P])
        neg_suffix = sb("neg_suffix", [P, P])
        neg_ones = sb("neg_ones", [P, P])
        before = sb("before", [P, P])
        ones = sb("ones", [P, P])
        fold = sb("fold", [P, CAP])
        iota = sb("iota", [P, CAP])
        thresholds = sb("thresholds", [1, T // CAP - 1])
        eps_col = sb("eps_col", [P, 1])
        router_w = sb("router_w", [P, KT, ROUTER])
        router_b = sb("router_b", [1, ROUTER])
        gate_w = sb("gate_w", [P, KT, 2 * ML_HEADS])
        gate_b = sb("gate_b", [ML_HEADS, 2])
        sumsq = sb("sumsq", [P, TB])
        mean_eps = sb("mean_eps", [P, TB])
        rstd = sb("rstd", [P, TB])
        newton = sb("newton", [P, TB])
        extra_f = sb("extra_f", [1, 1])
        extra_i = sb("extra_i", [1, 1], I32)
        count_max = sb("count_max", [1, 1])
        count_lt = sb("count_lt", [1, T // CAP - 1])

        rows_at = place[0]
        h = sb("h", [P, TB, D])
        o_hi = at("o_hi", rows_at, [P, KT, T], F32R)
        turned_at = place[0]
        hT_hi = sb("hT_hi", [P, KT, T], F32R)
        hT_lo = sb("hT_lo", [P, KT, T], F32R)
        hT = at("hT", turned_at, [P, KT, T])
        arena_two = at("arena_two", turned_at + 16 * KB, [P, 4096])
        ring_at = place[0]
        ring = sb("ring", [P, SLOTS, SLOT])
        w_hi = at("w_hi", ring_at + 4 * 8 * KB, [P, 2, SLOT], F32R)
        w_lo = at("w_lo", ring_at + 6 * 8 * KB, [P, 2, SLOT], F32R)
        o_lo = at("o_lo", ring_at + 8 * 8 * KB, [P, KT, T], F32R)
        arena_three = at("arena_three", ring_at + 10 * 8 * KB, [P, 4096])
        arena = sb("arena", [P, 7168])
        assert place[0] <= nc.sbuf_usable_end, place[0]

        over_w = hT[:, :, :].rearrange("p k t -> p (k t)")[:, 0:2 * SLOT].rearrange("p (s n) -> p s n", s=2)
        hv = h[:, :, :].rearrange("p b (c k) -> p b k c", k=KT)

        class Region:
            def __init__(self, whole):
                self.whole, self.at = whole, 0

            def __call__(self, *shape):
                n = int(np.prod(shape))
                view = self.whole[:, self.at:self.at + n]
                self.at += n
                assert self.at <= self.whole.shape[1], self.at
                names = " ".join("abcd"[:len(shape)])
                sizes = {"abcd"[k]: s for k, s in enumerate(shape) if k}
                return view.rearrange(f"p ({names}) -> p {names}", **sizes) if len(shape) > 1 else view

        r = Region(arena)
        q_raw, k_raw, v_raw = r(TB, COLS), r(TB, COLS), r(TB, COLS)
        qT, kT = r(SBG, T), r(SBG, T)
        r = Region(arena_three)
        soft, sp, prob = r(2, TRI), r(2, TRI), r(2, TRI)
        r = Region(arena_three)
        decay = r(ML_HEADS, TRI)
        weights = r(MLG, TRI)
        r = Region(arena)
        qk_raw, v_one, o_exp = r(TB, COLS), r(TB, MLG, ML_DV + 1), r(TB, COLS)
        at_selector = r.at
        qkT = r(MLG, 2, T)
        at_rows = r.at
        gated = r(MLG, TB, ML_DV)
        hs = r(TB, ML_DV)
        r.at = at_rows + 7 * T
        gate_cols = r(TB, 2 * ML_HEADS)
        u_col, m_col = r(TB, ML_HEADS), r(TB, ML_HEADS)
        den, ssq, ms, hrs, hnw = r(TB), r(TB), r(TB), r(TB), r(TB)
        r.at = at_rows
        g_y, g_clip, g_sp, g_negb, g_u, g_m, g_em = (r(T)[0:ML_HEADS] for _ in range(7))
        r.at = at_selector
        selector = r(ML_HEADS, P)[0:ML_HEADS]
        r = Region(arena_two)
        disp = r(TB, EXPERTS, CAP)
        acc = r(2, COLS)
        disp_g, spread = r(TB, P), r(TB, P)
        hid = r(QUAD, 2 * CAP)
        r = Region(arena)
        xe = r(KT, P)
        y = r(D)
        ex, sg, t13 = r(2 * CAP), r(2 * CAP), r(2 * CAP)
        logits = r(TB, ROUTER)
        gsel, gexp, gcmp = r(TB, GROUPS), r(TB, GROUPS), r(TB, GROUPS)
        gmax, gsum, tie, psel = r(TB, 1), r(TB, 1), r(TB, 1), r(TB, 1)
        picked = r(TB, GROUPS, PER_GROUP)
        es, cmp8, s1, s2, gate8, tmp8 = (r(TB, PER_GROUP) for _ in range(6))
        m1, m2, dm, w1c, w2c = (r(TB, 1) for _ in range(5))
        gates, mask, posm = (r(TB, EXPERTS) for _ in range(3))
        rank = r(PER_GROUP)
        over_d, over_g = r(TB, CAP), r(TB, CAP)

        psum = {b: ctx.enter_context(nc.psum_tensor(f"psum_{b}", [P, 512], F32)) for b in BANKS}

        filled = {b: sem(f"filled_{b}") for b in BANKS}
        emptied = {b: sem(f"emptied_{b}") for b in BANKS}
        slot_loaded = [sem(f"slot_loaded_{n}") for n in range(SLOTS)]
        raw_loaded = [sem(f"raw_loaded_{n}") for n in range(RAW)]
        hi_made = sem("hi_made")
        lo_made = sem("lo_made")
        split_read = sem("split_read")
        row_hi_made = sem("row_hi_made")
        out_hi_made = sem("out_hi_made")
        x_loaded = [sem(f"x_loaded_{b}") for b in range(TB)]
        grow_loaded = sem("grow_loaded")
        grow_used = sem("grow_used")
        small_loaded = [sem("small_loaded_0"), sem("small_loaded_1")]
        consts_made = sem("consts_made")
        squares_done = sem("squares_done")
        mean_ready = sem("mean_ready")
        rstd_seed = sem("rstd_seed")
        h_ready = sem("h_ready")
        clipped = sem("clipped")
        softplus_log = sem("softplus_log")
        softplus_full = sem("softplus_full")
        softplus_masked = sem("softplus_masked")
        suffix_summed = sem("suffix_summed")
        prob_exp = sem("prob_exp")
        mask_begun = sem("mask_begun")
        prob_masked = sem("prob_masked")
        gate_taken = sem("gate_taken")
        gate_clip = sem("gate_clip")
        gate_log = sem("gate_log")
        gate_rows = sem("gate_rows")
        gate_exp = sem("gate_exp")
        decay_exp = sem("decay_exp")
        decay_masked = sem("decay_masked")
        ones_set = sem("ones_set")
        weights_ready = sem("weights_ready")
        head_squares = sem("head_squares")
        head_seed = sem("head_seed")
        gated_ready = sem("gated_ready")
        group_shift = sem("group_shift")
        group_exp = sem("group_exp")
        top2_gap = sem("top2_gap")
        top2_exp = sem("top2_exp")
        mask_ready = sem("mask_ready")
        disp_ready = sem("disp_ready")
        extra_ready = sem("extra_ready")
        disp_gated = sem("disp_gated")
        silu_exp = sem("silu_exp")
        exp_taken = sem("exp_taken")
        hid_ready = sem("hid_ready")
        moe_done = sem("moe_done")
        over = [{n: sem(f"over_{n}_{layer}") for n in (
            "slots", "rows_filled", "rows", "spread_filled", "spread", "w_loaded", "w_used", "acc",
            "turned", "exp", "hid", "y", "scattered")} for layer in (0, 1)]
        out_ready = sem("out_ready")
        out_stored = sem("out_stored")

        block = ctx.enter_context(nc.Block())

        def norm_bank(u):
            return NORM_BANKS[u % 4], u // 4, 4 * (u % 4)

        def tiles(view, b, k0):
            return view[:, k0:k0 + 4, b * P:(b + 1) * P]

        def group_bank(c, b):
            return f"{'GSG'[c]}{b}"

        def chunk_filled(layer, i, c, b):
            bank = group_bank(c, b)
            return filled[bank], i * (1 if c == 1 else 2) + (first_use["mix", layer][bank] + c // 2 + 1)

        def out_filled(layer, c, b):
            bank = f"{'GS'[c % 2]}{b}"
            return filled[bank], first_use["out", layer][bank] + c // 2 + 1

        def copy_chunk(eng, copy, layer, i, c, b):
            bank = group_bank(c, b)
            eng.wait_ge(*chunk_filled(layer, i, c, b))
            src = psum[bank][:, :]
            if layer and c == 2:
                eng.activation(o_exp[:, b, :], src, ACT.Exp, scale=-1.0).then_inc(emptied[bank], 1)
            elif layer and c == 1:
                copy(v_one[:, b, :, 0:ML_DV], src.rearrange("p (h n) -> p h n", h=MLG)).then_inc(emptied[bank], 1)
            else:
                dst = qk_raw if layer else (q_raw, k_raw, v_raw)[c]
                copy(dst[:, b, :], src).then_inc(emptied[bank], 1)

        def mix_slot(layer, i, j):
            return i * 12 + (layer * MIX_SLOTS + j)

        def split_was_read(layer, i, j):
            if j < 0:
                i, j = i - 1, j + 12
            if isinstance(i, int) and i == NGROUP:
                c, n = OUT_ORDER[j]
                if n == 3:
                    return out_filled(layer, c, 1)
                done = sum(1 for _, m in OUT_ORDER[:j + 1] if m < 3)
                return split_read, layer * (9 * NGROUP + 12) + 9 * NGROUP + done
            c = j // 4
            if j % 4 == 3:
                return chunk_filled(layer, i, c, 1)
            return split_read, i * 9 + (layer * (9 * NGROUP + 12) + 3 * c + j % 4 + 1)

        def split_hi(act, layer, i, j):
            n = mix_slot(layer, i, j)
            act.wait_ge(raw_loaded[j % RAW], i * (16 * 12 // RAW) + 16 * ((layer * MIX_SLOTS + j) // RAW + 1))
            if not (isinstance(i, int) and i == 0 and j < 2):
                act.wait_ge(*split_was_read(layer, i, j - 2))
            act.copy(w_hi[:, j % 2, :], ring[:, j % RAW, :]).then_inc(hi_made, 1)

        def split_lo(dve, layer, i, j):
            dve.wait_ge(hi_made, mix_slot(layer, i, j) + 1)
            dve.tensor_tensor(w_lo[:, j % 2, :], ring[:, j % RAW, :], w_hi[:, j % 2, :].bitcast(F32),
                              ALU.subtract).then_inc(lo_made, 1)

        def overflow_passes(eng, layer, expert):
            eng.wait_ge(extra_ready, layer + 1)
            extra = eng.value_load(extra_i[0:1, 0:1], min_val=0, max_val=T // CAP - 1)
            with eng.If(extra > 0):
                with eng.Fori(0, extra) as turn:
                    with eng.Fori(0, EXPERTS) as e:
                        expert(turn * EXPERTS + e, e)

        def slot_at(n):
            return n % SLOTS

        def slot_value(layer, i, per, j):
            return 16 * ((layer * 6 * EXPERTS + j) // SLOTS + 1) + i * (16 * per // SLOTS)

        def w13_tile(n, k):
            s = slot_at(n + 2 * (k // 8))
            return ring[:, s:s + 2, (k % 8) * FF:(k % 8 + 1) * FF]

        @block.sync
        def _(sp_eng):
            def mix_stream(layer, i):
                w = (ml_w_in if layer else sb_w_in)[0].rearrange("(p k) n -> p k n", k=KT)
                for j in range(12):
                    c, k0 = j // CSLOT, 4 * (j % CSLOT)
                    if layer and isinstance(i, int) and i == 0 and j == 0:
                        base = first_use["moe", 0]
                        sp_eng.wait_ge(filled["A1"], base["A1"] + 2 * NQUAD)
                    elif not (isinstance(i, int) and i == 0 and j < RAW):
                        sp_eng.wait_ge(lo_made, mix_slot(layer, i, j) + (1 - RAW))
                    if layer and c == 0:
                        part, k8 = j // 2, 8 * (j % 2)
                        dst = ring[:, j % RAW, :].rearrange("p (k n) -> p k n", k=8)
                        src = w[:, k8:k8 + 8, bass.ds(i * FF + part * ML_HEADS * ML_DQ, FF)]
                    else:
                        dst = ring[:, j % RAW, :].rearrange("p (k n) -> p k n", k=4)
                        src = w[:, k0:k0 + 4, bass.ds(i * COLS + c * D, COLS)]
                    sp_eng.dma_start(dst, src).then_inc(raw_loaded[j % RAW], 16)

            def out_stream(layer):
                w = (ml_w_out if layer else sb_w_out)[0].rearrange("(k p) n -> p k n", p=P)
                for j, (c, n) in enumerate(OUT_ORDER):
                    sp_eng.wait_ge(lo_made, mix_slot(layer, NGROUP, j) + (1 - RAW))
                    sp_eng.dma_start(ring[:, j % RAW, :].rearrange("p (k n) -> p k n", k=4),
                                     w[:, 4 * n:4 * n + 4, c * COLS:(c + 1) * COLS]).then_inc(raw_loaded[j % RAW], 16)

            def freed_moe(layer, i):
                base = first_use["moe", layer]
                last = isinstance(i, int) and i == NQUAD - 1
                return ([(filled[f"A{q % 2}"], i * 2 + (base[f"A{q % 2}"] + q // 2 + 1)) for q in range(QUAD)]
                        + [(filled["G1"], i * 5 + (base["G1"] + (3 if last else 5)))] * 2)

            def moe_stream(layer, i, before):
                freed = before[-3:] + freed_moe(layer, i)
                for j in range(6 * QUAD):
                    if j % CSLOT == 0:
                        sp_eng.wait_ge(*freed[j // CSLOT])
                    s = slot_at(j)
                    if j < 4 * QUAD:
                        w = (moe_w1, moe_w3)[j % 2][layer].rearrange("e (p k) f -> p e (k f)", k=KT)
                        e, half = j // 4, (j % 4) // 2
                        src = w[:, bass.ds(i * QUAD + e, 1), half * SLOT:(half + 1) * SLOT]
                    else:
                        e, ft = (j - 4 * QUAD) // 2, j % 2
                        w = moe_w2[layer].rearrange("e (k p) n -> k p e n", p=P)
                        src = w[ft, :, bass.ds(i * QUAD + e, 1), :]
                    sp_eng.dma_start(ring[:, s:s + 1, :], src).then_inc(slot_loaded[s], 16)

            def overflow(layer):
                o = over[layer]

                def expert(k, e):
                    for half in range(2):
                        sp_eng.wait_ge(o["w_used"], k * 3 + (half + 1))
                        for n, w in enumerate((moe_w1, moe_w3)):
                            src = w[layer].rearrange("e (p k) f -> p e (k f)", k=KT)
                            sp_eng.dma_start(over_w[:, n:n + 1, :], src[:, bass.ds(e, 1), half * SLOT:(half + 1) * SLOT]
                                             ).then_inc(o["w_loaded"], 16)
                    sp_eng.wait_ge(o["w_used"], k * 3 + 3)
                    src = moe_w2[layer].rearrange("e (k p) n -> k p e n", p=P)
                    for ft in range(2):
                        sp_eng.dma_start(over_w[:, ft:ft + 1, :], src[ft, :, bass.ds(e, 1), :]
                                         ).then_inc(o["w_loaded"], 16)

                overflow_passes(sp_eng, layer, expert)

            for layer in (0, 1):
                mix_stream(layer, 0)
                with sp_eng.Fori(1, NGROUP) as g:
                    mix_stream(layer, g)
                out_stream(layer)
                moe_stream(layer, 0, [(lo_made, (layer + 1) * MIX_SLOTS)] + [out_filled(layer, 3, 1)] * 2)
                with sp_eng.Fori(1, NQUAD) as i:
                    moe_stream(layer, i, freed_moe(layer, i - 1))
                overflow(layer)
            for b in range(TB):
                sp_eng.wait_ge(out_ready, b + 1)
                sp_eng.dma_start(out[0, b * P:(b + 1) * P, :], h[:, b, :]).then_inc(out_stored, 16)
            sp_eng.wait_ge(out_stored, 16 * TB)

        @block.gpsimd
        def _(pool):
            def load_grow(row, n):
                if n:
                    pool.wait_ge(grow_used, n)
                pool.dma_start(grow[:, :], row.partition_broadcast(P)).then_inc(grow_loaded, 16)

            def load_small(layer):
                s = small_loaded[layer]
                pool.dma_start(router_w[:, :, 0:GROUPS], moe_w_group[layer].rearrange("(p k) n -> p k n", k=KT)).then_inc(s, 16)
                pool.dma_start(router_w[:, :, GROUPS:ROUTER], moe_w_expert[layer].rearrange("(p k) n -> p k n", k=KT)).then_inc(s, 16)
                pool.dma_start(router_b[:, 0:GROUPS], moe_b_group[layer:layer + 1, :]).then_inc(s, 16)
                pool.dma_start(router_b[:, GROUPS:ROUTER], moe_b_expert[layer:layer + 1, :]).then_inc(s, 16)

            load_grow(norm_mix[0], 0)
            pool.memset(ident[:, :], 0.0)
            pool.memset(fold[:, :], 0.0)
            pool.memset(neg_ones[:, :], -1.0)
            pool.memset(ones[:, :], 1.0)
            pool.memset(eps_col[:, :], EPS)
            pool.iota(iota[:, :], pattern=[[1, CAP]], base=0, channel_multiplier=0,
                      allow_small_or_imprecise_dtypes=True)
            pool.drain()
            pool.affine_select(out=ident[:, :], in_=ident[:, :], compare_op=ALU.not_equal, fill=1.0,
                               base=0, pattern=[[-1, P]], channel_multiplier=1)
            pool.affine_select(out=neg_suffix[:, :], in_=neg_ones[:, :], compare_op=ALU.is_ge, fill=0.0,
                               base=0, pattern=[[-1, P]], channel_multiplier=1)
            pool.affine_select(out=before[:, :], in_=ones[:, :], compare_op=ALU.is_gt, fill=0.0,
                               base=0, pattern=[[1, P]], channel_multiplier=-1)
            for q in range(QUAD):
                pool.affine_select(out=fold[:, :], in_=fold[:, :], compare_op=ALU.not_equal, fill=1.0,
                                   base=-q * CAP, pattern=[[-1, CAP]], channel_multiplier=1)
                pool.drain()
            pool.drain().then_inc(consts_made, 1)
            load_small(0)
            pool.dma_start(gate_w[:, :, :], ml_w_in[0, :, 3 * D:3 * D + 2 * ML_HEADS].rearrange("(p k) n -> p k n", k=KT)).then_inc(small_loaded[0], 16)
            pool.dma_start(gate_b[:, 0:1], ml_b_i.rearrange("o n -> n o")).then_inc(small_loaded[0], 16)
            pool.dma_start(gate_b[:, 1:2], ml_b_f.rearrange("o n -> n o")).then_inc(small_loaded[0], 16)
            load_grow(norm_ffn[0], 1)

            def keep_causal(view, strict):
                pool.affine_select(out=view, in_=view, compare_op=ALU.is_gt if strict else ALU.is_ge,
                                   fill=0.0, base=0, pattern=[[0, 2], [1, P]], channel_multiplier=-1)
                return pool.drain()

            def diagonals(tile):
                return tile.rearrange("p (c n) -> p c n", n=P)[:, 0:3:2, :]

            def sb_group(g):
                for _, step, k in SB_STEPS:
                    if step == "score":
                        pool.wait_ge(softplus_full, g * SBG + k + 1)
                        pool.sem_inc(mask_begun, 1)
                        keep_causal(diagonals(sp[:, k % 2, :]), True).then_inc(softplus_masked, 1)
                    if step == "suffix":
                        pool.wait_ge(prob_exp, g * SBG + k + 1)
                        pool.sem_inc(mask_begun, 1)
                        keep_causal(diagonals(prob[:, k % 2, :]), True).then_inc(prob_masked, 1)

            with pool.Fori(0, NGROUP) as g:
                sb_group(g)

            load_grow(norm_mix[1], 2)
            pool.wait_ge(mask_ready, 1)
            load_small(1)
            pool.wait_ge(h_ready, 3 * TB)
            pool.memset(v_one[:, :, :, ML_DV:ML_DV + 1], 1.0)
            pool.memset(selector, 1.0)
            pool.drain()
            pool.affine_select(out=selector, in_=selector, compare_op=ALU.is_equal, fill=0.0, base=0,
                               pattern=[[-1, ML_HEADS], [0, P]], channel_multiplier=1)
            pool.drain().then_inc(ones_set, 1)
            load_grow(ml_g_head[0], 3)
            for hd in range(ML_HEADS):
                pool.wait_ge(decay_exp, hd + 1)
                keep_causal(diagonals(decay[:, hd, :]), False).then_inc(decay_masked, 1)
            load_grow(norm_ffn[1], 4)
            load_grow(norm_final, 5)

        @block.tensor
        def _(pe):
            def claim(b, n):
                if not (isinstance(n, int) and n == 0):
                    pe.wait_ge(emptied[b], n)

            def mm(dst, lhsT, rhs, start, stop):
                return pe.matmul(dst, lhsT, rhs, start=start, stop=stop, skip_group_check=True)

            def turn_rows(phase, layer):
                base = first_use[phase, layer]
                for u in range(2 * KT // 4):
                    bank = NORM_BANKS[u % 4]
                    b, k0 = u // 4, 4 * (u % 4)
                    if u % 4 == 0:
                        pe.wait_ge(h_ready, {("norm_mix", 0): 0, ("norm_ffn", 0): 1, ("norm_mix", 1): 2,
                                             ("norm_ffn", 1): 3}[phase, layer] * TB + b + 1)
                    claim(bank, base[bank] + u // 4)
                    for k in range(4):
                        last = pe.transpose(psum[bank][:, k * P:(k + 1) * P], hv[:, b, k0 + k, :], ident[:, :])
                    last.then_inc(filled[bank], 1)

            def wait_turned(phase, layer):
                for b in NORM_BANKS:
                    pe.wait_ge(emptied[b], first_use[phase, layer][b] + 2)

            def gates_logits():
                pe.wait_ge(small_loaded[0], 16 * 7)
                claim("T0", first_use["gates", 1]["T0"])
                for b in range(TB):
                    for part in (hT_hi, hT_lo):
                        for k in range(KT):
                            last = mm(psum["T0"][:, b * 2 * ML_HEADS:(b + 1) * 2 * ML_HEADS],
                                      part[:, k, b * P:(b + 1) * P].bitcast(F32), gate_w[:, k, :],
                                      part is hT_hi and k == 0, part is hT_lo and k == KT - 1)
                last.then_inc(filled["T0"], 1)

            def gates_rows():
                pe.wait_ge(gate_taken, 1)
                claim("T0", first_use["gates", 1]["T0"] + 1)
                for n in range(2):
                    for b in range(TB):
                        last = pe.transpose(psum["T0"][0:ML_HEADS, n * T + b * P:n * T + (b + 1) * P],
                                            gate_cols[:, b, n * ML_HEADS:(n + 1) * ML_HEADS], ident[:, :])
                last.then_inc(filled["T0"], 1)

            def gates_turn():
                base = first_use["gates", 1]
                pe.wait_ge(gate_rows, 1)
                pe.wait_ge(gate_exp, 1)
                claim("T1", base["T1"])
                for n, row in enumerate((g_u, g_em)):
                    for b in range(TB):
                        c = (n * TB + b) * ML_HEADS
                        last = pe.transpose(psum["T1"][:, c:c + ML_HEADS], row[:, b * P:(b + 1) * P],
                                            ident[0:ML_HEADS, 0:ML_HEADS])
                last.then_inc(filled["T1"], 1)

            def gates_spread(hd):
                bank = ("A0", "A1")[hd % 2]
                if hd == 0:
                    pe.wait_ge(ones_set, 1)
                claim(bank, first_use["gates", 1][bank] + hd // 2)
                mm(psum[bank][:, 0:T], selector[:, hd, :], g_m, True, True).then_inc(filled[bank], 1)

            def three(dst, rows, b, k, w, first, last_one):
                hi, lo = rows
                t = slice(b * P, (b + 1) * P)
                mm(dst, hi[:, k, t], w_hi[:, w[0], w[1]], first, False)
                mm(dst, hi[:, k, t], w_lo[:, w[0], w[1]], False, False)
                return mm(dst, lo[:, k, t], w_hi[:, w[0], w[1]], False, last_one)

            def project(layer, i, event):
                base = first_use["mix", layer]
                for j in range(12):
                    c = j // CSLOT
                    if j % CSLOT == 0:
                        for b in range(TB):
                            bank = group_bank(c, b)
                            claim(bank, i * (1 if c == 1 else 2) + (base[bank] + c // 2))
                    pe.wait_ge(lo_made, mix_slot(layer, i, j) + 1)
                    halves = layer == 1 and c == 0
                    n, width = (8, FF) if halves else (4, COLS)
                    col = (j // 2) * FF if halves else 0
                    for kk in range(n):
                        k = (j % 2) * 8 + kk if halves else (j % 4) * 4 + kk
                        for b in range(TB):
                            m = kk * TB + b
                            if m % (n // 4) == 0:
                                event(8 * j + m // (n // 4))
                            last = three(psum[group_bank(c, b)][:, col:col + width], (hT_hi, hT_lo), b, k,
                                         (j % 2, slice(kk * width, (kk + 1) * width)), k == 0, k == KT - 1)
                            if k == KT - 1 and j % CSLOT == 3:
                                last.then_inc(filled[group_bank(c, b)], 1)
                    if j % CSLOT != 3:
                        last.then_inc(split_read, 1)

            def wait_chunk(layer, i, c):
                base = first_use["mix", layer]
                for b in range(TB):
                    bank = group_bank(c, b)
                    pe.wait_ge(emptied[bank], i * (1 if c == 1 else 2) + (base[bank] + c // 2 + 1))

            def sb_step(g, step, k):
                base = first_use["mix", 0]
                t, a = f"T{k % 2}", f"A{k % 2}"
                if step == "turn":
                    if k == 0:
                        wait_chunk(0, g, 0)
                        wait_chunk(0, g, 1)
                    claim(t, g * 4 + base[t] + k // 2)
                    for n, raw in enumerate((q_raw, k_raw)):
                        for b in range(TB):
                            last = pe.transpose(psum[t][:, n * T + b * P:n * T + (b + 1) * P],
                                                raw[:, b, k * SB_DH:(k + 1) * SB_DH], ident[:, :])
                    last.then_inc(filled[t], 1)
                if step == "score":
                    pe.wait_ge(emptied[t], g * 4 + (base[t] + k // 2 + 1))
                    claim(a, g * 2 + base[a] + k // 2)
                    mm(psum[a][:, 0:T], kT[:, k, 0:P], qT[:, k, :], True, False)
                    mm(psum[a][:, T:TRI], kT[:, k, P:T], qT[:, k, P:T], False, True).then_inc(filled[a], 1)
                if step == "suffix":
                    pe.wait_ge(softplus_masked, g * SBG + k + 1)
                    s = sp[:, k % 2, :]
                    mm(psum[a][:, 0:T], neg_suffix[:, :], s[:, 0:T], False, False)
                    mm(psum[a][:, P:T], neg_ones[:, :], s[:, T:TRI], False, False)
                    mm(psum[a][:, T:TRI], neg_suffix[:, :], s[:, T:TRI], False, True).then_inc(suffix_summed, 1)
                if step == "out":
                    if k == 0:
                        wait_chunk(0, g, 2)
                    pe.wait_ge(prob_masked, g * SBG + k + 1)
                    claim(t, g * 4 + base[t] + 2 + k // 2)
                    v = v_raw[:, :, k * SB_DH:(k + 1) * SB_DH]
                    mm(psum[t][:, 0:T], v[:, 0, :], prob[:, k % 2, 0:T], True, False)
                    mm(psum[t][:, P:T], v[:, 1, :], prob[:, k % 2, T:TRI], False, True).then_inc(filled[t], 1)

            def ml_step(g, step, k):
                base = first_use["mix", 1]
                t, a = f"T{k}", f"A{k}"
                if step == "turn":
                    if k == 0:
                        wait_chunk(1, g, 0)
                    claim(t, g * 4 + base[t])
                    for n in range(2):
                        for b in range(TB):
                            c = n * (COLS // 2) + k * ML_DQ
                            last = pe.transpose(psum[t][:, n * T + b * P:n * T + (b + 1) * P],
                                                qk_raw[:, b, c:c + ML_DQ], ident[:, :])
                    last.then_inc(filled[t], 1)
                if step == "score":
                    pe.wait_ge(emptied[t], g * 4 + (base[t] + 1))
                    claim(a, g + base[a])
                    q, kk = qkT[:, k, 0, :], qkT[:, k, 1, :]
                    mm(psum[a][:, 0:T], kk[:, 0:P], q, True, False)
                    mm(psum[a][:, T:TRI], kk[:, P:T], q[:, P:T], False, True).then_inc(filled[a], 1)
                if step == "num":
                    if k == 0:
                        wait_chunk(1, g, 1)
                    pe.wait_ge(weights_ready, g * MLG + k + 1)
                    claim("T0", g * 4 + base["T0"] + 1 + k)
                    claim("T1", g * 4 + base["T1"] + 1 + k)
                    w = weights[:, k, :]
                    mm(psum["T0"][:, 0:ML_DV + 1], w[:, 0:P], v_one[:, 0, k, :], True, True).then_inc(filled["T0"], 1)
                    mm(psum["T1"][:, 0:ML_DV + 1], w[:, P:T], v_one[:, 0, k, :], True, False)
                    mm(psum["T1"][:, 0:ML_DV + 1], w[:, T:TRI], v_one[:, 1, k, :], False, True).then_inc(filled["T1"], 1)
                if step == "join":
                    pe.wait_ge(gated_ready, g * MLG + k + 1)
                    claim(t, g * 4 + base[t] + 3)
                    for n in range(2):
                        for b in range(TB):
                            last = pe.transpose(psum[t][:, n * T + b * P:n * T + (b + 1) * P],
                                                gated[:, k, b, n * P:(n + 1) * P], ident[:, :])
                    last.then_inc(filled[t], 1)

            def mix(layer):
                step = ml_step if layer else sb_step

                def first_group(m):
                    for at_, name, k in SCHEDULES[layer, "first"]:
                        if at_ == m:
                            if name == "logits":
                                gates_logits()
                            elif name == "rows":
                                gates_rows()
                            elif name == "columns":
                                gates_turn()
                            elif name == "spread":
                                gates_spread(k)

                def during(kind, g):
                    def event(m):
                        for at_, name, k in SCHEDULES[layer, kind]:
                            if at_ == m and name not in ("chunk", "split"):
                                step(g, name, k)
                    return event

                project(layer, 0, first_group)
                with pe.Fori(1, NGROUP) as i:
                    project(layer, i, during("group", i - 1))
                project_out(layer, during("out", NGROUP - 1))

            def project_out(layer, event):
                base = first_use["out", layer]
                for j, (c, n) in enumerate(OUT_ORDER):
                    banks = [f"{'GS'[c % 2]}{b}" for b in range(TB)]
                    if n == 0:
                        for b in banks:
                            claim(b, base[b] + c // 2)
                    if j in (0, 6):
                        for t in ("T0", "T1"):
                            pe.wait_ge(emptied[t], first_use["mix", layer][t] + 4 * NGROUP - (0 if j else 4))
                    pe.wait_ge(lo_made, mix_slot(layer, NGROUP, j) + 1)
                    for kk in range(4):
                        k = 4 * n + kk
                        for b in range(TB):
                            event(8 * j + kk * TB + b)
                            last = three(psum[banks[b]][:, :], (o_hi, o_lo), b, k,
                                         (j % 2, slice(kk * COLS, (kk + 1) * COLS)), k == 0, k == KT - 1)
                            if k == KT - 1:
                                last.then_inc(filled[banks[b]], 1)
                    if n != 3:
                        last.then_inc(split_read, 1)

            def route(layer):
                base = first_use["route", layer]
                pe.wait_ge(small_loaded[layer], 16 * (4 if layer else 7))
                for b in range(TB):
                    bank = f"S{b}"
                    claim(bank, base[bank])
                    for k in range(KT):
                        mm(psum[bank][:, 0:ROUTER], hT[:, k, b * P:(b + 1) * P], router_w[:, k, :], k == 0, False)
                    mm(psum[bank][:, 0:ROUTER], ones[0:1, :], router_b[0:1, :], False, True).then_inc(filled[bank], 1)
                pe.wait_ge(mask_ready, layer + 1)
                claim("G0", base["G0"])
                g = psum["G0"]
                mm(g[:, 0:EXPERTS], before[:, :], mask[:, 0, :], True, True)
                mm(g[:, EXPERTS:2 * EXPERTS], before[:, :], mask[:, 1, :], True, False)
                mm(g[:, EXPERTS:2 * EXPERTS], ones[:, :], mask[:, 0, :], False, True)
                mm(g[:, 2 * EXPERTS:3 * EXPERTS], ones[:, :], mask[:, 0, :], True, False)
                mm(g[:, 2 * EXPERTS:3 * EXPERTS], ones[:, :], mask[:, 1, :], False, True).then_inc(filled["G0"], 1)

            def gather(layer, i, c, n):
                bank = f"G{c % 2}"
                claim(bank, n)
                for k in range(4):
                    for b in range(TB):
                        rhs = disp[:, b, :, :].rearrange("p e s -> p (e s)")[:, bass.ds(i * P, P)]
                        last = mm(psum[bank][:, k * P:(k + 1) * P], hv[:, b, 4 * c + k, :], rhs, b == 0, b == 1)
                last.then_inc(filled[bank], 1)

            def up(bank, n0, q):
                for k in range(KT):
                    if k % 8 == 0:
                        yield k // 8
                    j = k % QUAD
                    last = mm(psum[bank][CAP * j:CAP * (j + 1), :], xe[:, k, CAP * q:CAP * (q + 1)],
                              w13_tile(n0, k), k < QUAD, k >= KT - QUAD)
                last.then_inc(filled[bank], 1)

            def fold_turn(bank, a):
                for c in range(4):
                    last = mm(psum[bank][:, c * CAP:(c + 1) * CAP], a[:, c * P:(c + 1) * P], fold[:, :], True, True)
                last.then_inc(filled[bank], 1)

            def quad(layer, i, more):
                base = first_use["moe", layer]
                per = 6 * QUAD

                def turned(q):
                    t, a = f"T{q % 2}", f"A{q % 2}"
                    pe.wait_ge(emptied[a], i * 2 + (base[a] + q // 2 + 1))
                    claim(t, i * 2 + base[t] + q // 2)
                    fold_turn(t, acc[:, q % 2, :])

                pe.wait_ge(disp_gated, i + (layer * NQUAD + 1))
                for b in range(TB):
                    claim(f"G{b}", i * 5 + base[f"G{b}"])
                    pe.transpose(psum[f"G{b}"][:, 0:P], disp_g[:, b, :], ident[:, :]).then_inc(filled[f"G{b}"], 1)
                for b in range(2):
                    pe.wait_ge(emptied[f"G{b}"], i * 5 + base[f"G{b}"])
                for q in range(QUAD):
                    a = f"A{q % 2}"
                    claim(a, i * 2 + base[a] + q // 2)
                    for half in up(a, 4 * q, q):
                        for j in (4 * q + 2 * half, 4 * q + 2 * half + 1):
                            pe.wait_ge(slot_loaded[slot_at(j)], slot_value(layer, i, per, j))
                    if q:
                        turned(q - 1)
                if more:
                    for c in range(2):
                        gather(layer, i + 1, c, i * 5 + base[f"G{c}"] + 1)
                turned(QUAD - 1)
                if more:
                    for c in range(2, 4):
                        gather(layer, i + 1, c, i * 5 + base[f"G{c % 2}"] + 2)
                pe.wait_ge(hid_ready, i * QUAD + (layer * EXPERTS + QUAD))
                for j in range(4 * QUAD, 6 * QUAD):
                    pe.wait_ge(slot_loaded[slot_at(j)], slot_value(layer, i, per, j))
                for dc in range(4):
                    g = f"G{dc % 2}"
                    claim(g, i * 5 + base[g] + (3 if more else 1) + dc // 2)
                    for ft in range(2):
                        for q in range(QUAD):
                            w2 = ring[:, slot_at(4 * QUAD + 2 * q + ft), dc * COLS:(dc + 1) * COLS]
                            last = mm(psum[g][CAP * q:CAP * (q + 1), :], hid[:, q, ft * CAP:(ft + 1) * CAP], w2,
                                      ft == 0, ft == 1)
                    last.then_inc(filled[g], 1)
                for dc in range(4):
                    g = f"G{dc % 2}"
                    pe.wait_ge(emptied[g], i * 5 + (base[g] + (3 if more else 1) + dc // 2 + 1))
                    for b in range(TB):
                        s = f"S{b}"
                        claim(s, i * 4 + base[s] + dc)
                        mm(psum[s][:, :], spread[:, b, :], y[:, dc * COLS:(dc + 1) * COLS], True, True).then_inc(filled[s], 1)

            def experts(layer):
                pe.wait_ge(disp_ready, layer + 1)
                base = first_use["gather", layer]
                for c in range(4):
                    gather(layer, 0, c, base[f"G{c % 2}"] + c // 2)
                with pe.Fori(0, NQUAD - 1) as i:
                    quad(layer, i, True)
                quad(layer, NQUAD - 1, False)

            def overflow(layer):
                o = over[layer]
                over_x = xe[:, 0:QUAD, :].rearrange("p k n -> p (k n)").rearrange("p (k s) -> p k s", s=CAP)

                def expert(k, e):
                    pe.wait_ge(o["slots"], k + 1)
                    for kt in range(KT):
                        for b in range(TB):
                            last = mm(psum["G0"][:, kt * CAP:(kt + 1) * CAP], hv[:, b, kt, :], over_d[:, b, :], b == 0, b == 1)
                    last.then_inc(o["rows_filled"], 1)
                    for b in range(TB):
                        last = pe.transpose(psum["G1"][0:CAP, b * P:(b + 1) * P], over_g[:, b, :], ident[:, :])
                    last.then_inc(o["spread_filled"], 1)
                    pe.wait_ge(o["rows"], k + 1)
                    for kt in range(KT):
                        if kt % 8 == 0:
                            pe.wait_ge(o["w_loaded"], k * 96 + 32 * (kt // 8 + 1))
                        j = kt % QUAD
                        last = mm(psum["A0"][CAP * j:CAP * (j + 1), :], over_x[:, kt, :],
                                  over_w[:, :, (kt % 8) * FF:(kt % 8 + 1) * FF], kt < QUAD, kt >= KT - QUAD)
                        if kt % 8 == 7:
                            last.then_inc(o["w_used"], 1)
                    pe.wait_ge(o["acc"], k + 1)
                    for c in range(4):
                        last = mm(psum["T0"][:, c * CAP:(c + 1) * CAP], acc[:, 0, c * P:(c + 1) * P], fold[:, :], True, True)
                    last.then_inc(o["turned"], 1)
                    pe.wait_ge(o["hid"], k + 1)
                    pe.wait_ge(o["w_loaded"], k * 96 + 96)
                    for dc in range(4):
                        for ft in range(2):
                            last = mm(psum[("A1", "T1", "S0", "S1")[dc]][0:CAP, :], hid[:, 0, ft * CAP:(ft + 1) * CAP],
                                      over_w[:, ft, dc * COLS:(dc + 1) * COLS], ft == 0, ft == 1)
                    last.then_inc(o["w_used"], 1)
                    pe.wait_ge(o["y"], k + 1)
                    pe.wait_ge(o["spread"], k + 1)
                    for dc in range(4):
                        for b in range(TB):
                            last = mm(psum[BANKS[2 * dc + b]][:, :], spread[0:CAP, b, :], y[0:CAP, dc * COLS:(dc + 1) * COLS],
                                      True, True)
                    last.then_inc(o["scattered"], 1)

                overflow_passes(pe, layer, expert)

            pe.wait_ge(consts_made, 1)
            for layer in (0, 1):
                turn_rows("norm_mix", layer)
                wait_turned("norm_mix", layer)
                mix(layer)
                turn_rows("norm_ffn", layer)
                wait_turned("norm_ffn", layer)
                route(layer)
                experts(layer)
                overflow(layer)

        @block.scalar
        def _(act):
            act.preload_act_table_set("natural_log_exp_and_others")

            def norm(n, phase, layer):
                for b in range(TB):
                    if n == 0:
                        act.wait_ge(x_loaded[b], 16)
                    act.activation(h[:, b, :], x[:, b, :], ACT.Square, accum_out=sumsq[:, b:b + 1])
                act.drain().then_inc(squares_done, 1)
                act.activation(rstd[:, :], sumsq[:, :], ACT.Ln, scale=1.0 / D, bias=eps_col[:, 0:1])
                act.drain()
                act.activation(rstd[:, :], rstd[:, :], ACT.Exp, scale=-0.5).then_inc(rstd_seed, 1)
                for u in range(2 * KT // 4 if phase else 0):
                    bank, b, k0 = norm_bank(u)
                    value = first_use[phase, layer][bank] + u // 4 + 1
                    src = psum[bank][:, :].rearrange("p (k t) -> p k t", k=4)
                    if phase == "norm_mix":
                        act.wait_ge(filled[bank], value)
                        act.copy(tiles(hT_hi, b, k0), src).then_inc(row_hi_made, 1)
                    elif bank[0] == "T":
                        act.wait_ge(filled[bank], value)
                        act.copy(tiles(hT, b, k0), src).then_inc(emptied[bank], 1)

            def sb_group(kind, g, i):
                base = first_use["mix", 0]
                for _, step, k in SCHEDULES[0, kind]:
                    t, a = f"T{k % 2}", f"A{k % 2}"
                    if step == "split":
                        split_hi(act, 0, i, k)
                    if step == "chunk" and kind != "out":
                        copy_chunk(act, act.copy, 0, i, k, 0)
                    if step == "turn":
                        act.wait_ge(filled[t], g * 4 + (base[t] + k // 2 + 1))
                        act.mul(qT[:, k, :], psum[t][:, 0:T], SB_DH ** -0.5)
                        act.copy(kT[:, k, :], psum[t][:, T:2 * T]).then_inc(emptied[t], 1)
                    if step == "score":
                        act.wait_ge(clipped, g * SBG + k + 1)
                        s = soft[:, k % 2, :]
                        act.activation(s, s, ACT.Exp)
                        act.drain()
                        act.activation(s, s, ACT.Ln, bias=1.0).then_inc(softplus_log, 1)
                    if step == "suffix":
                        act.wait_ge(suffix_summed, g * SBG + k + 1)
                        act.activation(prob[:, k % 2, :], psum[a][:, 0:TRI], ACT.Exp).then_inc(emptied[a], 1)
                        act.drain().then_inc(prob_exp, 1)
                    if step == "out":
                        act.wait_ge(filled[t], g * 4 + (base[t] + 2 + k // 2 + 1))
                        act.copy(o_hi[:, bass.ds(g * SBG + k, 1), :], psum[t][:, 0:T].unsqueeze(1)).then_inc(out_hi_made, 1)

            def ml_group(kind, g, i):
                base = first_use["mix", 1]
                for _, step, k in SCHEDULES[1, kind]:
                    t = f"T{k % 2}"
                    if step == "split":
                        split_hi(act, 1, i, k)
                    if step == "chunk" and kind != "out":
                        copy_chunk(act, act.copy, 1, i, k, 0)
                        if k == 2:
                            copy_chunk(act, act.copy, 1, i, k, 1)
                    if step == "rows":
                        gates_early()
                    if step == "spread":
                        gates_decay(k)
                    if step == "turn":
                        act.wait_ge(filled[t], g * 4 + (base[t] + 1))
                        act.mul(qkT[:, k, 0, :], psum[t][:, 0:T], ML_DQ ** -0.5)
                        act.copy(qkT[:, k, 1, :], psum[t][:, T:2 * T]).then_inc(emptied[t], 1)
                    if step == "num":
                        act.wait_ge(head_squares, g * MLG + k + 1)
                        act.activation(hrs, ms, ACT.Ln)
                        act.drain()
                        act.activation(hrs, hrs, ACT.Exp, scale=-0.5).then_inc(head_seed, 1)
                    if step == "join":
                        act.wait_ge(filled[t], g * 4 + (base[t] + 4))
                        dst = o_hi[:, bass.ds((g * MLG + k) * 2, 2), :]
                        act.copy(dst, psum[t][:, :].rearrange("p (k t) -> p k t", k=2)).then_inc(out_hi_made, 1)

            def gates_early():
                act.wait_ge(gate_clip, 1)
                act.activation(g_clip, g_clip, ACT.Exp)
                act.drain()
                act.activation(g_clip, g_clip, ACT.Ln, bias=1.0).then_inc(gate_log, 1)
                act.wait_ge(gate_rows, 1)
                act.activation(g_em, g_em, ACT.Exp)
                act.drain().then_inc(gate_exp, 1)

            def gates_decay(hd):
                if hd == 0:
                    act.wait_ge(emptied["T1"], first_use["gates", 1]["T1"] + 1)
                a = f"A{hd % 2}"
                act.wait_ge(filled[a], first_use["gates", 1][a] + hd // 2 + 1)
                act.activation(decay[:, hd, 0:T], psum[a][:, 0:T], ACT.Exp, bias=u_col[:, 0, hd:hd + 1])
                act.activation(decay[:, hd, T:TRI], psum[a][:, P:T], ACT.Exp, bias=u_col[:, 1, hd:hd + 1]
                               ).then_inc(emptied[a], 1)
                act.drain().then_inc(decay_exp, 1)

            def experts(layer):
                base = first_use["gather", layer]

                def take(c, n):
                    g = f"G{c % 2}"
                    act.wait_ge(filled[g], n + 1)
                    act.copy(xe[:, 4 * c:4 * c + 4, :].rearrange("p k n -> p (k n)"), psum[g][:, :]).then_inc(emptied[g], 1)

                act.wait_ge(group_shift, layer + 1)
                act.activation(gexp, gexp, ACT.Exp).then_inc(group_exp, 1)
                act.wait_ge(top2_gap, layer + 1)
                act.activation(dm, dm, ACT.Exp).then_inc(top2_exp, 1)
                for c in range(4):
                    take(c, base[f"G{c % 2}"] + c // 2)

                def quad(i, more):
                    base = first_use["moe", layer]

                    def silu(q):
                        t = f"T{q % 2}"
                        act.wait_ge(filled[t], i * 2 + (base[t] + q // 2 + 1))
                        act.wait_ge(exp_taken, i * QUAD + (layer * EXPERTS + q + 1))
                        act.activation(ex, psum[t][:, 0:2 * CAP], ACT.Exp, scale=-1.0).then_inc(silu_exp, 1)

                    for b in range(TB):
                        g = f"G{b}"
                        act.wait_ge(filled[g], i * 5 + (base[g] + 1))
                        act.copy(spread[:, b, :], psum[g][:, 0:P]).then_inc(emptied[g], 1)
                    for q in range(QUAD - 1):
                        silu(q)
                    if more:
                        for c in range(2):
                            take(c, i * 5 + (base[f"G{c}"] + 1))
                    silu(QUAD - 1)
                    if more:
                        for c in range(2, 4):
                            take(c, i * 5 + (base[f"G{c % 2}"] + 2))
                    for dc in range(4):
                        g = f"G{dc % 2}"
                        act.wait_ge(filled[g], i * 5 + (base[g] + (3 if more else 1) + dc // 2 + 1))
                        act.copy(y[:, dc * COLS:(dc + 1) * COLS], psum[g][:, :]).then_inc(emptied[g], 1)

                with act.Fori(0, NQUAD - 1) as i:
                    quad(i, True)
                quad(NQUAD - 1, False)

            def overflow(layer):
                o = over[layer]

                def expert(k, e):
                    act.wait_ge(o["rows_filled"], k + 1)
                    act.copy(xe[:, 0:QUAD, :].rearrange("p k n -> p (k n)"), psum["G0"][:, :]).then_inc(o["rows"], 1)
                    act.wait_ge(o["spread_filled"], k + 1)
                    act.copy(spread[0:CAP, :, :].rearrange("p b t -> p (b t)"), psum["G1"][0:CAP, 0:T]).then_inc(o["spread"], 1)
                    act.wait_ge(o["turned"], k + 1)
                    act.activation(ex, psum["T0"][:, 0:2 * CAP], ACT.Exp, scale=-1.0).then_inc(o["exp"], 1)
                    act.wait_ge(o["w_used"], k * 3 + 4)
                    for dc in range(4):
                        act.copy(y[0:CAP, dc * COLS:(dc + 1) * COLS], psum[("A1", "T1", "S0", "S1")[dc]][0:CAP, :])
                    act.drain().then_inc(o["y"], 1)

                overflow_passes(act, layer, expert)

            for b in range(TB):
                act.dma_start(x[:, b, :], x_in[0, b * P:(b + 1) * P, :]).then_inc(x_loaded[b], 16)
            act.wait_ge(consts_made, 1)
            for layer in (0, 1):
                group = ml_group if layer else sb_group
                norm(2 * layer, "norm_mix", layer)
                split_hi(act, layer, 0, 0)
                group("first", None, 0)
                with act.Fori(1, NGROUP) as i:
                    group("group", i - 1, i)
                group("out", NGROUP - 1, NGROUP)
                for b in ("G0", "G1", "S0", "S1"):
                    act.wait_ge(emptied[b], first_use["out", layer][b] + 2)
                norm(2 * layer + 1, "norm_ffn", layer)
                experts(layer)
                overflow(layer)
                act.wait_ge(moe_done, layer + 1)
            norm(4, None, 0)

        @block.vector
        def _(dve):
            def norm(n, phase, layer):
                dve.wait_ge(squares_done, n + 1)
                dve.tensor_scalar(mean_eps[:, :], sumsq[:, :], 1.0 / D, EPS, ALU.mult, ALU.add)
                dve.drain()
                dve.wait_ge(rstd_seed, n + 1)
                refine(rstd[:, :], mean_eps[:, :], newton[:, :])
                dve.wait_ge(grow_loaded, 16 * ({0: 0, 1: 1, 2: 2, 3: 4, 4: 5}[n] + 1))
                for b in range(TB):
                    dve.scalar_tensor_tensor(out=h[:, b, :], in0=x[:, b, :], scalar=rstd[:, b:b + 1],
                                             in1=grow[:, :], op0=ALU.mult, op1=ALU.mult
                                             ).then_inc(h_ready if phase else out_ready, 1)
                if phase:
                    dve.drain().then_inc(grow_used, 1)
                for u in range(2 * KT // 4 if phase else 0):
                    bank, b, k0 = norm_bank(u)
                    src = psum[bank][:, :].rearrange("p (k t) -> p k t", k=4)
                    if phase == "norm_mix":
                        dve.wait_ge(row_hi_made, layer * (2 * KT // 4) + u + 1)
                        dve.tensor_tensor(tiles(hT_lo, b, k0), src, tiles(hT_hi, b, k0).bitcast(F32), ALU.subtract
                                          ).then_inc(emptied[bank], 1)
                    elif bank[0] == "A":
                        dve.wait_ge(filled[bank], first_use[phase, layer][bank] + u // 4 + 1)
                        dve.tensor_copy(tiles(hT, b, k0), src).then_inc(emptied[bank], 1)

            def refine(r_, v_, t_):
                dve.tensor_tensor(t_, r_, r_, ALU.mult)
                dve.drain()
                dve.tensor_tensor(t_, t_, v_, ALU.mult)
                dve.drain()
                dve.tensor_scalar(t_, t_, -0.5, 1.5, ALU.mult, ALU.add)
                dve.drain()
                dve.tensor_tensor(r_, r_, t_, ALU.mult)
                dve.drain()

            def sb_group(kind, g, i):
                base = first_use["mix", 0]
                for _, step, k in SCHEDULES[0, kind]:
                    t, a = f"T{k % 2}", f"A{k % 2}"
                    if step == "split":
                        split_lo(dve, 0, i, k)
                    if step == "chunk":
                        if kind == "out":
                            add_chunk(0, k)
                        else:
                            copy_chunk(dve, dve.tensor_copy, 0, i, k, 1)
                    if step == "score":
                        dve.wait_ge(filled[a], g * 2 + (base[a] + k // 2 + 1))
                        dve.tensor_scalar(soft[:, k % 2, :], psum[a][:, 0:TRI], CLAMP, None, ALU.min).then_inc(clipped, 1)
                        dve.wait_ge(softplus_log, g * SBG + k + 1)
                        dve.tensor_tensor(sp[:, k % 2, :], soft[:, k % 2, :], psum[a][:, 0:TRI], ALU.max)
                        dve.drain().then_inc(softplus_full, 1)
                    if step == "out":
                        dve.wait_ge(out_hi_made, g * SBG + k + 1)
                        at_ = bass.ds(g * SBG + k, 1)
                        dve.tensor_tensor(o_lo[:, at_, :], psum[t][:, 0:T].unsqueeze(1), o_hi[:, at_, :].bitcast(F32),
                                          ALU.subtract).then_inc(emptied[t], 1)

            def ml_group(kind, g, i):
                base = first_use["mix", 1]
                for _, step, k in SCHEDULES[1, kind]:
                    t, a = f"T{k % 2}", f"A{k % 2}"
                    if step == "split":
                        split_lo(dve, 1, i, k)
                    if step == "chunk":
                        if kind == "out":
                            add_chunk(1, k)
                        elif k < 2:
                            copy_chunk(dve, dve.tensor_copy, 1, i, k, 1)
                    if step == "logits":
                        gates_take()
                    if step == "rows":
                        gates_early()
                    if step == "columns":
                        gates_cols()
                    if g is None:
                        continue
                    hd = g * MLG + k
                    if step == "turn":
                        if k == 0:
                            for b in range(TB):
                                dve.wait_ge(emptied[f"G{b}"], g * 2 + (base[f"G{b}"] + 2))
                        sig = o_exp[:, :, k * ML_DV:(k + 1) * ML_DV]
                        dve.tensor_scalar(sig, sig, 1.0, None, ALU.add)
                        dve.drain()
                        dve.reciprocal(sig, sig)
                        dve.drain()
                    if step == "score":
                        dve.wait_ge(filled[a], g + (base[a] + 1))
                        dve.wait_ge(decay_masked, ML_HEADS)
                        dve.tensor_tensor(weights[:, k, :].unsqueeze(1), psum[a][:, 0:TRI].unsqueeze(1),
                                          decay[:, bass.ds(hd, 1), :], ALU.mult).then_inc(emptied[a], 1)
                        dve.drain().then_inc(weights_ready, 1)
                    if step == "num":
                        for b in range(TB):
                            n = psum[f"T{b}"]
                            dve.wait_ge(filled[f"T{b}"], g * 4 + (base[f"T{b}"] + 1 + k + 1))
                            dve.tensor_scalar(ssq[:, b:b + 1], n[:, ML_DV:ML_DV + 1], -1.0, None, ALU.mult)
                        dve.drain()
                        for b in range(TB):
                            dve.tensor_tensor(den[:, b:b + 1], psum[f"T{b}"][:, ML_DV:ML_DV + 1], ssq[:, b:b + 1], ALU.max)
                        dve.drain()
                        dve.tensor_tensor(den.unsqueeze(2), den.unsqueeze(2), m_col[:, :, bass.ds(hd, 1)], ALU.max)
                        dve.drain()
                        dve.reciprocal(den, den)
                        dve.drain()
                        for b in range(TB):
                            n = psum[f"T{b}"]
                            dve.tensor_scalar(hs[:, b, :], n[:, 0:ML_DV], den[:, b:b + 1], None, ALU.mult
                                              ).then_inc(emptied[f"T{b}"], 1)
                        dve.drain()
                        for b in range(TB):
                            dve.tensor_tensor_reduce(gated[:, k, b, :], hs[:, b, :], hs[:, b, :], 1.0, 0.0,
                                                     ALU.mult, ALU.add, ssq[:, b:b + 1])
                            dve.drain()
                        dve.tensor_scalar(ms, ssq, 1.0 / ML_DV, EPS, ALU.mult, ALU.add)
                        dve.drain().then_inc(head_squares, 1)
                    if step == "gate":
                        dve.wait_ge(head_seed, g * MLG + k + 1)
                        refine(hrs, ms, hnw)
                        if k == 0:
                            dve.wait_ge(grow_loaded, 16 * 4)
                        for b in range(TB):
                            dve.scalar_tensor_tensor(out=hs[:, b, :], in0=hs[:, b, :], scalar=hrs[:, b:b + 1],
                                                     in1=grow[:, bass.ds(hd * ML_DV, ML_DV)],
                                                     op0=ALU.mult, op1=ALU.mult)
                        dve.drain()
                        dve.tensor_tensor(gated[:, k, :, :], hs, o_exp[:, :, k * ML_DV:(k + 1) * ML_DV], ALU.mult)
                        dve.drain().then_inc(gated_ready, 1)
                    if step == "join":
                        dve.wait_ge(out_hi_made, SB_HEADS + g * MLG + k + 1)
                        at_ = bass.ds((g * MLG + k) * 2, 2)
                        dve.tensor_tensor(o_lo[:, at_, :], psum[t][:, :].rearrange("p (k t) -> p k t", k=2),
                                          o_hi[:, at_, :].bitcast(F32), ALU.subtract).then_inc(emptied[t], 1)

            def gates_take():
                dve.wait_ge(filled["T0"], first_use["gates", 1]["T0"] + 1)
                dve.tensor_copy(gate_cols.rearrange("p b n -> p (b n)"), psum["T0"][:, 0:TB * 2 * ML_HEADS]
                                ).then_inc(emptied["T0"], 1)
                dve.drain().then_inc(gate_taken, 1)

            def gates_early():
                pg = psum["T0"]
                dve.wait_ge(filled["T0"], first_use["gates", 1]["T0"] + 2)
                dve.tensor_scalar(g_y, pg[0:ML_HEADS, T:2 * T], gate_b[:, 1:2], -1.0, ALU.add, ALU.mult)
                dve.drain()
                dve.tensor_scalar(g_clip, g_y, CLAMP, None, ALU.min).then_inc(gate_clip, 1)
                dve.wait_ge(gate_log, 1)
                dve.tensor_tensor(g_sp, g_clip, g_y, ALU.max)
                dve.drain()
                dve.memset(g_y, 1.0)
                dve.drain()
                dve.tensor_tensor_scan(g_negb, g_y, g_sp, 0.0, ALU.mult, ALU.add)
                dve.drain()
                dve.scalar_tensor_tensor(out=g_u, in0=pg[0:ML_HEADS, 0:T], scalar=gate_b[:, 0:1], in1=g_negb,
                                         op0=ALU.add, op1=ALU.add).then_inc(emptied["T0"], 1)
                dve.drain()
                dve.tensor_tensor_scan(g_m, g_u, g_u, 0.0, ALU.max, ALU.max)
                dve.drain()
                dve.tensor_tensor(g_em, g_negb, g_m, ALU.subtract)
                dve.drain()
                dve.tensor_scalar(g_m, g_m, -1.0, None, ALU.mult)
                dve.drain().then_inc(gate_rows, 1)

            def gates_cols():
                dve.wait_ge(filled["T1"], first_use["gates", 1]["T1"] + 1)
                pg = psum["T1"]
                w = TB * ML_HEADS
                dve.tensor_copy(u_col.rearrange("p b h -> p (b h)"), pg[:, 0:w])
                dve.tensor_copy(m_col.rearrange("p b h -> p (b h)"), pg[:, w:2 * w]).then_inc(emptied["T1"], 1)

            def add_chunk(layer, c):
                for b in range(TB):
                    dve.wait_ge(*out_filled(layer, c, b))
                    bank = f"{'GS'[c % 2]}{b}"
                    xs = x[:, b, c * COLS:(c + 1) * COLS]
                    dve.tensor_tensor(xs, xs, psum[bank][:, :], ALU.add).then_inc(emptied[bank], 1)

            def wide(view, shape):
                return view.to_broadcast(shape)

            def route(layer):
                base = first_use["route", layer]
                for b in range(TB):
                    dve.wait_ge(filled[f"S{b}"], base[f"S{b}"] + 1)
                    dve.tensor_copy(logits[:, b, :], psum[f"S{b}"][:, 0:ROUTER]).then_inc(emptied[f"S{b}"], 1)
                dve.tensor_scalar(rank, iota[:, 0:PER_GROUP], -1.0, float(PER_GROUP), ALU.mult, ALU.add)
                dve.drain()
                gl = logits[:, :, 0:GROUPS]
                g4 = [P, TB, GROUPS]
                e8 = [P, TB, PER_GROUP]

                def first_max(vals, top, cmp_, sel, shape, n):
                    dve.tensor_reduce(top, vals, AX, ALU.max)
                    dve.drain()
                    dve.tensor_tensor(cmp_, vals, wide(top, shape), ALU.is_equal)
                    dve.drain()
                    dve.tensor_tensor(cmp_, cmp_, wide(rank[:, 0:n].unsqueeze(1), shape), ALU.mult)
                    dve.drain()
                    dve.tensor_reduce(tie, cmp_, AX, ALU.max)
                    dve.drain()
                    dve.tensor_tensor(sel, cmp_, wide(tie, shape), ALU.is_equal)
                    dve.drain()

                first_max(gl, gmax, gcmp, gsel, g4, GROUPS)
                dve.tensor_tensor(gexp, gl, wide(gmax, g4), ALU.subtract).then_inc(group_shift, 1)
                el = logits[:, :, GROUPS:ROUTER].rearrange("p b (g e) -> p b g e", g=GROUPS)
                for b in range(TB):
                    dve.tensor_tensor(picked[:, b], el[:, b],
                                      wide(gsel[:, b, :].unsqueeze(2), [P, GROUPS, PER_GROUP]), ALU.mult)
                dve.drain()
                for b in range(TB):
                    dve.tensor_reduce(es[:, b, :].unsqueeze(2), picked[:, b].rearrange("p g e -> p e g"), AX, ALU.add)
                dve.drain()
                first_max(es, m1, cmp8, s1, e8, PER_GROUP)
                dve.scalar_tensor_tensor(out=tmp8, in0=s1, scalar=-3e38, in1=es, op0=ALU.mult, op1=ALU.add)
                dve.drain()
                first_max(tmp8, m2, cmp8, s2, e8, PER_GROUP)
                dve.tensor_tensor(dm, m2, m1, ALU.subtract).then_inc(top2_gap, 1)
                dve.tensor_tensor(tmp8, s1, s2, ALU.add)
                dve.drain()
                m4 = mask.rearrange("p b (g e) -> p b g e", g=GROUPS)
                ge = [P, GROUPS, PER_GROUP]
                for b in range(TB):
                    dve.tensor_tensor(m4[:, b], wide(gsel[:, b, :].unsqueeze(2), ge), wide(tmp8[:, b, :].unsqueeze(1), ge), ALU.mult)
                dve.drain().then_inc(mask_ready, 1)
                dve.wait_ge(group_exp, layer + 1)
                dve.tensor_reduce(gsum, gexp, AX, ALU.add)
                dve.drain()
                dve.reciprocal(psel, gsum)
                dve.wait_ge(top2_exp, layer + 1)
                dve.tensor_scalar(w1c, dm, 1.0, None, ALU.add)
                dve.drain()
                dve.reciprocal(w1c, w1c)
                dve.drain()
                dve.tensor_tensor(w1c, w1c, psel, ALU.mult)
                dve.drain()
                dve.tensor_tensor(w2c, w1c, dm, ALU.mult)
                dve.tensor_tensor(gate8, s1, wide(w1c, e8), ALU.mult)
                dve.drain()
                dve.tensor_tensor(tmp8, s2, wide(w2c, e8), ALU.mult)
                dve.drain()
                dve.tensor_tensor(gate8, gate8, tmp8, ALU.add)
                dve.drain()
                w4 = gates.rearrange("p b (g e) -> p b g e", g=GROUPS)
                for b in range(TB):
                    dve.tensor_tensor(w4[:, b], wide(gsel[:, b, :].unsqueeze(2), ge), wide(gate8[:, b, :].unsqueeze(1), ge), ALU.mult)
                dve.wait_ge(filled["G0"], base["G0"] + 1)
                pg = psum["G0"]
                dve.scalar_tensor_tensor(out=posm.rearrange("p b e -> p (b e)"), in0=pg[:, 0:TB * EXPERTS], scalar=1.0,
                                         in1=mask.rearrange("p b e -> p (b e)"), op0=ALU.add, op1=ALU.mult)
                dve.tensor_reduce(count_max[:, :], pg[0:1, 2 * EXPERTS:3 * EXPERTS], AX, ALU.max).then_inc(emptied["G0"], 1)
                dve.drain()
                dve.tensor_scalar(posm, posm, -1.0, None, ALU.add)
                dve.tensor_scalar(count_lt[:, :], thresholds[:, :], count_max[:, 0:1], None, ALU.is_lt)
                dve.drain()
                dve.tensor_reduce(extra_f[:, :], count_lt[:, :], AX, ALU.add)
                dve.drain()
                dve.tensor_copy(extra_i[:, :], extra_f[:, :])
                dve.drain().then_inc(extra_ready, 1)
                full = [P, EXPERTS, CAP]
                for b in range(TB):
                    dve.tensor_tensor(disp[:, b], wide(iota[:, :].unsqueeze(1), full),
                                      wide(posm[:, b, :].unsqueeze(2), full), ALU.is_equal)
                dve.drain().then_inc(disp_ready, 1)

            def experts(layer):
                base = first_use["moe", layer]

                def quad(i):
                    for b in range(TB):
                        dve.tensor_tensor(disp_g[:, b, :].rearrange("p (e s) -> p e s", e=QUAD),
                                          disp[:, b, bass.ds(i * QUAD, QUAD), :],
                                          wide(gates[:, b, bass.ds(i * QUAD, QUAD)].unsqueeze(2), [P, QUAD, CAP]), ALU.mult)
                    dve.drain().then_inc(disp_gated, 1)

                    def take(q):
                        a = f"A{q % 2}"
                        dve.wait_ge(filled[a], i * 2 + (base[a] + q // 2 + 1))
                        dve.tensor_copy(acc[:, q % 2, :], psum[a][:, :]).then_inc(emptied[a], 1)

                    def silu(q):
                        t = f"T{q % 2}"
                        dve.wait_ge(silu_exp, i * QUAD + (layer * EXPERTS + q + 1))
                        dve.tensor_scalar(sg, ex, 1.0, None, ALU.add).then_inc(exp_taken, 1)
                        dve.drain()
                        dve.reciprocal(sg, sg)
                        dve.drain()
                        dve.tensor_tensor(t13, sg, psum[t][:, 0:2 * CAP], ALU.mult)
                        dve.drain()
                        dve.tensor_tensor(hid[:, q, :], t13, psum[t][:, 2 * CAP:4 * CAP], ALU.mult).then_inc(emptied[t], 1)
                        dve.drain().then_inc(hid_ready, 1)

                    take(0)
                    for q in range(1, QUAD):
                        take(q)
                        silu(q - 1)
                    silu(QUAD - 1)
                    for dc in range(4):
                        for b in range(TB):
                            s = f"S{b}"
                            dve.wait_ge(filled[s], i * 4 + (base[s] + dc + 1))
                            xs = x[:, b, dc * COLS:(dc + 1) * COLS]
                            dve.tensor_tensor(xs, xs, psum[s][:, :], ALU.add).then_inc(emptied[s], 1)
                    dve.drain()

                with dve.Fori(0, NQUAD) as i:
                    quad(i)
                dve.drain()

            def overflow(layer):
                o = over[layer]
                dve.sem_inc(o["w_used"], 1)

                def expert(k, e):
                    for b in range(TB):
                        at = posm[:, b, bass.ds(e, 1)]
                        dve.tensor_scalar(at, at, -float(CAP), None, ALU.add)
                    dve.drain()
                    for b in range(TB):
                        dve.tensor_scalar(over_d[:, b, :], iota[:, :], posm[:, b, bass.ds(e, 1)], None, ALU.is_equal)
                    dve.drain()
                    for b in range(TB):
                        dve.tensor_scalar(over_g[:, b, :], over_d[:, b, :], gates[:, b, bass.ds(e, 1)], None, ALU.mult)
                    dve.drain().then_inc(o["slots"], 1)
                    dve.wait_ge(o["w_used"], k * 3 + 3)
                    dve.tensor_copy(acc[:, 0, :], psum["A0"][:, :]).then_inc(o["acc"], 1)
                    dve.wait_ge(o["exp"], k + 1)
                    dve.tensor_scalar(sg, ex, 1.0, None, ALU.add)
                    dve.drain()
                    dve.reciprocal(sg, sg)
                    dve.drain()
                    dve.tensor_tensor(t13, sg, psum["T0"][:, 0:2 * CAP], ALU.mult)
                    dve.drain()
                    dve.tensor_tensor(hid[:, 0, :], t13, psum["T0"][:, 2 * CAP:4 * CAP], ALU.mult)
                    dve.drain().then_inc(o["hid"], 1)
                    dve.wait_ge(o["scattered"], k + 1)
                    for dc in range(4):
                        for b in range(TB):
                            xs = x[:, b, dc * COLS:(dc + 1) * COLS]
                            dve.tensor_tensor(xs, xs, psum[BANKS[2 * dc + b]][:, :], ALU.add)
                    dve.drain()

                overflow_passes(dve, layer, expert)

            dve.wait_ge(consts_made, 1)
            dve.tensor_scalar(thresholds[:, :], iota[0:1, 0:T // CAP - 1], float(CAP), float(CAP), ALU.mult, ALU.add)
            dve.drain().then_inc(exp_taken, 1)
            for b in range(TB):
                dve.wait_ge(x_loaded[b], 16)
            for layer in (0, 1):
                group = ml_group if layer else sb_group
                norm(2 * layer, "norm_mix", layer)
                split_lo(dve, layer, 0, 0)
                group("first", None, 0)
                with dve.Fori(1, NGROUP) as i:
                    group("group", i - 1, i)
                group("out", NGROUP - 1, NGROUP)
                if layer:
                    dve.drain().then_inc(grow_used, 1)
                dve.drain()
                norm(2 * layer + 1, "norm_ffn", layer)
                route(layer)
                experts(layer)
                overflow(layer)
                dve.drain().then_inc(moe_done, 1)
            norm(4, None, 0)



_INS = ["x", "norm_mix", "norm_ffn", "norm_final", "sb_w_in", "sb_w_out", "ml_w_in", "ml_b_i", "ml_b_f",
        "ml_g_head", "ml_w_out", "moe_w_group", "moe_b_group", "moe_w_expert", "moe_b_expert",
        "moe_w1", "moe_w3", "moe_w2"]


def kernel(**inputs):
    import concourse.bacc as bacc
    from concourse.bass_utils import run_bass_kernel_spmd

    nc = bacc.Bacc("TRN2", target_bir_lowering=False, num_devices=1)
    arrays, args = {}, []
    for name in _INS:
        a = np.ascontiguousarray(inputs[name])
        arrays[f"in_{name}"] = a
        args.append(nc.dram_tensor(f"in_{name}", a.shape, mybir.dt.from_np(a.dtype), kind="ExternalInput").ap())
    args.append(nc.dram_tensor("out_x", (1, T, D), F32, kind="ExternalOutput").ap())
    build(nc, *args)
    r = run_bass_kernel_spmd(nc, [arrays], core_ids=[0])
    return r.results[0]["out_x"]
```

```python
from contextlib import ExitStack

import numpy as np

import concourse.bass as bass
from concourse import mybir

F32 = mybir.dt.float32
F32R = mybir.dt.float32r
I32 = mybir.dt.int32
ALU = mybir.AluOpType
ACT = mybir.ActivationFunctionType
AX = mybir.AxisListType.X

P = 128
D = 2048
T = 256
TB = T // P
KT = D // P
EPS = 1e-6
SB_HEADS, SB_DH = 16, 128
ML_HEADS, ML_DQ, ML_DV = 8, 128, 256
GROUPS, PER_GROUP = 4, 8
EXPERTS = GROUPS * PER_GROUP
FF = D // 8
ROUTER = GROUPS + EXPERTS
CAP = 32
QUAD = P // CAP
NQUAD = EXPERTS // QUAD
SLOTS = 12
HILO = 3
SLOT = 2048
COLS = 512
CSLOT = 4
TRI = 384
CLAMP = 40.0
SBG = 4
MLG = 2
NGROUP = 4
GATE_M = 5 * ML_HEADS
SMALL_LOADS = 4 + 2 * (KT // 4) + 4
XC = D // COLS
BANKS = ["T0", "T1", "A0", "A1", "G0", "G1", "S0", "S1"]

ARENA = 7280
RAW = 3
MIX_SLOTS = 12 * NGROUP + 16
OUT_ORDER = [(0, 0), (0, 1), (0, 2), (1, 0), (1, 1), (1, 2), (0, 3), (1, 3),
             (2, 0), (2, 1), (2, 2), (2, 3), (3, 0), (3, 1), (3, 2), (3, 3)]

SB_STEPS = [(2, "score", 0), (6, "score", 1), (14, "suffix", 0), (18, "suffix", 1),
            (20, "score", 2), (26, "out", 0), (28, "score", 3), (30, "out", 1),
            (38, "suffix", 2), (42, "suffix", 3), (50, "out", 2), (54, "out", 3)]
FIRST_STEPS = [(1 + n, "squares", n) for n in range(8)] + [(13, "rstd", 0), (27, "row", 0)]
ROUTER_STEPS = [(66, "turn", 0), (74, "turn", 1), (82, "logits", 0), (90, "logits", 1), (104, "turn", 2),
                (114, "logits", 2), (130, "turn", 3), (131, "logits", 3)]
ML_STEPS = [(0, "score", 0), (4, "sigmoid", 0), (8, "score", 1), (12, "num", 0), (20, "gate", 0),
            (27, "num", 1), (29, "sigmoid", 1), (36, "gate", 1), (39, "join", 0), (54, "join", 1)]
GATE_STEPS = (FIRST_STEPS + [(34, "gates", 0), (54, "columns", 0)] + [(66 + 3 * n, "spread", n) for n in range(8)])


def schedule(steps, slots, ends, scale=1.0, more=()):
    found = [(8 * (j - 2), 0, "split", j) for j in range(2, slots)]
    found += [(int(at * scale), 1 + n / 100, name, k) for n, (at, name, k) in enumerate(steps)]
    found += [(at, 0.5, "chunk", c) for c, at in enumerate(ends)]
    found += [(at, 2, name, k) for at, name, k in more]
    return [(at, name, k) for at, _, name, k in sorted(found)]


GROUP_ENDS = (32, 64, 96)
OUT_ENDS = (56, 64, 96, 128)
SCHEDULES = {}
for _layer, _steps in ((0, SB_STEPS), (1, ML_STEPS)):
    SCHEDULES[_layer, "first"] = schedule(GATE_STEPS if _layer else FIRST_STEPS, 14, GROUP_ENDS)
    SCHEDULES[_layer, "group"] = schedule(_steps, 14, GROUP_ENDS)
    SCHEDULES[_layer, "out"] = schedule(_steps, 16, OUT_ENDS, 0.75, ROUTER_STEPS)


def bank_uses():
    total = {b: 0 for b in BANKS}
    first = {}

    def phase(name, **n):
        first[name] = dict(total)
        for k, v in n.items():
            for b in BANKS:
                if b == k or b[0] == k:
                    total[b] += v

    phase("scales", S0=1)
    for layer in (0, 1):
        phase(("norm_mix", layer), T=2, A=1, S=1)
        phase(("row", layer), T1=1)
        if layer:
            phase(("gates", layer), T=1, A=ML_HEADS // 2)
        phase(("mix", layer), G=2 * NGROUP, S=NGROUP, T=(3 if layer else 2) * NGROUP, A=(1 if layer else 2) * NGROUP)
        phase(("out", layer), G=2, S=2)
        phase(("norm_ffn", layer), A=XC, T0=1)
        phase(("route", layer), G0=1, S0=1)
        phase(("gather", layer), G=2)
        phase(("moe", layer), G=5 * NQUAD - 2, A=2 * NQUAD, T=2 * NQUAD, S=4 * NQUAD)
    return first


def build(nc, x_in, norm_mix, norm_ffn, norm_final, sb_w_in, sb_w_out, ml_w_in, ml_b_i, ml_b_f,
          ml_g_head, ml_w_out, moe_w_group, moe_b_group, moe_w_expert, moe_b_expert,
          moe_w1, moe_w3, moe_w2, out):
    first_use = bank_uses()
    ctx = ExitStack()
    with ctx:
        place = [(nc.sbuf_base + 63) // 64 * 64]

        def at(name, offset, shape, dt=F32):
            return nc.alloc_sbuf_tensor_at(name, shape, dt, offset=offset)

        def sb(name, shape, dt=F32):
            size = 4 * int(np.prod(shape[1:]))
            offset = place[0]
            place[0] += (size + 63) // 64 * 64
            return at(name, offset, shape, dt)

        def sem(name):
            return ctx.enter_context(nc.semaphore(name))

        KB = 1024
        x = sb("x", [P, TB, D])
        expert_scale = sb("expert_scale", [P, 2, KT])
        scales = sb("scales", [P, 5, KT])
        ident = sb("ident", [P, P])
        neg_suffix = sb("neg_suffix", [P, P])
        neg_ones = sb("neg_ones", [P, P])
        before = sb("before", [P, P])
        ones = sb("ones", [P, P])
        fold = sb("fold", [P, CAP])
        iota = sb("iota", [P, CAP])
        thresholds = sb("thresholds", [1, T // CAP - 1])
        router_w = sb("router_w", [P, KT, ROUTER])
        router_b = sb("router_b", [P, ROUTER])
        gate_w = sb("gate_w", [P, KT // 4, 2, 4, ML_HEADS])
        gate_hi = sb("gate_hi", [P, KT * 2 * ML_HEADS], F32R)
        gate_lo = sb("gate_lo", [P, KT * 2 * ML_HEADS], F32R)
        gate_b = sb("gate_b", [ML_HEADS, 2])
        squares = sb("squares", [P, COLS])
        sumsq_c = sb("sumsq_c", [P, TB, XC])
        sumsq = sb("sumsq", [P, TB])
        mean_eps = sb("mean_eps", [P, TB])
        rstd = sb("rstd", [P, TB])
        neg_rstd = sb("neg_rstd", [P, TB])
        newton = sb("newton", [P, TB])
        extra_f = sb("extra_f", [1, 1])
        extra_i = sb("extra_i", [1, 1], I32)
        count_max = sb("count_max", [1, 1])
        count_lt = sb("count_lt", [1, T // CAP - 1])

        rows_at = place[0]
        h = sb("h", [P, TB, D])
        o_hi = at("o_hi", rows_at, [P, KT, T], F32R)
        turned_at = place[0]
        xT_hi = sb("xT_hi", [P, KT, T], F32R)
        xT_lo = sb("xT_lo", [P, KT, T], F32R)
        xT = at("xT", turned_at, [P, KT, T])
        arena_two = at("arena_two", turned_at + 16 * KB, [P, 4096])
        ring_at = place[0]
        ring = sb("ring", [P, SLOTS, SLOT])
        after_ring = place[0]
        last_scale = sb("last_scale", [P, D])
        w_hi = at("w_hi", ring_at + 3 * 8 * KB, [P, HILO, SLOT], F32R)
        w_lo = at("w_lo", ring_at + 6 * 8 * KB, [P, HILO, SLOT], F32R)
        o_lo = at("o_lo", ring_at + 9 * 8 * KB, [P, KT, T], F32R)
        arena_three = at("arena_three", ring_at + 11 * 8 * KB, [P, 4096])
        arena = sb("arena", [P, ARENA])
        extra_slots = (at("extra_one", after_ring, [P, 2, SLOT]), at("extra_two", turned_at, [P, 2, SLOT]))
        assert place[0] <= nc.sbuf_usable_end, place[0]

        over_w = xT[:, :, :].rearrange("p k t -> p (k t)")[:, 0:2 * SLOT].rearrange("p (s n) -> p s n", s=2)
        hv = h[:, :, :].rearrange("p b (c k) -> p b k c", k=KT)

        class Region:
            def __init__(self, whole):
                self.whole, self.at = whole, 0

            def __call__(self, *shape):
                n = int(np.prod(shape))
                view = self.whole[:, self.at:self.at + n]
                self.at += n
                assert self.at <= self.whole.shape[1], self.at
                names = " ".join("abcd"[:len(shape)])
                sizes = {"abcd"[k]: s for k, s in enumerate(shape) if k}
                return view.rearrange(f"p ({names}) -> p {names}", **sizes) if len(shape) > 1 else view

        rstd_row = arena[:, ARENA - T:]
        diag = arena_three[:, 0:TB * P].rearrange("p (b t) -> p b t", b=TB)
        scale_rows = arena[:, 0:P]
        r = Region(arena)
        qT, kT = r(SBG, T), r(SBG, T)
        v_raw = r(TB, COLS)
        r = Region(arena_three)
        soft, sp, prob = r(2, TRI), r(2, TRI), r(2, TRI)
        r = Region(arena_three)
        decay = r(ML_HEADS, TRI)
        weights = r(MLG, TRI)
        r = Region(arena)
        v_one, o_exp = r(TB, MLG, ML_DV + 1), r(TB, COLS)
        qkT = r(MLG, 2, T)
        selector = r(ML_HEADS, P)[0:ML_HEADS]
        at_rows = r.at
        gated = r(MLG, TB, ML_DV)
        hs = r(TB, ML_DV)
        r.at = at_rows + 7 * T
        u_col, m_col = r(TB, ML_HEADS), r(TB, ML_HEADS)
        den, ssq, ms, hrs, hnw = r(TB), r(TB), r(TB), r(TB), r(TB)
        r.at = at_rows
        g_y, g_clip, g_sp, g_negb, g_u, g_m, g_em = (r(T)[0:ML_HEADS] for _ in range(7))
        r = Region(arena_two)
        disp = r(TB, EXPERTS, CAP)
        acc = r(2, COLS)
        disp_g, spread = r(TB, P), r(TB, P)
        hid = r(QUAD, 2 * CAP)
        r = Region(arena)
        r(SLOT)
        xe = r(KT, P)
        y = r(D)
        ex, sg, t13 = r(2 * CAP), r(2 * CAP), r(2 * CAP)
        logits = r(TB, ROUTER)
        gsel, gexp, gcmp = r(TB, GROUPS), r(TB, GROUPS), r(TB, GROUPS)
        gmax, gsum, tie, psel = r(TB, 1), r(TB, 1), r(TB, 1), r(TB, 1)
        picked = r(TB, GROUPS, PER_GROUP)
        es, cmp8, s1, s2, gate8, tmp8 = (r(TB, PER_GROUP) for _ in range(6))
        m1, m2, dm, w1c, w2c = (r(TB, 1) for _ in range(5))
        gates, mask, posm = (r(TB, EXPERTS) for _ in range(3))
        rank = r(PER_GROUP)
        over_d, over_g = r(TB, CAP), r(TB, CAP)

        psum = {b: ctx.enter_context(nc.psum_tensor(f"psum_{b}", [P, 512], F32)) for b in BANKS}

        filled = {b: sem(f"filled_{b}") for b in BANKS}
        emptied = {b: sem(f"emptied_{b}") for b in BANKS}
        slot_loaded = [sem(f"slot_loaded_{n}") for n in range(SLOTS + CSLOT)]
        raw_loaded = [sem(f"raw_loaded_{n}") for n in range(RAW)]
        hi_made = sem("hi_made")
        lo_made = sem("lo_made")
        split_read = sem("split_read")
        pool_lo_made = sem("pool_lo_made")
        row_hi_made = sem("row_hi_made")
        out_hi_made = sem("out_hi_made")
        gate_hi_made = sem("gate_hi_made")
        gate_lo_made = sem("gate_lo_made")
        rows_loaded = sem("rows_loaded")
        scales_made = sem("scales_made")
        router_scaled = sem("router_scaled")
        x_final = sem("x_final")
        row_ready = sem("row_ready")
        x_loaded = [sem(f"x_loaded_{b}") for b in range(TB)]
        last_scale_loaded = sem("last_scale_loaded")
        small_loaded = [sem("small_loaded_0"), sem("small_loaded_1")]
        ident_made = sem("ident_made")
        consts_made = sem("consts_made")
        squares_done = sem("squares_done")
        mean_ready = sem("mean_ready")
        rstd_seed = sem("rstd_seed")
        rstd_ready = sem("rstd_ready")
        h_ready = sem("h_ready")
        clipped = sem("clipped")
        softplus_log = sem("softplus_log")
        softplus_full = sem("softplus_full")
        softplus_masked = sem("softplus_masked")
        suffix_summed = sem("suffix_summed")
        prob_exp = sem("prob_exp")
        mask_begun = sem("mask_begun")
        prob_masked = sem("prob_masked")
        gate_clip = sem("gate_clip")
        gate_log = sem("gate_log")
        gate_rows = sem("gate_rows")
        gate_exp = sem("gate_exp")
        decay_exp = sem("decay_exp")
        decay_masked = sem("decay_masked")
        ones_set = sem("ones_set")
        weights_ready = sem("weights_ready")
        head_squares = sem("head_squares")
        head_seed = sem("head_seed")
        gated_ready = sem("gated_ready")
        group_shift = sem("group_shift")
        group_exp = sem("group_exp")
        top2_gap = sem("top2_gap")
        top2_exp = sem("top2_exp")
        mask_ready = sem("mask_ready")
        disp_ready = sem("disp_ready")
        extra_ready = sem("extra_ready")
        disp_gated = sem("disp_gated")
        silu_exp = sem("silu_exp")
        exp_taken = sem("exp_taken")
        hid_ready = sem("hid_ready")
        over = [{n: sem(f"over_{n}_{layer}") for n in (
            "slots", "rows_filled", "rows", "spread_filled", "spread", "w_loaded", "w_used", "acc",
            "turned", "exp", "hid", "y", "scattered", "done")} for layer in (0, 1)]
        out_ready = sem("out_ready")
        out_stored = sem("out_stored")

        block = ctx.enter_context(nc.Block())

        def turned_bank(layer, u):
            bank = ("T0", "T1", "A0", "A1", "S0", "S1")[u % 6]
            return bank, first_use["norm_mix", layer][bank] + u // 6

        def group_bank(c, b):
            return f"{'GSG'[c]}{b}"

        def chunk_filled(layer, i, c, b):
            bank = group_bank(c, b)
            return filled[bank], i * (1 if c == 1 else 2) + (first_use["mix", layer][bank] + c // 2 + 1)

        def out_filled(layer, c, b):
            bank = f"{'GS'[c % 2]}{b}"
            return filled[bank], first_use["out", layer][bank] + c // 2 + 1

        def value_chunk(layer):
            return 1 if layer else 2

        def value_parts(layer, i, b):
            c = value_chunk(layer)
            bank = group_bank(c, b)
            if layer:
                return (bank, chunk_filled(layer, i, c, b), psum[bank][:, :].rearrange("p (h n) -> p h n", h=MLG),
                        v_one[:, b, :, 0:ML_DV])
            return bank, chunk_filled(layer, i, c, b), psum[bank][:, :], v_raw[:, b, :]

        def mix_slot(layer, i, j):
            return i * 12 + (layer * MIX_SLOTS + j)

        def slot_place(j):
            return (j + 2) % RAW

        def split_was_read(layer, i, j):
            if j < 0:
                i, j = i - 1, j + 12
            if isinstance(i, int) and i == NGROUP:
                c, n = OUT_ORDER[j]
                if n == 3:
                    return out_filled(layer, c, 1)
                done = sum(1 for _, m in OUT_ORDER[:j + 1] if m < 3)
                return split_read, layer * (9 * NGROUP + 12) + 9 * NGROUP + done
            c = j // 4
            if j % 4 == 3:
                return chunk_filled(layer, i, c, 1)
            return split_read, i * 9 + (layer * (9 * NGROUP + 12) + 3 * c + j % 4 + 1)

        def split_hi(act, layer, i, j):
            n = mix_slot(layer, i, j)
            former = layer * -(-(MIX_SLOTS - j % RAW) // RAW)
            act.wait_ge(raw_loaded[j % RAW], i * (16 * 12 // RAW) + 16 * (former + j // RAW + 1))
            if not (isinstance(i, int) and i == 0 and j < HILO):
                act.wait_ge(*split_was_read(layer, i, j - HILO))
            act.copy(w_hi[:, slot_place(j), :], ring[:, slot_place(j), :]).then_inc(hi_made, 1)

        def split_lo(dve, layer, i, j):
            dve.wait_ge(hi_made, mix_slot(layer, i, j) + 1)
            dve.tensor_tensor(w_lo[:, slot_place(j), :], ring[:, slot_place(j), :], w_hi[:, slot_place(j), :].bitcast(F32),
                              ALU.subtract).then_inc(lo_made, 1)

        def overflow_passes(eng, layer, expert, after=None):
            eng.wait_ge(extra_ready, layer + 1)
            extra = eng.value_load(extra_i[0:1, 0:1], min_val=0, max_val=T // CAP - 1)
            with eng.If(extra > 0):
                with eng.Fori(0, extra) as turn:
                    with eng.Fori(0, EXPERTS) as e:
                        expert(turn * EXPERTS + e, e)
                if after:
                    after()

        def slot_at(j, first):
            return j if first and j < 4 * QUAD else (j + 2 * CSLOT) % SLOTS

        def slot_view(n, count):
            return ring[:, n:n + count, :] if n < SLOTS else extra_slots[(n - SLOTS) // 2][:, n % 2:n % 2 + count, :]

        def slot_value(layer, i, j, first):
            unit, where = j // CSLOT, slot_at(j, first) // CSLOT
            if where == 3:
                return 16 * (layer + 1)
            former = layer * (2 * NQUAD - (where == 2))
            if first:
                return 16 * (former + (1 if unit < 3 else 2))
            return i * 32 + 16 * (former + {1: 1, 4: 2, 2: 1, 5: 2, 0: 0, 3: 1}[unit])

        def w13_tile(q, k, first):
            n = slot_at(4 * q + 2 * (k // 8), first)
            return slot_view(n, 2)[:, :, (k % 8) * FF:(k % 8 + 1) * FF]

        @block.sync
        def _(sp_eng):
            def mix_stream(layer, i, slots=range(12)):
                w = (ml_w_in if layer else sb_w_in)[0].rearrange("(k p) n -> p k n", p=P)
                for j in slots:
                    c, k0 = j // CSLOT, 4 * (j % CSLOT)
                    if layer and isinstance(i, int) and i == 0 and j == 0:
                        sp_eng.wait_ge(*freed_moe(0, NQUAD - 1)[4])
                    elif not (isinstance(i, int) and i == 0 and j < RAW):
                        sp_eng.wait_ge(lo_made, mix_slot(layer, i, j) + (1 - RAW))
                    if layer and c == 0:
                        part, k8 = j // 2, 8 * (j % 2)
                        dst = ring[:, slot_place(j), :].rearrange("p (k n) -> p k n", k=8)
                        src = w[:, k8:k8 + 8, bass.ds(i * FF + part * ML_HEADS * ML_DQ, FF)]
                    else:
                        dst = ring[:, slot_place(j), :].rearrange("p (k n) -> p k n", k=4)
                        src = w[:, k0:k0 + 4, bass.ds(i * COLS + c * D, COLS)]
                    sp_eng.dma_start(dst, src).then_inc(raw_loaded[j % RAW], 16)

            def out_stream(layer):
                w = (ml_w_out if layer else sb_w_out)[0].rearrange("(k p) n -> p k n", p=P)
                for j, (c, n) in enumerate(OUT_ORDER):
                    sp_eng.wait_ge(lo_made, mix_slot(layer, NGROUP, j) + (1 - RAW))
                    sp_eng.dma_start(ring[:, slot_place(j), :].rearrange("p (k n) -> p k n", k=4),
                                     w[:, 4 * n:4 * n + 4, c * COLS:(c + 1) * COLS]).then_inc(raw_loaded[j % RAW], 16)

            def freed_moe(layer, i):
                base = first_use["moe", layer]
                last = isinstance(i, int) and i == NQUAD - 1
                return ([(filled[f"A{q % 2}"], i * 2 + (base[f"A{q % 2}"] + q // 2 + 1)) for q in range(QUAD)]
                        + [(filled["G1"], i * 5 + (base["G1"] + (1 if last else 3) + n)) for n in (1, 2)])

            def moe_stream(layer, i, before):
                first = isinstance(i, int)
                freed = dict(before)
                early = [j for j in before if first]
                own = freed_moe(layer, i)
                for unit in range(4 if first else 3, 6):
                    freed[CSLOT * unit] = own[unit - (4 if first else 3)]
                for j in early + [j for j in range(6 * QUAD) if j not in early]:
                    if j in freed:
                        sp_eng.wait_ge(*freed[j])
                    s = slot_at(j, first)
                    if j < 4 * QUAD:
                        w = (moe_w1, moe_w3)[j % 2][layer].rearrange("e (p k) f -> p e (k f)", k=KT)
                        e, half = j // 4, (j % 4) // 2
                        src = w[:, bass.ds(i * QUAD + e, 1), half * SLOT:(half + 1) * SLOT]
                    else:
                        half, e = (j - 4 * QUAD) // QUAD, j % QUAD
                        w = moe_w2[layer].rearrange("e (k p) n -> p e k n", p=P)
                        src = w[:, bass.ds(i * QUAD + e, 1), :, half * D // 2:(half + 1) * D // 2]
                    dst = slot_view(s, 1)
                    if j >= 4 * QUAD:
                        dst = dst.rearrange("p s (k n) -> p s k n", k=2)
                    sp_eng.dma_start(dst, src).then_inc(slot_loaded[s], 16)

            def overflow(layer):
                o = over[layer]

                def expert(k, e):
                    for half in range(2):
                        sp_eng.wait_ge(o["w_used"], k * 3 + (half + 1))
                        for n, w in enumerate((moe_w1, moe_w3)):
                            src = w[layer].rearrange("e (p k) f -> p e (k f)", k=KT)
                            sp_eng.dma_start(over_w[:, n:n + 1, :], src[:, bass.ds(e, 1), half * SLOT:(half + 1) * SLOT]
                                             ).then_inc(o["w_loaded"], 16)
                    sp_eng.wait_ge(o["w_used"], k * 3 + 3)
                    src = moe_w2[layer].rearrange("e (k p) n -> k p e n", p=P)
                    for ft in range(2):
                        sp_eng.dma_start(over_w[:, ft:ft + 1, :], src[ft, :, bass.ds(e, 1), :]
                                         ).then_inc(o["w_loaded"], 16)

                overflow_passes(sp_eng, layer, expert)

            for n, w in ((0, norm_mix), (2, norm_ffn), (4, ml_g_head)):
                m = w.shape[0] * KT
                sp_eng.dma_start(scale_rows[n * KT:n * KT + m, :], w.rearrange("n (k p) -> (n k) p", p=P)
                                 ).then_inc(rows_loaded, 16)
            for b in range(TB):
                sp_eng.dma_start(x[:, b, :], x_in[0, b * P:(b + 1) * P, :]).then_inc(x_loaded[b], 16)
            for layer in (0, 1):
                if layer == 0:
                    mix_stream(layer, 0, range(RAW))
                mix_stream(layer, 0, range(RAW, 12))
                with sp_eng.Fori(1, NGROUP) as g:
                    mix_stream(layer, g)
                out_stream(layer)
                attended = (filled["T1"], first_use["mix", layer]["T1"] + (3 if layer else 2) * NGROUP)
                last = len(OUT_ORDER) - RAW
                before = {SLOTS: attended, SLOTS + 1: attended}
                before.update((n, (lo_made, mix_slot(layer, NGROUP, last + n) + 1)) for n in range(RAW))
                before.update((RAW + n + m * HILO, split_was_read(layer, NGROUP, last + n))
                              for n in range(RAW) for m in range(2))
                before.update((j, out_filled(layer, 3, 1)) for j in range(RAW + 2 * HILO, SLOTS))
                before.update((j, (filled["T0"], first_use["norm_ffn", layer]["T0"] + 1)) for j in (SLOTS + 2, SLOTS + 3))
                moe_stream(layer, 0, before)
                with sp_eng.Fori(1, NQUAD) as i:
                    moe_stream(layer, i, {CSLOT * n: signal for n, signal in enumerate(freed_moe(layer, i - 1)[3:])})
                if layer == 0:
                    mix_stream(1, 0, range(RAW))
                overflow(layer)
            for n in range(2 * TB):
                b, c = n // 2, slice((n % 2) * D // 2, (n % 2 + 1) * D // 2)
                sp_eng.wait_ge(out_ready, n + 1)
                sp_eng.dma_start(out[0, b * P:(b + 1) * P, c], h[:, b, c]).then_inc(out_stored, 16)
            sp_eng.wait_ge(out_stored, 16 * 2 * TB)

        @block.gpsimd
        def _(pool):
            def load_small(layer):
                s = small_loaded[layer]
                pool.dma_start(router_w[:, :, 0:GROUPS], moe_w_group[layer].rearrange("(k p) n -> p k n", p=P)).then_inc(s, 16)
                pool.dma_start(router_w[:, :, GROUPS:ROUTER], moe_w_expert[layer].rearrange("(k p) n -> p k n", p=P)).then_inc(s, 16)
                pool.dma_start(router_b[:, 0:GROUPS], moe_b_group[layer].partition_broadcast(P)).then_inc(s, 16)
                pool.dma_start(router_b[:, GROUPS:ROUTER], moe_b_expert[layer].partition_broadcast(P)).then_inc(s, 16)

            pool.memset(ident[:, :], 0.0)
            pool.drain()
            pool.affine_select(out=ident[:, :], in_=ident[:, :], compare_op=ALU.not_equal, fill=1.0,
                               base=0, pattern=[[-1, P]], channel_multiplier=1)
            pool.drain().then_inc(ident_made, 1)
            pool.memset(fold[:, :], 0.0)
            pool.memset(neg_ones[:, :], -1.0)
            pool.memset(ones[:, :], 1.0)
            pool.iota(iota[:, :], pattern=[[1, CAP]], base=1, channel_multiplier=0,
                      allow_small_or_imprecise_dtypes=True)
            pool.drain()
            pool.affine_select(out=neg_suffix[:, :], in_=neg_ones[:, :], compare_op=ALU.is_ge, fill=0.0,
                               base=0, pattern=[[-1, P]], channel_multiplier=1)
            pool.affine_select(out=before[:, :], in_=ones[:, :], compare_op=ALU.is_gt, fill=0.0,
                               base=0, pattern=[[1, P]], channel_multiplier=-1)
            for q in range(QUAD):
                pool.affine_select(out=fold[:, :], in_=fold[:, :], compare_op=ALU.not_equal, fill=1.0,
                                   base=-q * CAP, pattern=[[-1, CAP]], channel_multiplier=1)
                pool.drain()
            pool.drain().then_inc(consts_made, 1)
            def split_lo_one(layer):
                pool.wait_ge(hi_made, mix_slot(layer, 0, 1) + 1)
                pool.tensor_tensor(w_lo[:, slot_place(1), :], ring[:, slot_place(1), :],
                                   w_hi[:, slot_place(1), :].bitcast(F32), ALU.subtract)
                pool.drain().then_inc(pool_lo_made, 1)

            def keep_causal(view, strict):
                pool.affine_select(out=view, in_=view, compare_op=ALU.is_gt if strict else ALU.is_ge,
                                   fill=0.0, base=0, pattern=[[0, 2], [1, P]], channel_multiplier=-1)
                return pool.drain()

            def diagonals(tile):
                return tile.rearrange("p (c n) -> p c n", n=P)[:, 0:3:2, :]

            def sb_group(g):
                for _, step, k in SB_STEPS:
                    if step == "score":
                        pool.wait_ge(softplus_full, g * SBG + k + 1)
                        pool.sem_inc(mask_begun, 1)
                        keep_causal(diagonals(sp[:, k % 2, :]), True).then_inc(softplus_masked, 1)
                    if step == "suffix":
                        pool.wait_ge(prob_exp, g * SBG + k + 1)
                        pool.sem_inc(mask_begun, 1)
                        keep_causal(diagonals(prob[:, k % 2, :]), True).then_inc(prob_masked, 1)

            split_lo_one(0)
            load_small(0)
            for n, c in ((0, 3 * D + ML_HEADS), (1, 3 * D)):
                for m in range(KT // 4):
                    pool.dma_start(gate_w[:, m, n, :, :], ml_w_in[0, :, c:c + ML_HEADS].rearrange(
                        "(m k p) n -> m p k n", m=KT // 4, p=P)[m]).then_inc(small_loaded[0], 16)
            for n in range(2):
                pool.dma_start(expert_scale[:, n, :], norm_ffn[n].rearrange("(p k) -> p k", k=KT)).then_inc(small_loaded[0], 16)
            pool.dma_start(gate_b[:, 0:1], ml_b_i.rearrange("o n -> n o")).then_inc(small_loaded[0], 16)
            pool.dma_start(gate_b[:, 1:2], ml_b_f.rearrange("o n -> n o")).then_inc(small_loaded[0], 16)

            with pool.Fori(0, NGROUP) as g:
                sb_group(g)

            pool.wait_ge(mask_ready, 1)
            load_small(1)
            split_lo_one(1)
            pool.wait_ge(rstd_ready, 3)
            pool.memset(v_one[:, :, :, ML_DV:ML_DV + 1], 1.0)
            pool.memset(selector, 1.0)
            pool.drain()
            pool.affine_select(out=selector, in_=selector, compare_op=ALU.is_equal, fill=0.0, base=0,
                               pattern=[[-1, ML_HEADS], [0, P]], channel_multiplier=1)
            pool.drain().then_inc(ones_set, 1)
            for hd in range(ML_HEADS):
                pool.wait_ge(decay_exp, hd + 1)
                keep_causal(diagonals(decay[:, hd, :]), False).then_inc(decay_masked, 1)
            pool.wait_ge(filled["A1"], first_use["moe", 1]["A1"] + 2)
            pool.dma_start(last_scale[:, :], norm_final.partition_broadcast(P)).then_inc(last_scale_loaded, 16)

        @block.tensor
        def _(pe):
            def claim(b, n):
                if not (isinstance(n, int) and n == 0):
                    pe.wait_ge(emptied[b], n)

            def mm(dst, lhsT, rhs, start, stop):
                return pe.matmul(dst, lhsT, rhs, start=start, stop=stop, skip_group_check=True)

            def turn_tiles(bank, k0):
                for k in (k0, k0 + 1):
                    for b in range(TB):
                        c = (k - k0) * T + b * P
                        last = pe.transpose(psum[bank][:, c:c + P], x[:, b, k * P:(k + 1) * P], ident[:, :])
                last.then_inc(filled[bank], 1)

            def turn_x(layer):
                for u in range(KT // 2):
                    bank, n = turned_bank(layer, u)
                    claim(bank, n)
                    turn_tiles(bank, 2 * u)

            def wait_turned(layer, units):
                for u in units:
                    bank, n = turned_bank(layer, u)
                    pe.wait_ge(emptied[bank], n + 1)

            def rstd_rows(layer):
                if layer == 0:
                    pe.wait_ge(consts_made, 1)
                pe.wait_ge(row_ready, layer + 1)
                claim("T1", first_use["row", layer]["T1"])
                for b in range(TB):
                    last = mm(psum["T1"][:, b * P:(b + 1) * P], ones[:, :], diag[:, b, :], True, True)
                last.then_inc(filled["T1"], 1)

            def router_step(layer, step, c):
                base = first_use["norm_ffn", layer]
                if step == "turn":
                    for b in range(TB):
                        bank = f"{'GS'[c % 2]}{b}"
                        pe.wait_ge(emptied[bank], first_use["out", layer][bank] + c // 2 + 1)
                    for n in range(2):
                        claim(f"A{n}", base[f"A{n}"] + c)
                        turn_tiles(f"A{n}", 4 * c + 2 * n)
                else:
                    if c == 0:
                        pe.wait_ge(router_scaled, layer + 1)
                        claim("T0", base["T0"])
                    for n in range(2):
                        pe.wait_ge(emptied[f"A{n}"], base[f"A{n}"] + c + 1)
                    for k in range(4 * c, 4 * c + 4):
                        for b in range(TB):
                            last = mm(psum["T0"][:, b * ROUTER:(b + 1) * ROUTER], xT[:, k, b * P:(b + 1) * P],
                                      router_w[:, k, :], k == 0 and b == 0, k == KT - 1)
                    if c == XC - 1:
                        last.then_inc(filled["T0"], 1)

            def gates_logits():
                pe.wait_ge(gate_lo_made, 1)
                wait_turned(1, range(KT // 2))
                claim("T0", first_use["gates", 1]["T0"])
                dst = psum["T0"][0:GATE_M, 0:T]
                for k in range(KT):
                    at_ = 8 * ML_HEADS * (k // 4) + ML_HEADS * (k % 4)
                    hi, lo = gate_hi[:, at_:at_ + GATE_M], gate_lo[:, at_:at_ + GATE_M]
                    mm(dst, hi, xT_hi[:, k, :], k == 0, False)
                    mm(dst, hi, xT_lo[:, k, :], False, False)
                    last = mm(dst, lo, xT_hi[:, k, :], False, k == KT - 1)
                last.then_inc(filled["T0"], 1)

            def gates_turn():
                base = first_use["gates", 1]
                pe.wait_ge(gate_rows, 1)
                pe.wait_ge(gate_exp, 1)
                claim("T1", base["T1"])
                for n, row in enumerate((g_u, g_em)):
                    for b in range(TB):
                        c = (n * TB + b) * ML_HEADS
                        last = pe.transpose(psum["T1"][:, c:c + ML_HEADS], row[:, b * P:(b + 1) * P],
                                            ident[0:ML_HEADS, 0:ML_HEADS])
                last.then_inc(filled["T1"], 1)

            def gates_spread(hd):
                bank = ("A0", "A1")[hd % 2]
                if hd == 0:
                    pe.wait_ge(ones_set, 1)
                claim(bank, first_use["gates", 1][bank] + hd // 2)
                mm(psum[bank][:, 0:T], selector[:, hd, :], g_m, True, True).then_inc(filled[bank], 1)

            def three(dst, rows, b, k, w, first, last_one):
                hi, lo = rows
                t = slice(b * P, (b + 1) * P)
                mm(dst, hi[:, k, t], w_hi[:, w[0], w[1]], first, False)
                mm(dst, hi[:, k, t], w_lo[:, w[0], w[1]], False, False)
                return mm(dst, lo[:, k, t], w_hi[:, w[0], w[1]], False, last_one)

            def three_turned(dst, k, w, first, last_one):
                mm(dst, w_hi[:, w[0], w[1]], xT_hi[:, k, :], first, False)
                mm(dst, w_hi[:, w[0], w[1]], xT_lo[:, k, :], False, False)
                return mm(dst, w_lo[:, w[0], w[1]], xT_hi[:, k, :], False, last_one)

            def project(layer, i, event):
                base = first_use["mix", layer]
                for j in range(12):
                    c = j // CSLOT

                    def begin(n):
                        if j % CSLOT == 0:
                            bank = group_bank(c, n)
                            claim(bank, i * (1 if c == 1 else 2) + (base[bank] + c // 2))

                    pe.wait_ge(lo_made, mix_slot(layer, i, j) + 1)
                    if layer and c == 0:
                        for hd in range(MLG):
                            begin(hd)
                            for kk in range(8):
                                k = (j % 2) * 8 + kk
                                if isinstance(i, int) and i == 0 and j < 2 and hd == 0 and kk % 2 == 0:
                                    wait_turned(layer, (k // 2,))
                                if kk % 2 == 0:
                                    event(8 * j + 4 * hd + kk // 2)
                                last = three_turned(psum[f"G{hd}"][:, (j // 2) * T:(j // 2 + 1) * T], k,
                                                    (slot_place(j), slice(kk * FF + hd * P, kk * FF + (hd + 1) * P)),
                                                    k == 0, k == KT - 1)
                                if k == KT - 1 and j == 3:
                                    last.then_inc(filled[f"G{hd}"], 1)
                    elif layer == 0 and c < 2:
                        for hd, kk in ((2 * n + m, kk) for n in range(2) for kk in range(4) for m in range(2)):
                            k = (j % 4) * 4 + kk
                            if hd % 2 == 0:
                                if kk == 0:
                                    begin(hd // 2)
                                if isinstance(i, int) and i == 0 and c == 0 and hd == 0 and kk % 2 == 0:
                                    wait_turned(layer, (k // 2,))
                                event(8 * j + 4 * (hd // 2) + kk)
                            bank = group_bank(c, hd // 2)
                            last = three_turned(psum[bank][:, (hd % 2) * T:(hd % 2 + 1) * T], k,
                                                (slot_place(j), slice(kk * COLS + hd * P, kk * COLS + (hd + 1) * P)),
                                                k == 0 and hd % 2 == 0, k == KT - 1)
                            if k == KT - 1 and hd % 2 == 1:
                                last.then_inc(filled[bank], 1)
                    else:
                        for b in range(TB):
                            begin(b)
                            for kk in range(4):
                                k = (j % 4) * 4 + kk
                                event(8 * j + 4 * b + kk)
                                last = three(psum[group_bank(c, b)][:, :], (xT_hi, xT_lo), b, k,
                                             (slot_place(j), slice(kk * COLS, (kk + 1) * COLS)), k == 0, k == KT - 1)
                                if k == KT - 1:
                                    last.then_inc(filled[group_bank(c, b)], 1)
                    if j % CSLOT != 3:
                        last.then_inc(split_read, 1)

            def wait_chunk(layer, i, c):
                base = first_use["mix", layer]
                for b in range(TB):
                    bank = group_bank(c, b)
                    pe.wait_ge(emptied[bank], i * (1 if c == 1 else 2) + (base[bank] + c // 2 + 1))

            def sb_step(g, step, k):
                base = first_use["mix", 0]
                t, a = f"T{k % 2}", f"A{k % 2}"
                if step == "score":
                    if k == 0:
                        wait_chunk(0, g, 0)
                        wait_chunk(0, g, 1)
                    claim(a, g * 2 + base[a] + k // 2)
                    mm(psum[a][:, 0:T], kT[:, k, 0:P], qT[:, k, :], True, False)
                    mm(psum[a][:, T:TRI], kT[:, k, P:T], qT[:, k, P:T], False, True).then_inc(filled[a], 1)
                if step == "suffix":
                    pe.wait_ge(softplus_masked, g * SBG + k + 1)
                    s = sp[:, k % 2, :]
                    mm(psum[a][:, 0:T], neg_suffix[:, :], s[:, 0:T], False, False)
                    mm(psum[a][:, P:T], neg_ones[:, :], s[:, T:TRI], False, False)
                    mm(psum[a][:, T:TRI], neg_suffix[:, :], s[:, T:TRI], False, True).then_inc(suffix_summed, 1)
                if step == "out":
                    if k == 0:
                        wait_chunk(0, g, 2)
                    pe.wait_ge(prob_masked, g * SBG + k + 1)
                    claim(t, g * 2 + base[t] + k // 2)
                    v = v_raw[:, :, k * SB_DH:(k + 1) * SB_DH]
                    mm(psum[t][:, 0:T], v[:, 0, :], prob[:, k % 2, 0:T], True, False)
                    mm(psum[t][:, P:T], v[:, 1, :], prob[:, k % 2, T:TRI], False, True).then_inc(filled[t], 1)

            def ml_step(g, step, k):
                base = first_use["mix", 1]
                t, a = f"T{k}", f"A{k}"
                if step == "score":
                    if k == 0:
                        wait_chunk(1, g, 0)
                    claim(a, g + base[a])
                    q, kk = qkT[:, k, 0, :], qkT[:, k, 1, :]
                    mm(psum[a][:, 0:T], kk[:, 0:P], q, True, False)
                    mm(psum[a][:, T:TRI], kk[:, P:T], q[:, P:T], False, True).then_inc(filled[a], 1)
                if step == "num":
                    if k == 0:
                        wait_chunk(1, g, 1)
                    pe.wait_ge(weights_ready, g * MLG + k + 1)
                    claim("T0", g * 3 + base["T0"] + k)
                    claim("T1", g * 3 + base["T1"] + k)
                    w = weights[:, k, :]
                    mm(psum["T0"][:, 0:ML_DV + 1], w[:, 0:P], v_one[:, 0, k, :], True, True).then_inc(filled["T0"], 1)
                    mm(psum["T1"][:, 0:ML_DV + 1], w[:, P:T], v_one[:, 0, k, :], True, False)
                    mm(psum["T1"][:, 0:ML_DV + 1], w[:, T:TRI], v_one[:, 1, k, :], False, True).then_inc(filled["T1"], 1)
                if step == "join":
                    pe.wait_ge(gated_ready, g * MLG + k + 1)
                    claim(t, g * 3 + base[t] + 2)
                    for n in range(2):
                        for b in range(TB):
                            last = pe.transpose(psum[t][:, n * T + b * P:n * T + (b + 1) * P],
                                                gated[:, k, b, n * P:(n + 1) * P], ident[:, :])
                    last.then_inc(filled[t], 1)

            def mix(layer):
                step = ml_step if layer else sb_step

                def first_group(m):
                    for at_, name, k in SCHEDULES[layer, "first"]:
                        if at_ == m:
                            if name == "row":
                                rstd_rows(layer)
                            elif name == "gates":
                                gates_logits()
                            elif name == "columns":
                                gates_turn()
                            elif name == "spread":
                                gates_spread(k)

                def during(kind, g):
                    def event(m):
                        for at_, name, k in SCHEDULES[layer, kind]:
                            if at_ == m and name in ("turn", "logits"):
                                router_step(layer, name, k)
                            elif at_ == m and name not in ("chunk", "split"):
                                step(g, name, k)
                    return event

                project(layer, 0, first_group)
                with pe.Fori(1, NGROUP) as i:
                    project(layer, i, during("group", i - 1))
                project_out(layer, during("out", NGROUP - 1))

            def project_out(layer, event):
                base = first_use["out", layer]
                for j, (c, n) in enumerate(OUT_ORDER):
                    banks = [f"{'GS'[c % 2]}{b}" for b in range(TB)]
                    if n == 0:
                        for b in banks:
                            claim(b, base[b] + c // 2)
                    if j in (0, 6):
                        for t in ("T0", "T1"):
                            per = 3 if layer else 2
                            pe.wait_ge(emptied[t], first_use["mix", layer][t] + per * (NGROUP if j else NGROUP - 1))
                    pe.wait_ge(lo_made, mix_slot(layer, NGROUP, j) + 1)
                    for kk in range(4):
                        k = 4 * n + kk
                        for b in range(TB):
                            event(8 * j + kk * TB + b)
                            last = three(psum[banks[b]][:, :], (o_hi, o_lo), b, k,
                                         (slot_place(j), slice(kk * COLS, (kk + 1) * COLS)), k == 0, k == KT - 1)
                            if k == KT - 1:
                                last.then_inc(filled[banks[b]], 1)
                    if n != 3:
                        last.then_inc(split_read, 1)
                for m, _, _ in SCHEDULES[layer, "out"]:
                    if m > 8 * len(OUT_ORDER):
                        event(m)

            def route(layer):
                base = first_use["route", layer]
                pe.wait_ge(mask_ready, layer + 1)
                g = psum["G0"]
                claim("G0", base["G0"])
                mm(g[:, 0:EXPERTS], before[:, :], mask[:, 0, :], True, True)
                mm(g[:, EXPERTS:2 * EXPERTS], before[:, :], mask[:, 1, :], True, False)
                mm(g[:, EXPERTS:2 * EXPERTS], ones[:, :], mask[:, 0, :], False, True).then_inc(filled["G0"], 1)
                g = psum["S0"]
                claim("S0", base["S0"])
                mm(g[:, 0:EXPERTS], ones[:, :], mask[:, 0, :], True, False)
                mm(g[:, 0:EXPERTS], ones[:, :], mask[:, 1, :], False, True).then_inc(filled["S0"], 1)

            def gather(layer, i, c, n):
                bank = f"G{c % 2}"
                claim(bank, n)
                for k in range(4):
                    for b in range(TB):
                        rhs = disp[:, b, :, :].rearrange("p e s -> p (e s)")[:, bass.ds(i * P, P)]
                        last = mm(psum[bank][:, k * P:(k + 1) * P], hv[:, b, 4 * c + k, :], rhs, b == 0, b == 1)
                last.then_inc(filled[bank], 1)

            def up(bank, q, first):
                for k in range(KT):
                    if k % 8 == 0:
                        yield k // 8
                    j = k % QUAD
                    last = mm(psum[bank][CAP * j:CAP * (j + 1), :], xe[:, k, CAP * q:CAP * (q + 1)],
                              w13_tile(q, k, first), k < QUAD, k >= KT - QUAD)
                last.then_inc(filled[bank], 1)

            def fold_turn(bank, a):
                for c in range(4):
                    last = mm(psum[bank][:, c * CAP:(c + 1) * CAP], a[:, c * P:(c + 1) * P], fold[:, :], True, True)
                last.then_inc(filled[bank], 1)

            def quad(layer, i, more):
                base = first_use["moe", layer]
                first = isinstance(i, int) and i == 0

                def wait_slot(j):
                    pe.wait_ge(slot_loaded[slot_at(j, first)], slot_value(layer, i, j, first))

                def turned(q):
                    t, a = f"T{q % 2}", f"A{q % 2}"
                    pe.wait_ge(emptied[a], i * 2 + (base[a] + q // 2 + 1))
                    claim(t, i * 2 + base[t] + q // 2)
                    fold_turn(t, acc[:, q % 2, :])

                def turn_gated():
                    pe.wait_ge(disp_gated, i + (layer * NQUAD + 1))
                    for b in range(TB):
                        claim(f"G{b}", i * 5 + base[f"G{b}"])
                        pe.transpose(psum[f"G{b}"][:, 0:P], disp_g[:, b, :], ident[:, :]).then_inc(filled[f"G{b}"], 1)

                for b in range(2):
                    pe.wait_ge(emptied[f"G{b}"], i * 5 + base[f"G{b}"])
                for q in range(QUAD):
                    a = f"A{q % 2}"
                    claim(a, i * 2 + base[a] + q // 2)
                    for half in up(a, q, first):
                        wait_slot(4 * q + 2 * half)
                        wait_slot(4 * q + 2 * half + 1)
                    if q:
                        turned(q - 1)
                    else:
                        turn_gated()
                if first:
                    pe.wait_ge(disp_ready, 2 * layer + 2)
                if more:
                    for c in range(2):
                        gather(layer, i + 1, c, i * 5 + base[f"G{c}"] + 1)
                turned(QUAD - 1)
                if more:
                    for c in range(2, 4):
                        gather(layer, i + 1, c, i * 5 + base[f"G{c % 2}"] + 2)
                pe.wait_ge(hid_ready, i * QUAD + (layer * EXPERTS + QUAD))
                y0 = 3 if more else 1
                for half in range(2):
                    for j in range((4 + half) * QUAD, (5 + half) * QUAD):
                        wait_slot(j)
                    for dc in (2 * half, 2 * half + 1):
                        g = f"G{dc % 2}"
                        claim(g, i * 5 + base[g] + y0 + half)
                        for ft in range(2):
                            for q in range(QUAD):
                                c = ft * D // 2 + (dc % 2) * COLS
                                w2 = ring[:, slot_at((4 + half) * QUAD + q, first), c:c + COLS]
                                last = mm(psum[g][CAP * q:CAP * (q + 1), :], hid[:, q, ft * CAP:(ft + 1) * CAP], w2,
                                          ft == 0, ft == 1)
                        last.then_inc(filled[g], 1)
                    for dc in (2 * half, 2 * half + 1):
                        g = f"G{dc % 2}"
                        pe.wait_ge(emptied[g], i * 5 + (base[g] + y0 + half + 1))
                        for b in range(TB):
                            s = f"S{b}"
                            claim(s, i * 4 + base[s] + dc)
                            mm(psum[s][:, :], spread[:, b, :], y[:, dc * COLS:(dc + 1) * COLS], True, True).then_inc(filled[s], 1)

            def experts(layer):
                pe.wait_ge(disp_ready, 2 * layer + 1)
                pe.wait_ge(h_ready, (layer + 1) * TB)
                base = first_use["gather", layer]
                for c in range(4):
                    gather(layer, 0, c, base[f"G{c % 2}"] + c // 2)
                quad(layer, 0, True)
                with pe.Fori(1, NQUAD - 1) as i:
                    quad(layer, i, True)
                quad(layer, NQUAD - 1, False)

            def overflow(layer):
                o = over[layer]
                over_x = xe[:, 0:QUAD, :].rearrange("p k n -> p (k n)").rearrange("p (k s) -> p k s", s=CAP)

                def expert(k, e):
                    pe.wait_ge(o["slots"], k + 1)
                    for kt in range(KT):
                        for b in range(TB):
                            last = mm(psum["G0"][:, kt * CAP:(kt + 1) * CAP], hv[:, b, kt, :], over_d[:, b, :], b == 0, b == 1)
                    last.then_inc(o["rows_filled"], 1)
                    for b in range(TB):
                        last = pe.transpose(psum["G1"][0:CAP, b * P:(b + 1) * P], over_g[:, b, :], ident[:, :])
                    last.then_inc(o["spread_filled"], 1)
                    pe.wait_ge(o["rows"], k + 1)
                    for kt in range(KT):
                        if kt % 8 == 0:
                            pe.wait_ge(o["w_loaded"], k * 96 + 32 * (kt // 8 + 1))
                        j = kt % QUAD
                        last = mm(psum["A0"][CAP * j:CAP * (j + 1), :], over_x[:, kt, :],
                                  over_w[:, :, (kt % 8) * FF:(kt % 8 + 1) * FF], kt < QUAD, kt >= KT - QUAD)
                        if kt % 8 == 7:
                            last.then_inc(o["w_used"], 1)
                    pe.wait_ge(o["acc"], k + 1)
                    for c in range(4):
                        last = mm(psum["T0"][:, c * CAP:(c + 1) * CAP], acc[:, 0, c * P:(c + 1) * P], fold[:, :], True, True)
                    last.then_inc(o["turned"], 1)
                    pe.wait_ge(o["hid"], k + 1)
                    pe.wait_ge(o["w_loaded"], k * 96 + 96)
                    for dc in range(4):
                        for ft in range(2):
                            last = mm(psum[("A1", "T1", "S0", "S1")[dc]][0:CAP, :], hid[:, 0, ft * CAP:(ft + 1) * CAP],
                                      over_w[:, ft, dc * COLS:(dc + 1) * COLS], ft == 0, ft == 1)
                    last.then_inc(o["w_used"], 1)
                    pe.wait_ge(o["y"], k + 1)
                    pe.wait_ge(o["spread"], k + 1)
                    for dc in range(4):
                        for b in range(TB):
                            last = mm(psum[BANKS[2 * dc + b]][:, :], spread[0:CAP, b, :], y[0:CAP, dc * COLS:(dc + 1) * COLS],
                                      True, True)
                    last.then_inc(o["scattered"], 1)

                overflow_passes(pe, layer, expert)

            pe.wait_ge(ident_made, 1)
            pe.wait_ge(rows_loaded, 16 * 3)
            pe.transpose(psum["S0"][:, 0:5 * KT], scale_rows[0:5 * KT, :], ident[0:5 * KT, 0:5 * KT]
                         ).then_inc(filled["S0"], 1)
            for layer in (0, 1):
                if layer:
                    pe.wait_ge(x_final, 1)
                else:
                    for b in range(TB):
                        pe.wait_ge(x_loaded[b], 16)
                turn_x(layer)
                mix(layer)
                route(layer)
                experts(layer)
                overflow(layer)

        @block.scalar
        def _(act):
            act.preload_act_table_set("natural_log_exp_and_others")

            def sum_squares(b, c):
                act.activation(squares[:, :], x[:, b, c * COLS:(c + 1) * COLS], ACT.Square,
                               accum_out=sumsq_c[:, b, c:c + 1])
                act.drain()

            def rstd_seed_of(n):
                act.drain().then_inc(squares_done, 1)
                act.wait_ge(mean_ready, n + 1)
                act.activation(rstd[:, :], mean_eps[:, :], ACT.Ln)
                act.drain()
                act.activation(rstd[:, :], rstd[:, :], ACT.Exp, scale=-0.5).then_inc(rstd_seed, 1)

            def scaled_hi(layer):
                for u in range(KT // 2):
                    bank, n = turned_bank(layer, u)
                    act.wait_ge(filled[bank], n + 1)
                    for k in (0, 1):
                        last = act.activation(xT_hi[:, 2 * u + k, :], psum[bank][:, k * T:(k + 1) * T], ACT.Copy,
                                              scale=scales[:, layer, 2 * u + k:2 * u + k + 1])
                    last.then_inc(row_hi_made, 1)
                    if u == 3 or (u == 1 and layer == 0):
                        split_hi(act, layer, 0, u // 2)

            def take_values(layer, i):
                if isinstance(i, int) and i == 0:
                    act.wait_ge(rstd_ready, 2 * layer + 1)
                bank, full, src, dst = value_parts(layer, i, 0)
                act.wait_ge(*full)
                act.activation(dst, src, ACT.Copy, scale=rstd[:, 0:1]).then_inc(emptied[bank], 1)

            def turn_copy(layer, c):
                act.wait_ge(filled["A0"], first_use["norm_ffn", layer]["A0"] + c + 1)
                act.copy(xT[:, 4 * c:4 * c + 2, :].rearrange("p k t -> p (k t)"), psum["A0"][:, :]).then_inc(emptied["A0"], 1)

            def sb_group(kind, g, i):
                base = first_use["mix", 0]
                for _, step, k in SCHEDULES[0, kind]:
                    t, a = f"T{k % 2}", f"A{k % 2}"
                    if step == "split":
                        split_hi(act, 0, i, k)
                    if step == "squares":
                        sum_squares(k // XC, k % XC)
                    if step == "rstd":
                        rstd_seed_of(0)
                    if step == "turn":
                        turn_copy(0, k)
                    if step == "chunk" and kind != "out" and k == 2:
                        take_values(0, i)
                    if step == "chunk" and kind == "out":
                        chunk_squares(0, k)
                    if step == "chunk" and kind == "first" and k == 0:
                        split_gates(act)
                    if step == "score":
                        act.wait_ge(clipped, g * SBG + k + 1)
                        s = soft[:, k % 2, :]
                        act.activation(s, s, ACT.Exp)
                        act.drain()
                        act.activation(s, s, ACT.Ln, bias=1.0).then_inc(softplus_log, 1)
                    if step == "suffix":
                        act.wait_ge(suffix_summed, g * SBG + k + 1)
                        act.activation(prob[:, k % 2, :], psum[a][:, 0:TRI], ACT.Exp).then_inc(emptied[a], 1)
                        act.drain().then_inc(prob_exp, 1)
                    if step == "out":
                        act.wait_ge(filled[t], g * 2 + (base[t] + k // 2 + 1))
                        act.copy(o_hi[:, bass.ds(g * SBG + k, 1), :], psum[t][:, 0:T].unsqueeze(1)).then_inc(out_hi_made, 1)

            def ml_group(kind, g, i):
                base = first_use["mix", 1]
                for _, step, k in SCHEDULES[1, kind]:
                    t = f"T{k % 2}"
                    if step == "split":
                        split_hi(act, 1, i, k)
                    if step == "squares":
                        sum_squares(k // XC, k % XC)
                    if step == "rstd":
                        rstd_seed_of(2)
                    if step == "turn":
                        turn_copy(1, k)
                    if step == "chunk" and kind != "out" and k == 1:
                        take_values(1, i)
                    if step == "chunk" and kind != "out" and k == 2:
                        for b in range(TB):
                            bank = group_bank(2, b)
                            act.wait_ge(*chunk_filled(1, i, 2, b))
                            act.activation(o_exp[:, b, :], psum[bank][:, :], ACT.Exp, scale=neg_rstd[:, b:b + 1]
                                           ).then_inc(emptied[bank], 1)
                    if step == "chunk" and kind == "out":
                        chunk_squares(1, k)
                    if step == "gates":
                        gates_early()
                    if step == "spread":
                        gates_decay(k)
                    if step == "num":
                        act.wait_ge(head_squares, g * MLG + k + 1)
                        act.activation(hrs, ms, ACT.Ln)
                        act.drain()
                        act.activation(hrs, hrs, ACT.Exp, scale=-0.5).then_inc(head_seed, 1)
                    if step == "join":
                        act.wait_ge(filled[t], g * 3 + (base[t] + 3))
                        for n in range(2):
                            at_ = bass.ds((g * MLG + k) * 2 + n, 1)
                            act.activation(o_hi[:, at_, :], psum[t][:, n * T:(n + 1) * T].unsqueeze(1), ACT.Copy,
                                           scale=scales[:, 4, at_]).then_inc(out_hi_made, 1)

            def chunk_squares(layer, c):
                for b in range(TB):
                    bank = f"{'GS'[c % 2]}{b}"
                    act.wait_ge(emptied[bank], first_use["out", layer][bank] + c // 2 + 1)
                    sum_squares(b, c)

            def split_gates(act):
                act.wait_ge(small_loaded[0], 16 * SMALL_LOADS)
                act.copy(gate_hi[:, :], gate_w[:, :, :, :, :].rearrange("p m n k h -> p (m n k h)")).then_inc(gate_hi_made, 1)

            def gates_early():
                act.wait_ge(gate_clip, 1)
                act.activation(g_clip, g_clip, ACT.Exp)
                act.drain()
                act.activation(g_clip, g_clip, ACT.Ln, bias=1.0).then_inc(gate_log, 1)
                act.wait_ge(gate_rows, 1)
                act.activation(g_em, g_em, ACT.Exp)
                act.drain().then_inc(gate_exp, 1)

            def gates_decay(hd):
                if hd == 0:
                    act.wait_ge(emptied["T1"], first_use["gates", 1]["T1"] + 1)
                a = f"A{hd % 2}"
                act.wait_ge(filled[a], first_use["gates", 1][a] + hd // 2 + 1)
                act.activation(decay[:, hd, 0:T], psum[a][:, 0:T], ACT.Exp, bias=u_col[:, 0, hd:hd + 1])
                act.activation(decay[:, hd, T:TRI], psum[a][:, P:T], ACT.Exp, bias=u_col[:, 1, hd:hd + 1]
                               ).then_inc(emptied[a], 1)
                act.drain().then_inc(decay_exp, 1)

            def experts(layer):
                act.wait_ge(rstd_ready, 2 * layer + 2)
                for b in range(TB):
                    act.activation(h[:, b, :], x[:, b, :], ACT.Copy, scale=rstd[:, b:b + 1]).then_inc(h_ready, 1)
                act.wait_ge(group_shift, layer + 1)
                act.activation(gexp, gexp, ACT.Exp).then_inc(group_exp, 1)
                act.wait_ge(top2_gap, layer + 1)
                act.activation(dm, dm, ACT.Exp).then_inc(top2_exp, 1)

                def quad(i, more):
                    base = first_use["moe", layer]

                    def silu(q):
                        t = f"T{q % 2}"
                        act.wait_ge(filled[t], i * 2 + (base[t] + q // 2 + 1))
                        act.wait_ge(exp_taken, i * QUAD + (layer * EXPERTS + q + 1))
                        act.activation(ex, psum[t][:, 0:2 * CAP], ACT.Exp, scale=-1.0).then_inc(silu_exp, 1)

                    for b in range(TB):
                        g = f"G{b}"
                        act.wait_ge(filled[g], i * 5 + (base[g] + 1))
                        act.copy(spread[:, b, :], psum[g][:, 0:P]).then_inc(emptied[g], 1)
                    for q in range(QUAD):
                        silu(q)
                    for dc in range(4):
                        g = f"G{dc % 2}"
                        act.wait_ge(filled[g], i * 5 + (base[g] + (3 if more else 1) + dc // 2 + 1))
                        act.copy(y[:, dc * COLS:(dc + 1) * COLS], psum[g][:, :]).then_inc(emptied[g], 1)
                        if layer and not more and dc % 2:
                            for c, b in ((dc - 1, 0), (dc - 1, 1), (dc, 0), (dc, 1)):
                                act.wait_ge(emptied[f"S{b}"], base[f"S{b}"] + 4 * (NQUAD - 1) + c + 1)
                                sum_squares(b, c)

                with act.Fori(0, NQUAD - 1) as i:
                    quad(i, True)
                quad(NQUAD - 1, False)
                if layer == 0:
                    split_hi(act, 1, 0, 0)

            def overflow(layer):
                o = over[layer]

                def expert(k, e):
                    act.wait_ge(o["spread_filled"], k + 1)
                    act.copy(spread[0:CAP, :, :].rearrange("p b t -> p (b t)"), psum["G1"][0:CAP, 0:T]).then_inc(o["spread"], 1)
                    act.wait_ge(o["turned"], k + 1)
                    act.activation(ex, psum["T0"][:, 0:2 * CAP], ACT.Exp, scale=-1.0).then_inc(o["exp"], 1)
                    act.wait_ge(o["w_used"], k * 3 + 4)
                    for dc in range(4):
                        act.copy(y[0:CAP, dc * COLS:(dc + 1) * COLS], psum[("A1", "T1", "S0", "S1")[dc]][0:CAP, :])
                    act.drain().then_inc(o["y"], 1)

                def after():
                    act.wait_ge(o["done"], 1)
                    for b in range(TB):
                        for c in range(XC):
                            sum_squares(b, c)

                overflow_passes(act, layer, expert, after if layer else None)

            act.wait_ge(scales_made, 1)
            for layer in (0, 1):
                group = ml_group if layer else sb_group
                scaled_hi(layer)
                group("first", None, 0)
                with act.Fori(1, NGROUP) as i:
                    group("group", i - 1, i)
                group("out", NGROUP - 1, NGROUP)
                rstd_seed_of(2 * layer + 1)
                experts(layer)
                overflow(layer)
            rstd_seed_of(4)

        @block.vector
        def _(dve):
            def make_rstd(n):
                dve.wait_ge(squares_done, n + 1)
                dve.tensor_reduce(sumsq[:, :].unsqueeze(2), sumsq_c[:, :, :], AX, ALU.add)
                dve.drain()
                dve.tensor_scalar(mean_eps[:, :], sumsq[:, :], 1.0 / D, EPS, ALU.mult, ALU.add)
                dve.drain().then_inc(mean_ready, 1)
                dve.wait_ge(rstd_seed, n + 1)
                refine(rstd[:, :], mean_eps[:, :], newton[:, :])
                if n == 2:
                    dve.tensor_scalar(neg_rstd[:, :], rstd[:, :], -1.0, None, ALU.mult)
                dve.drain().then_inc(rstd_ready, 1)

            def scaled_lo(layer):
                for u in range(KT // 2):
                    bank, n = turned_bank(layer, u)
                    dve.wait_ge(row_hi_made, layer * KT // 2 + u + 1)
                    for k in (0, 1):
                        last = dve.scalar_tensor_tensor(
                            out=xT_lo[:, 2 * u + k, :], in0=psum[bank][:, k * T:(k + 1) * T],
                            scalar=scales[:, layer, 2 * u + k:2 * u + k + 1], in1=xT_hi[:, 2 * u + k, :].bitcast(F32),
                            op0=ALU.mult, op1=ALU.subtract)
                    last.then_inc(emptied[bank], 1)
                    if u == 1 and layer == 0:
                        split_lo(dve, layer, 0, 0)
                dve.wait_ge(pool_lo_made, layer + 1)
                dve.drain().then_inc(lo_made, 1)

            def make_diag():
                for b in range(TB):
                    dve.tensor_scalar(diag[:, b, :], ident[:, :], rstd[:, b:b + 1], None, ALU.mult)
                dve.drain().then_inc(row_ready, 1)

            def take_row(layer):
                dve.wait_ge(filled["T1"], first_use["row", layer]["T1"] + 1)
                dve.tensor_copy(rstd_row, psum["T1"][:, 0:T]).then_inc(emptied["T1"], 1)
                dve.drain()

            def times_row(dst, bank, scale):
                src = psum[bank][:, :].rearrange("p (n t) -> p n t", n=2)
                row = rstd_row.unsqueeze(1).to_broadcast([P, 2, T])
                if scale == 1.0:
                    op = dve.tensor_tensor(dst, src, row, ALU.mult)
                else:
                    op = dve.scalar_tensor_tensor(out=dst, in0=src, scalar=scale, in1=row, op0=ALU.mult, op1=ALU.mult)
                op.then_inc(emptied[bank], 1)

            def take_chunk(layer, i, c):
                if c == value_chunk(layer):
                    bank, full, src, dst = value_parts(layer, i, 1)
                    dve.wait_ge(*full)
                    dve.tensor_scalar(dst, src, rstd[:, 1:2], None, ALU.mult).then_inc(emptied[bank], 1)
                elif c < 2:
                    for n in range(TB):
                        dve.wait_ge(*chunk_filled(layer, i, c, n))
                        dst = qkT[:, n, :, :] if layer else (qT, kT)[c][:, 2 * n:2 * n + 2, :]
                        times_row(dst, group_bank(c, n), SB_DH ** -0.5 if layer == 0 and c == 0 else 1.0)

            def scale_router(layer):
                dve.wait_ge(small_loaded[layer], 16 * (4 if layer else SMALL_LOADS))
                dve.tensor_tensor(router_w[:, :, :], router_w[:, :, :],
                                  scales[:, 2 + layer, :].unsqueeze(2).to_broadcast([P, KT, ROUTER]), ALU.mult)
                dve.drain().then_inc(router_scaled, 1)

            def common_step(layer, kind, step, k, i):
                if step == "split":
                    split_lo(dve, layer, i, k)
                if step == "chunk":
                    if kind == "out":
                        add_chunk(layer, k)
                    else:
                        take_chunk(layer, i, k)
                    if kind == "first" and k == 0:
                        scale_router(layer)
                if step == "rstd":
                    make_rstd(2 * layer)
                    make_diag()
                if step == "row":
                    take_row(layer)
                if step == "turn":
                    dve.wait_ge(filled["A1"], first_use["norm_ffn", layer]["A1"] + k + 1)
                    dve.tensor_copy(xT[:, 4 * k + 2:4 * k + 4, :].rearrange("p k t -> p (k t)"), psum["A1"][:, :]
                                    ).then_inc(emptied["A1"], 1)

            def refine(r_, v_, t_):
                dve.tensor_tensor(t_, r_, r_, ALU.mult)
                dve.drain()
                dve.tensor_tensor(t_, t_, v_, ALU.mult)
                dve.drain()
                dve.tensor_scalar(t_, t_, -0.5, 1.5, ALU.mult, ALU.add)
                dve.drain()
                dve.tensor_tensor(r_, r_, t_, ALU.mult)
                dve.drain()

            def sb_group(kind, g, i):
                base = first_use["mix", 0]
                for _, step, k in SCHEDULES[0, kind]:
                    t, a = f"T{k % 2}", f"A{k % 2}"
                    common_step(0, kind, step, k, i)
                    if step == "chunk":
                        if kind == "first" and k == 0:
                            dve.wait_ge(consts_made, 1)
                            dve.tensor_scalar(thresholds[:, :], iota[0:1, 0:T // CAP - 1], float(CAP), None,
                                              ALU.mult)
                            dve.drain().then_inc(exp_taken, 1)
                            dve.wait_ge(gate_hi_made, 1)
                            dve.tensor_tensor(gate_lo[:, :], gate_w[:, :, :, :, :].rearrange("p m n k h -> p (m n k h)"),
                                              gate_hi[:, :].bitcast(F32), ALU.subtract).then_inc(gate_lo_made, 1)
                    if step == "score":
                        dve.wait_ge(filled[a], g * 2 + (base[a] + k // 2 + 1))
                        dve.tensor_scalar(soft[:, k % 2, :], psum[a][:, 0:TRI], CLAMP, None, ALU.min).then_inc(clipped, 1)
                        dve.wait_ge(softplus_log, g * SBG + k + 1)
                        dve.tensor_tensor(sp[:, k % 2, :], soft[:, k % 2, :], psum[a][:, 0:TRI], ALU.max)
                        dve.drain().then_inc(softplus_full, 1)
                    if step == "out":
                        dve.wait_ge(out_hi_made, g * SBG + k + 1)
                        at_ = bass.ds(g * SBG + k, 1)
                        dve.tensor_tensor(o_lo[:, at_, :], psum[t][:, 0:T].unsqueeze(1), o_hi[:, at_, :].bitcast(F32),
                                          ALU.subtract).then_inc(emptied[t], 1)

            def ml_group(kind, g, i):
                base = first_use["mix", 1]
                for _, step, k in SCHEDULES[1, kind]:
                    t, a = f"T{k % 2}", f"A{k % 2}"
                    common_step(1, kind, step, k, i)
                    if step == "gates":
                        gates_early()
                    if step == "columns":
                        gates_cols()
                    if g is None:
                        continue
                    hd = g * MLG + k
                    if step == "sigmoid":
                        if k == 0:
                            for b in range(TB):
                                dve.wait_ge(emptied[f"G{b}"], g * 2 + (base[f"G{b}"] + 2))
                        sig = o_exp[:, :, k * ML_DV:(k + 1) * ML_DV]
                        dve.tensor_scalar(sig, sig, 1.0, None, ALU.add)
                        dve.drain()
                        dve.reciprocal(sig, sig)
                        dve.drain()
                    if step == "score":
                        dve.wait_ge(filled[a], g + (base[a] + 1))
                        dve.wait_ge(decay_masked, ML_HEADS)
                        dve.scalar_tensor_tensor(out=weights[:, k, :].unsqueeze(1), in0=psum[a][:, 0:TRI].unsqueeze(1),
                                                 scalar=ML_DQ ** -0.5, in1=decay[:, bass.ds(hd, 1), :],
                                                 op0=ALU.mult, op1=ALU.mult).then_inc(emptied[a], 1)
                        dve.drain().then_inc(weights_ready, 1)
                    if step == "num":
                        for b in range(TB):
                            n = psum[f"T{b}"]
                            dve.wait_ge(filled[f"T{b}"], g * 3 + (base[f"T{b}"] + k + 1))
                            dve.tensor_scalar(ssq[:, b:b + 1], n[:, ML_DV:ML_DV + 1], -1.0, None, ALU.mult)
                        dve.drain()
                        for b in range(TB):
                            dve.tensor_tensor(den[:, b:b + 1], psum[f"T{b}"][:, ML_DV:ML_DV + 1], ssq[:, b:b + 1], ALU.max)
                        dve.drain()
                        dve.tensor_tensor(den.unsqueeze(2), den.unsqueeze(2), m_col[:, :, bass.ds(hd, 1)], ALU.max)
                        dve.drain()
                        dve.reciprocal(den, den)
                        dve.drain()
                        for b in range(TB):
                            n = psum[f"T{b}"]
                            dve.tensor_scalar(hs[:, b, :], n[:, 0:ML_DV], den[:, b:b + 1], None, ALU.mult
                                              ).then_inc(emptied[f"T{b}"], 1)
                        dve.drain()
                        for b in range(TB):
                            dve.tensor_tensor_reduce(gated[:, k, b, :], hs[:, b, :], hs[:, b, :], 1.0, 0.0,
                                                     ALU.mult, ALU.add, ssq[:, b:b + 1])
                            dve.drain()
                        dve.tensor_scalar(ms, ssq, 1.0 / ML_DV, EPS, ALU.mult, ALU.add)
                        dve.drain().then_inc(head_squares, 1)
                    if step == "gate":
                        dve.wait_ge(head_seed, g * MLG + k + 1)
                        refine(hrs, ms, hnw)
                        for b in range(TB):
                            dve.scalar_tensor_tensor(out=gated[:, k, b, :], in0=hs[:, b, :], scalar=hrs[:, b:b + 1],
                                                     in1=o_exp[:, b, k * ML_DV:(k + 1) * ML_DV],
                                                     op0=ALU.mult, op1=ALU.mult)
                        dve.drain().then_inc(gated_ready, 1)
                    if step == "join":
                        dve.wait_ge(out_hi_made, SB_HEADS + g * (2 * MLG) + (2 * k + 2))
                        for n in range(2):
                            at_ = bass.ds((g * MLG + k) * 2 + n, 1)
                            last = dve.scalar_tensor_tensor(
                                out=o_lo[:, at_, :], in0=psum[t][:, n * T:(n + 1) * T].unsqueeze(1),
                                scalar=scales[:, 4, at_], in1=o_hi[:, at_, :].bitcast(F32),
                                op0=ALU.mult, op1=ALU.subtract)
                        last.then_inc(emptied[t], 1)

            def gates_early():
                pg = psum["T0"]
                dve.wait_ge(filled["T0"], first_use["gates", 1]["T0"] + 1)
                row = rstd_row[0:ML_HEADS]
                dve.tensor_tensor(g_y, pg[0:ML_HEADS, 0:T], row, ALU.mult)
                dve.tensor_copy(g_u, pg[GATE_M - ML_HEADS:GATE_M, 0:T]).then_inc(emptied["T0"], 1)
                dve.drain()
                dve.tensor_scalar(g_y, g_y, gate_b[:, 1:2], -1.0, ALU.add, ALU.mult)
                dve.tensor_tensor(g_u, g_u, row, ALU.mult)
                dve.drain()
                dve.tensor_scalar(g_clip, g_y, CLAMP, None, ALU.min).then_inc(gate_clip, 1)
                dve.wait_ge(gate_log, 1)
                dve.tensor_tensor(g_sp, g_clip, g_y, ALU.max)
                dve.drain()
                dve.memset(g_y, 1.0)
                dve.drain()
                dve.tensor_tensor_scan(g_negb, g_y, g_sp, 0.0, ALU.mult, ALU.add)
                dve.drain()
                dve.scalar_tensor_tensor(out=g_u, in0=g_u, scalar=gate_b[:, 0:1], in1=g_negb,
                                         op0=ALU.add, op1=ALU.add)
                dve.drain()
                dve.tensor_tensor_scan(g_m, g_u, g_u, 0.0, ALU.max, ALU.max)
                dve.drain()
                dve.tensor_tensor(g_em, g_negb, g_m, ALU.subtract)
                dve.drain()
                dve.tensor_scalar(g_m, g_m, -1.0, None, ALU.mult)
                dve.drain().then_inc(gate_rows, 1)

            def gates_cols():
                dve.wait_ge(filled["T1"], first_use["gates", 1]["T1"] + 1)
                pg = psum["T1"]
                w = TB * ML_HEADS
                dve.tensor_copy(u_col.rearrange("p b h -> p (b h)"), pg[:, 0:w])
                dve.tensor_copy(m_col.rearrange("p b h -> p (b h)"), pg[:, w:2 * w]).then_inc(emptied["T1"], 1)

            def add_chunk(layer, c):
                for b in range(TB):
                    dve.wait_ge(*out_filled(layer, c, b))
                    bank = f"{'GS'[c % 2]}{b}"
                    xs = x[:, b, c * COLS:(c + 1) * COLS]
                    dve.tensor_tensor(xs, xs, psum[bank][:, :], ALU.add).then_inc(emptied[bank], 1)

            def wide(view, shape):
                return view.to_broadcast(shape)

            def slots_of(e0, e1):
                full = [P, e1 - e0, CAP]
                for b in range(TB):
                    dve.tensor_tensor(disp[:, b, e0:e1], wide(iota[:, :].unsqueeze(1), full),
                                      wide(posm[:, b, e0:e1].unsqueeze(2), full), ALU.is_equal)
                dve.drain().then_inc(disp_ready, 1)

            def route(layer):
                base = first_use["route", layer]
                dve.tensor_scalar(rank, iota[:, 0:PER_GROUP], -1.0, float(PER_GROUP + 1), ALU.mult, ALU.add)
                dve.wait_ge(filled["T0"], first_use["norm_ffn", layer]["T0"] + 1)
                for b in range(TB):
                    last = dve.scalar_tensor_tensor(out=logits[:, b, :], in0=psum["T0"][:, b * ROUTER:(b + 1) * ROUTER],
                                                    scalar=rstd[:, b:b + 1], in1=router_b[:, :],
                                                    op0=ALU.mult, op1=ALU.add)
                last.then_inc(emptied["T0"], 1)
                dve.drain()
                gl = logits[:, :, 0:GROUPS]
                g4 = [P, TB, GROUPS]
                e8 = [P, TB, PER_GROUP]

                def first_max(vals, top, cmp_, sel, shape, n):
                    dve.tensor_reduce(top, vals, AX, ALU.max)
                    dve.drain()
                    for b in range(TB):
                        dve.scalar_tensor_tensor(out=cmp_[:, b, :], in0=vals[:, b, :], scalar=top[:, b, :],
                                                 in1=rank[:, 0:n], op0=ALU.is_equal, op1=ALU.mult)
                    dve.drain()
                    dve.tensor_reduce(tie, cmp_, AX, ALU.max)
                    dve.drain()
                    dve.tensor_tensor(sel, cmp_, wide(tie, shape), ALU.is_equal)
                    dve.drain()

                first_max(gl, gmax, gcmp, gsel, g4, GROUPS)
                dve.tensor_tensor(gexp, gl, wide(gmax, g4), ALU.subtract).then_inc(group_shift, 1)
                el = logits[:, :, GROUPS:ROUTER].rearrange("p b (g e) -> p b g e", g=GROUPS)
                for b in range(TB):
                    dve.tensor_tensor(picked[:, b], el[:, b],
                                      wide(gsel[:, b, :].unsqueeze(2), [P, GROUPS, PER_GROUP]), ALU.mult)
                dve.drain()
                for b in range(TB):
                    dve.tensor_reduce(es[:, b, :].unsqueeze(2), picked[:, b].rearrange("p g e -> p e g"), AX, ALU.add)
                dve.drain()
                first_max(es, m1, cmp8, s1, e8, PER_GROUP)
                dve.scalar_tensor_tensor(out=tmp8, in0=s1, scalar=-3e38, in1=es, op0=ALU.mult, op1=ALU.add)
                dve.drain()
                first_max(tmp8, m2, cmp8, s2, e8, PER_GROUP)
                dve.tensor_tensor(dm, m2, m1, ALU.subtract).then_inc(top2_gap, 1)
                dve.tensor_tensor(tmp8, s1, s2, ALU.add)
                dve.drain()
                m4 = mask.rearrange("p b (g e) -> p b g e", g=GROUPS)
                ge = [P, GROUPS, PER_GROUP]
                for b in range(TB):
                    dve.tensor_tensor(m4[:, b], wide(gsel[:, b, :].unsqueeze(2), ge), wide(tmp8[:, b, :].unsqueeze(1), ge), ALU.mult)
                dve.drain().then_inc(mask_ready, 1)
                dve.wait_ge(filled["G0"], base["G0"] + 1)
                pg = psum["G0"]
                dve.scalar_tensor_tensor(out=posm.rearrange("p b e -> p (b e)"), in0=pg[:, 0:TB * EXPERTS], scalar=1.0,
                                         in1=mask.rearrange("p b e -> p (b e)"), op0=ALU.add, op1=ALU.mult
                                         ).then_inc(emptied["G0"], 1)
                dve.drain()

                slots_of(0, QUAD)
                dve.wait_ge(group_exp, layer + 1)
                dve.tensor_reduce(gsum, gexp, AX, ALU.add)
                dve.drain()
                dve.reciprocal(psel, gsum)
                dve.wait_ge(top2_exp, layer + 1)
                dve.tensor_scalar(w1c, dm, 1.0, None, ALU.add)
                dve.drain()
                dve.reciprocal(w1c, w1c)
                dve.drain()
                dve.tensor_tensor(w1c, w1c, psel, ALU.mult)
                dve.drain()
                dve.tensor_tensor(w2c, w1c, dm, ALU.mult)
                dve.tensor_tensor(gate8, s1, wide(w1c, e8), ALU.mult)
                dve.drain()
                dve.tensor_tensor(tmp8, s2, wide(w2c, e8), ALU.mult)
                dve.drain()
                dve.tensor_tensor(gate8, gate8, tmp8, ALU.add)
                dve.drain()
                w4 = gates.rearrange("p b (g e) -> p b g e", g=GROUPS)
                for b in range(TB):
                    dve.tensor_tensor(w4[:, b], wide(gsel[:, b, :].unsqueeze(2), ge), wide(gate8[:, b, :].unsqueeze(1), ge), ALU.mult)
                dve.drain()

            def experts(layer):
                base = first_use["moe", layer]

                def take_rows(c, n):
                    g = f"G{c % 2}"
                    dve.wait_ge(filled[g], n + 1)
                    dve.tensor_tensor(xe[:, 4 * c:4 * c + 4, :], psum[g][:, :].rearrange("p (k n) -> p k n", k=4),
                                      wide(expert_scale[:, layer, 4 * c:4 * c + 4].unsqueeze(2), [P, 4, P]), ALU.mult
                                      ).then_inc(emptied[g], 1)

                def quad(i, more):
                    for b in range(TB):
                        dve.tensor_tensor(disp_g[:, b, :].rearrange("p (e s) -> p e s", e=QUAD),
                                          disp[:, b, bass.ds(i * QUAD, QUAD), :],
                                          wide(gates[:, b, bass.ds(i * QUAD, QUAD)].unsqueeze(2), [P, QUAD, CAP]), ALU.mult)
                    dve.drain().then_inc(disp_gated, 1)

                    def take(q):
                        a = f"A{q % 2}"
                        dve.wait_ge(filled[a], i * 2 + (base[a] + q // 2 + 1))
                        dve.tensor_copy(acc[:, q % 2, :], psum[a][:, :]).then_inc(emptied[a], 1)

                    def silu(q):
                        t = f"T{q % 2}"
                        dve.wait_ge(silu_exp, i * QUAD + (layer * EXPERTS + q + 1))
                        dve.tensor_scalar(sg, ex, 1.0, None, ALU.add).then_inc(exp_taken, 1)
                        dve.drain()
                        dve.reciprocal(sg, sg)
                        dve.drain()
                        dve.tensor_tensor(t13, sg, psum[t][:, 0:2 * CAP], ALU.mult)
                        dve.drain()
                        dve.tensor_tensor(hid[:, q, :], t13, psum[t][:, 2 * CAP:4 * CAP], ALU.mult).then_inc(emptied[t], 1)
                        dve.drain().then_inc(hid_ready, 1)

                    take(0)
                    for q in range(1, QUAD):
                        take(q)
                        silu(q - 1)
                    if more:
                        for c in range(2):
                            take_rows(c, i * 5 + (base[f"G{c}"] + 1))
                    silu(QUAD - 1)
                    if more:
                        for c in range(2, 4):
                            take_rows(c, i * 5 + (base[f"G{c % 2}"] + 2))
                    for dc in range(4):
                        for b in range(TB):
                            s = f"S{b}"
                            dve.wait_ge(filled[s], i * 4 + (base[s] + dc + 1))
                            xs = x[:, b, dc * COLS:(dc + 1) * COLS]
                            dve.tensor_tensor(xs, xs, psum[s][:, :], ALU.add).then_inc(emptied[s], 1)
                    dve.drain()

                for c in range(4):
                    take_rows(c, first_use["gather", layer][f"G{c % 2}"] + c // 2)
                slots_of(QUAD, EXPERTS)
                dve.wait_ge(filled["S0"], first_use["route", layer]["S0"] + 1)
                dve.tensor_reduce(count_max[:, :], psum["S0"][0:1, 0:EXPERTS], AX, ALU.max).then_inc(emptied["S0"], 1)
                dve.drain()
                dve.tensor_scalar(count_lt[:, :], thresholds[:, :], count_max[:, 0:1], None, ALU.is_lt)
                dve.drain()
                dve.tensor_reduce(extra_f[:, :], count_lt[:, :], AX, ALU.add)
                dve.drain()
                dve.tensor_copy(extra_i[:, :], extra_f[:, :])
                dve.drain().then_inc(extra_ready, 1)
                with dve.Fori(0, NQUAD - 1) as i:
                    quad(i, True)
                quad(NQUAD - 1, False)
                if layer == 0:
                    split_lo(dve, 1, 0, 0)
                dve.drain()

            def overflow(layer):
                o = over[layer]
                dve.sem_inc(o["w_used"], 1)

                def expert(k, e):
                    for b in range(TB):
                        at = posm[:, b, bass.ds(e, 1)]
                        dve.tensor_scalar(at, at, -float(CAP), None, ALU.add)
                    dve.drain()
                    for b in range(TB):
                        dve.tensor_scalar(over_d[:, b, :], iota[:, :], posm[:, b, bass.ds(e, 1)], None, ALU.is_equal)
                    dve.drain()
                    for b in range(TB):
                        dve.tensor_scalar(over_g[:, b, :], over_d[:, b, :], gates[:, b, bass.ds(e, 1)], None, ALU.mult)
                    dve.drain().then_inc(o["slots"], 1)
                    dve.wait_ge(o["rows_filled"], k + 1)
                    over_x = xe[:, 0:QUAD, :].rearrange("p k n -> p (k n)").rearrange("p (k s) -> p k s", s=CAP)
                    dve.tensor_tensor(over_x, psum["G0"][:, :].rearrange("p (k s) -> p k s", s=CAP),
                                      wide(expert_scale[:, layer, :].unsqueeze(2), [P, KT, CAP]), ALU.mult
                                      ).then_inc(o["rows"], 1)
                    dve.wait_ge(o["w_used"], k * 3 + 3)
                    dve.tensor_copy(acc[:, 0, :], psum["A0"][:, :]).then_inc(o["acc"], 1)
                    dve.wait_ge(o["exp"], k + 1)
                    dve.tensor_scalar(sg, ex, 1.0, None, ALU.add)
                    dve.drain()
                    dve.reciprocal(sg, sg)
                    dve.drain()
                    dve.tensor_tensor(t13, sg, psum["T0"][:, 0:2 * CAP], ALU.mult)
                    dve.drain()
                    dve.tensor_tensor(hid[:, 0, :], t13, psum["T0"][:, 2 * CAP:4 * CAP], ALU.mult)
                    dve.drain().then_inc(o["hid"], 1)
                    dve.wait_ge(o["scattered"], k + 1)
                    for dc in range(4):
                        for b in range(TB):
                            xs = x[:, b, dc * COLS:(dc + 1) * COLS]
                            dve.tensor_tensor(xs, xs, psum[BANKS[2 * dc + b]][:, :], ALU.add)
                    dve.drain()

                def after():
                    dve.drain().then_inc(o["done"], 1)

                overflow_passes(dve, layer, expert, after)

            dve.wait_ge(filled["S0"], 1)
            dve.tensor_copy(scales[:, :, :].rearrange("p n k -> p (n k)"), psum["S0"][:, 0:5 * KT]).then_inc(emptied["S0"], 1)
            dve.drain().then_inc(scales_made, 1)
            dve.wait_ge(ident_made, 1)
            for layer in (0, 1):
                group = ml_group if layer else sb_group
                scaled_lo(layer)
                group("first", None, 0)
                with dve.Fori(1, NGROUP) as i:
                    group("group", i - 1, i)
                group("out", NGROUP - 1, NGROUP)
                dve.drain()
                make_rstd(2 * layer + 1)
                route(layer)
                experts(layer)
                overflow(layer)
                dve.drain().then_inc(x_final, 1)
            make_rstd(4)
            dve.wait_ge(last_scale_loaded, 16)
            for n in range(2 * TB):
                b, c = n // 2, slice((n % 2) * D // 2, (n % 2 + 1) * D // 2)
                dve.scalar_tensor_tensor(out=h[:, b, c], in0=x[:, b, c], scalar=rstd[:, b:b + 1], in1=last_scale[:, c],
                                         op0=ALU.mult, op1=ALU.mult).then_inc(out_ready, 1)



_INS = ["x", "norm_mix", "norm_ffn", "norm_final", "sb_w_in", "sb_w_out", "ml_w_in", "ml_b_i", "ml_b_f",
        "ml_g_head", "ml_w_out", "moe_w_group", "moe_b_group", "moe_w_expert", "moe_b_expert",
        "moe_w1", "moe_w3", "moe_w2"]


def kernel(**inputs):
    import concourse.bacc as bacc
    from concourse.bass_utils import run_bass_kernel_spmd

    nc = bacc.Bacc("TRN2", target_bir_lowering=False, num_devices=1)
    arrays, args = {}, []
    for name in _INS:
        a = np.ascontiguousarray(inputs[name])
        arrays[f"in_{name}"] = a
        args.append(nc.dram_tensor(f"in_{name}", a.shape, mybir.dt.from_np(a.dtype), kind="ExternalInput").ap())
    args.append(nc.dram_tensor("out_x", (1, T, D), F32, kind="ExternalOutput").ap())
    build(nc, *args)
    r = run_bass_kernel_spmd(nc, [arrays], core_ids=[0])
    return r.results[0]["out_x"]
```
